# Optimizing a Trainium2 kernel written in Bass

```python
import math
import jax, jax.numpy as jnp
from jax import lax
import numpy as np

D_MODEL = 2048
BATCH = 1
SEQ = 256
DEPTH = 2
DEC_BATCH = 8
DEC_SEQ = 4
PAST_LEN = 1024
PAGE_SIZE = 128

D_MIX = 2 * D_MODEL
SSD_WIDTH = D_MIX // 2
SSD_HEAD_DIM = 64
SSD_HEADS = SSD_WIDTH // SSD_HEAD_DIM
SSD_GROUPS = 4
SSD_STATE = 128
SSD_CONV = 4
SSD_CHUNK = 128
SSD_CONV_CH = SSD_WIDTH + 2 * SSD_GROUPS * SSD_STATE
ATT_WIDTH = D_MIX // 4
HEAD_DIM = 64
N_Q_HEADS = ATT_WIDTH // HEAD_DIM
N_KV_HEADS = 4
Q_PER_KV = N_Q_HEADS // N_KV_HEADS
WINDOW = 128
ATT_BLOCK = 128
ROPE_THETA = 10000.0
W_BUF = min(WINDOW, PAST_LEN)
SC_WIDTH = D_MIX // 4
SC_CONV = 3
PLE_DIM = 256
EPS = 1e-6
IN_SIZES = (SSD_WIDTH, SSD_CONV_CH, SSD_HEADS,
            ATT_WIDTH, N_KV_HEADS * HEAD_DIM, N_KV_HEADS * HEAD_DIM, ATT_WIDTH,
            SC_WIDTH, SC_WIDTH, SC_WIDTH, SC_WIDTH)
N_IN = sum(IN_SIZES)

kernel_name = "hybrid_ssd_swa_shortconv_step"

def _split_points():
    pts, acc = [], 0
    for s in IN_SIZES[:-1]:
        acc += s
        pts.append(acc)
    return pts

def _rmsnorm(x, w):
    xf = x.astype(jnp.float32)
    y = xf * lax.rsqrt(jnp.mean(xf * xf, axis=-1, keepdims=True) + EPS)
    return (y * w.astype(jnp.float32)).astype(x.dtype)

def _rope(x, pos):
    d = x.shape[-1]
    half = d // 2
    inv_freq = jnp.exp(-math.log(ROPE_THETA) * jnp.arange(half, dtype=jnp.float32) * (2.0 / d))
    ang = pos.astype(jnp.float32)[:, None] * inv_freq[None, :]
    cos = jnp.cos(ang)[None, :, None, :]
    sin = jnp.sin(ang)[None, :, None, :]
    xf = x.astype(jnp.float32)
    x1, x2 = xf[..., :half], xf[..., half:]
    return jnp.concatenate([x1 * cos - x2 * sin, x2 * cos + x1 * sin], axis=-1).astype(x.dtype)

def _causal_dwconv(u, buf, w):
    k = w.shape[0]
    L = u.shape[1]
    full = jnp.concatenate([buf.astype(u.dtype), u], axis=1)
    out = full[:, 0:L] * w[0]
    for j in range(1, k):
        out = out + full[:, j:j + L] * w[j]
    return out, full[:, L:]

def _ssd_scan(x, dt, a, bm, cm, s0):
    b, L, H, P = x.shape
    G, N = bm.shape[2], bm.shape[3]
    R = H // G
    Q = min(SSD_CHUNK, L)
    pad = (-L) % Q
    if pad:
        x = jnp.pad(x, ((0, 0), (0, pad), (0, 0), (0, 0)))
        dt = jnp.pad(dt, ((0, 0), (0, pad), (0, 0)))
        bm = jnp.pad(bm, ((0, 0), (0, pad), (0, 0), (0, 0)))
        cm = jnp.pad(cm, ((0, 0), (0, pad), (0, 0), (0, 0)))
    nc = (L + pad) // Q
    xc = x.astype(jnp.float32).reshape(b, nc, Q, G, R, P)
    dtc = dt.reshape(b, nc, Q, G, R)
    bc = bm.astype(jnp.float32).reshape(b, nc, Q, G, N)
    cc = cm.astype(jnp.float32).reshape(b, nc, Q, G, N)
    a_cum = jnp.cumsum(dtc * a.reshape(G, R), axis=2)
    seg = a_cum[:, :, :, None] - a_cum[:, :, None, :]
    causal = jnp.tril(jnp.ones((Q, Q), dtype=bool))[:, :, None, None]
    decay = jnp.exp(jnp.where(causal, seg, -jnp.inf))
    cb = jnp.einsum('bclgn,bcsgn->bclsg', cc, bc)
    m = cb[..., None] * decay * dtc[:, :, None]
    y_diag = jnp.einsum('bclsgr,bcsgrp->bclgrp', m, xc)
    w_state = jnp.exp(a_cum[:, :, -1:] - a_cum) * dtc
    st = jnp.einsum('bcsgn,bcsgr,bcsgrp->bcgrpn', bc, w_state, xc)
    chunk_decay = jnp.exp(a_cum[:, :, -1])

    def step(carry, inp):
        dec, s_c = inp
        return dec[..., None, None] * carry + s_c, carry

    s_init = s0.astype(jnp.float32).reshape(b, G, R, P, N)
    s_fin, s_in = lax.scan(step, s_init, (jnp.moveaxis(chunk_decay, 1, 0), jnp.moveaxis(st, 1, 0)))
    s_in = jnp.moveaxis(s_in, 0, 1)
    y_off = jnp.einsum('bclgn,bcgrpn,bclgr->bclgrp', cc, s_in, jnp.exp(a_cum))
    y = (y_diag + y_off).reshape(b, nc * Q, H, P)[:, :L]
    return y, s_fin.reshape(b, H, P, N)

def _ssd_branch(z, xbc, dt_raw, conv_buf, s0, conv_w, conv_b, a_log, dt_bias, d_skip, norm_w):
    b, L = z.shape[0], z.shape[1]
    xbc_c, conv_buf_new = _causal_dwconv(xbc, conv_buf, conv_w)
    xbc_c = jax.nn.silu(xbc_c + conv_b)
    xs = xbc_c[..., :SSD_WIDTH].reshape(b, L, SSD_HEADS, SSD_HEAD_DIM)
    bm = xbc_c[..., SSD_WIDTH:SSD_WIDTH + SSD_GROUPS * SSD_STATE].reshape(b, L, SSD_GROUPS, SSD_STATE)
    cm = xbc_c[..., SSD_WIDTH + SSD_GROUPS * SSD_STATE:].reshape(b, L, SSD_GROUPS, SSD_STATE)
    dt = jax.nn.softplus(dt_raw.astype(jnp.float32) + dt_bias.astype(jnp.float32))
    a = -jnp.exp(a_log.astype(jnp.float32))
    y, s_fin = _ssd_scan(xs, dt, a, bm, cm, s0)
    y = y + d_skip.astype(jnp.float32)[:, None] * xs.astype(jnp.float32)
    y = y.reshape(b, L, SSD_WIDTH) * jax.nn.silu(z.astype(jnp.float32))
    yg = y.reshape(b, L, SSD_GROUPS, SSD_WIDTH // SSD_GROUPS)
    yg = yg * lax.rsqrt(jnp.mean(yg * yg, axis=-1, keepdims=True) + EPS)
    y = yg.reshape(b, L, SSD_WIDTH) * norm_w.astype(jnp.float32)
    return y.astype(z.dtype), conv_buf_new, s_fin.astype(s0.dtype)

def _swa_branch(q, k, v, g, k_buf, v_buf, pos0, sinks):
    b, L = q.shape[0], q.shape[1]
    wb = k_buf.shape[1]
    q = q.reshape(b, L, N_Q_HEADS, HEAD_DIM)
    k = k.reshape(b, L, N_KV_HEADS, HEAD_DIM)
    v = v.reshape(b, L, N_KV_HEADS, HEAD_DIM)
    q_pos = pos0 + jnp.arange(L, dtype=jnp.int32)
    q = _rope(q, q_pos)
    k = _rope(k, q_pos)
    k_full = jnp.concatenate([k_buf, k.astype(k_buf.dtype)], axis=1)
    v_full = jnp.concatenate([v_buf, v.astype(v_buf.dtype)], axis=1)
    k_pos = pos0 - wb + jnp.arange(wb + L, dtype=jnp.int32)
    k_new, v_new = k_full[:, -W_BUF:], v_full[:, -W_BUF:]
    if L <= ATT_BLOCK:
        tq, nb = L, 1
        kb, vb, kp = k_full[:, None], v_full[:, None], k_pos[None]
    else:
        tq = ATT_BLOCK
        nb = L // tq
        k5 = k_full.reshape(b, nb + 1, tq, N_KV_HEADS, HEAD_DIM)
        v5 = v_full.reshape(b, nb + 1, tq, N_KV_HEADS, HEAD_DIM)
        kb = jnp.concatenate([k5[:, :-1], k5[:, 1:]], axis=2)
        vb = jnp.concatenate([v5[:, :-1], v5[:, 1:]], axis=2)
        kp5 = k_pos.reshape(nb + 1, tq)
        kp = jnp.concatenate([kp5[:-1], kp5[1:]], axis=1)
    qb = q.reshape(b, nb, tq, N_KV_HEADS, Q_PER_KV, HEAD_DIM)
    qp = q_pos.reshape(nb, tq)
    s = jnp.einsum('bntkgd,bnskd->bnkgts', qb, kb.astype(qb.dtype)).astype(jnp.float32) * (HEAD_DIM ** -0.5)
    kpe, qpe = kp[:, None, :], qp[:, :, None]
    mask = (kpe <= qpe) & (kpe > qpe - WINDOW) & (kpe >= 0)
    s = jnp.where(mask[None, :, None, None], s, -jnp.inf)
    sink = jnp.broadcast_to(sinks.astype(jnp.float32).reshape(N_KV_HEADS, Q_PER_KV)[None, None, :, :, None, None],
                            s.shape[:-1] + (1,))
    pr = jax.nn.softmax(jnp.concatenate([s, sink], axis=-1), axis=-1)[..., :-1]
    o = jnp.einsum('bnkgts,bnskd->bntkgd', pr.astype(q.dtype), vb.astype(q.dtype))
    o = o.reshape(b, L, ATT_WIDTH) * jax.nn.silu(g)
    return o, k_new, v_new

def _sc_branch(bg, cg, hh, g, buf, w):
    u = cg * hh
    conv, buf_new = _causal_dwconv(u, buf, w)
    return bg * conv * jax.nn.silu(g), buf_new

def _layer(x, p, pos0, ssd_buf, ssm0, k_buf, v_buf, sc_buf,
           w_in, w_out, norm_pre, norm_post, ssd_conv_w, ssd_conv_b, ssd_a_log, ssd_dt_bias,
           ssd_d, ssd_norm, attn_sinks, sc_conv_w, ple_proj, ple_gate):
    h = _rmsnorm(x, norm_pre)
    proj = jnp.einsum('bld,dn->bln', h, w_in)
    (z, xbc, dt_raw, q, k, v, g_att, b_sc, c_sc, h_sc, g_sc) = jnp.split(proj, _split_points(), axis=-1)
    y_ssd, ssd_buf_new, ssm_new = _ssd_branch(z, xbc, dt_raw, ssd_buf, ssm0, ssd_conv_w, ssd_conv_b,
                                              ssd_a_log, ssd_dt_bias, ssd_d, ssd_norm)
    y_att, k_new, v_new = _swa_branch(q, k, v, g_att, k_buf, v_buf, pos0, attn_sinks)
    y_sc, sc_buf_new = _sc_branch(b_sc, c_sc, h_sc, g_sc, sc_buf, sc_conv_w)
    mix = jnp.einsum('bln,nd->bld', jnp.concatenate([y_ssd, y_att, y_sc], axis=-1), w_out)
    x = x + _rmsnorm(mix, norm_post)
    gate = jax.nn.sigmoid(jnp.einsum('bld,de->ble', x, ple_gate).astype(jnp.float32))
    e = jnp.einsum('blp,pd->bld', p, ple_proj).astype(jnp.float32)
    x = x + (gate * e).astype(x.dtype)
    return x, ssd_buf_new, ssm_new, k_new, v_new, sc_buf_new

def setup_inputs(seed: int = 0) -> dict:
    key = jax.random.key(seed)
    ks = jax.random.split(key, 24)
    f32 = jnp.float32
    nrm = lambda k, shape, scale: jax.random.normal(k, shape, f32) * scale
    dt0 = jnp.exp(jax.random.uniform(ks[16], (DEPTH, SSD_HEADS), f32, math.log(1e-3), math.log(1e-1)))
    return {
        "x_prompt": nrm(ks[0], (BATCH, SEQ, D_MODEL), 1.0),
        "x_sample": nrm(ks[1], (DEC_BATCH, DEC_SEQ, D_MODEL), 1.0),
        "p_prompt": nrm(ks[2], (DEPTH, BATCH, SEQ, PLE_DIM), 1.0),
        "p_sample": nrm(ks[3], (DEPTH, DEC_BATCH, DEC_SEQ, PLE_DIM), 1.0),
        "state_ssd_conv": nrm(ks[4], (DEPTH, DEC_BATCH, SSD_CONV - 1, SSD_CONV_CH), 1.0),
        "state_ssm": nrm(ks[5], (DEPTH, DEC_BATCH, SSD_HEADS, SSD_HEAD_DIM, SSD_STATE), 0.1),
        "cache_k": nrm(ks[6], (DEPTH, DEC_BATCH, W_BUF, N_KV_HEADS, HEAD_DIM), 1.0),
        "cache_v": nrm(ks[7], (DEPTH, DEC_BATCH, W_BUF, N_KV_HEADS, HEAD_DIM), 1.0),
        "state_sc_conv": nrm(ks[8], (DEPTH, DEC_BATCH, SC_CONV - 1, SC_WIDTH), 1.0),
        "w_in": nrm(ks[9], (DEPTH, D_MODEL, N_IN), D_MODEL ** -0.5),
        "w_out": nrm(ks[10], (DEPTH, D_MIX, D_MODEL), D_MIX ** -0.5),
        "norm_pre": 1.0 + nrm(ks[11], (DEPTH, D_MODEL), 0.02),
        "norm_post": 1.0 + nrm(ks[12], (DEPTH, D_MODEL), 0.02),
        "ssd_conv_w": nrm(ks[13], (DEPTH, SSD_CONV, SSD_CONV_CH), SSD_CONV ** -0.5),
        "ssd_conv_b": nrm(ks[14], (DEPTH, SSD_CONV_CH), 0.02),
        "ssd_a_log": jnp.log(jax.random.uniform(ks[15], (DEPTH, SSD_HEADS), f32, 1.0, 16.0)),
        "ssd_dt_bias": dt0 + jnp.log(-jnp.expm1(-dt0)),
        "ssd_d": 1.0 + nrm(ks[17], (DEPTH, SSD_HEADS), 0.02),
        "ssd_norm": 1.0 + nrm(ks[18], (DEPTH, SSD_WIDTH), 0.02),
        "attn_sinks": nrm(ks[19], (DEPTH, N_Q_HEADS), 0.5),
        "sc_conv_w": nrm(ks[20], (DEPTH, SC_CONV, SC_WIDTH), SC_CONV ** -0.5),
        "ple_proj": nrm(ks[21], (DEPTH, PLE_DIM, D_MODEL), PLE_DIM ** -0.5),
        "ple_gate": nrm(ks[22], (DEPTH, D_MODEL, D_MODEL), D_MODEL ** -0.5),
    }

def reference(x_prompt, x_sample, p_prompt, p_sample, state_ssd_conv, state_ssm, cache_k, cache_v,
              state_sc_conv, w_in, w_out, norm_pre, norm_post, ssd_conv_w, ssd_conv_b, ssd_a_log,
              ssd_dt_bias, ssd_d, ssd_norm, attn_sinks, sc_conv_w, ple_proj, ple_gate):
    bp = x_prompt.shape[0]
    dtp = x_prompt.dtype
    z_ssd_buf = jnp.zeros((bp, SSD_CONV - 1, SSD_CONV_CH), dtp)
    z_ssm = jnp.zeros((bp, SSD_HEADS, SSD_HEAD_DIM, SSD_STATE), jnp.float32)
    z_kv = jnp.zeros((bp, WINDOW, N_KV_HEADS, HEAD_DIM), dtp)
    z_sc_buf = jnp.zeros((bp, SC_CONV - 1, SC_WIDTH), dtp)
    yp, ys = x_prompt, x_sample
    pr_conv, pr_ssm, pr_k, pr_v, pr_sc = [], [], [], [], []
    sa_conv, sa_ssm, sa_k, sa_v, sa_sc = [], [], [], [], []
    for i in range(DEPTH):
        lw = (w_in[i], w_out[i], norm_pre[i], norm_post[i], ssd_conv_w[i], ssd_conv_b[i], ssd_a_log[i],
              ssd_dt_bias[i], ssd_d[i], ssd_norm[i], attn_sinks[i], sc_conv_w[i], ple_proj[i], ple_gate[i])
        yp, c1, s1, k1, v1, sc1 = _layer(yp, p_prompt[i], 0, z_ssd_buf, z_ssm, z_kv, z_kv, z_sc_buf, *lw)
        ys, c2, s2, k2, v2, sc2 = _layer(ys, p_sample[i], PAST_LEN, state_ssd_conv[i], state_ssm[i],
                                         cache_k[i], cache_v[i], state_sc_conv[i], *lw)
        pr_conv.append(c1); pr_ssm.append(s1); pr_k.append(k1); pr_v.append(v1); pr_sc.append(sc1)
        sa_conv.append(c2); sa_ssm.append(s2); sa_k.append(k2); sa_v.append(v2); sa_sc.append(sc2)
    return (yp, ys,
            jnp.stack(pr_conv), jnp.stack(pr_ssm), jnp.stack(pr_k), jnp.stack(pr_v), jnp.stack(pr_sc),
            jnp.stack(sa_conv), jnp.stack(sa_ssm), jnp.stack(sa_k), jnp.stack(sa_v), jnp.stack(sa_sc))


_drawn_inputs = setup_inputs


def setup_inputs(seed=0):
    import zlib

    import numpy as np

    out = dict(_drawn_inputs(seed))
    spreads = {}
    factors = {'norm_post': 3.053, 'ssd_d': 4.681, 'ssd_norm': 2.895, 'attn_sinks': 25.593}
    for name, (base, spread) in spreads.items():
        noise = np.random.default_rng([zlib.crc32(name.encode()), seed]).standard_normal(out[name].shape)
        drawn = base * np.exp(spread * noise) if base else spread * noise
        out[name] = __import__('jax').numpy.asarray(drawn.astype(out[name].dtype))
    for name, factor in factors.items():
        out[name] = (out[name] * factor).astype(out[name].dtype)
    return out
```

```python
from contextlib import ExitStack

import concourse.bass as bass
from concourse import mybir

F32 = mybir.dt.float32
F32R = mybir.dt.float32r
ALU = mybir.AluOpType
ACT = mybir.ActivationFunctionType
AX = mybir.AxisListType

P = 128
DEPTH = 2
DM = 2048
KT = DM // P
NPR = 256
NB, NS = 8, 4
NSM = NB * NS
T = NPR + NSM
G = 4
HG = 8
HD = 64
NST = 128
GW = HG * HD
EPS = 1e-6
BLK = P
UNIT = KT * BLK

PRE_U = 4
GRP_U = 22
OUT_U0 = PRE_U + G * GRP_U
OUT_U = 2 * KT
PLE_U0 = OUT_U0 + OUT_U
GATE_U0 = PLE_U0 + 2
LAYER_U = GATE_U0 + KT
LAYER_F = OUT_U0 + 3 * KT
NUNITS = DEPTH * LAYER_U

C_COS, C_SIN = 0, T
C_ID = 2 * T
C_TRI = C_ID + P
C_ONE = C_TRI + T
C_SEQ = C_ONE + P
C_EPS = C_SEQ + NB
NCONST = C_EPS + 2
NMASK = 3 * P + NB * P + NSM

G_CW, G_CB = 0, 24
G_D, G_NW = 30, 34
G_SW = 38
G_SK, G_SKS = 44, 48
NGP = 49

FW = 3 + NPR + NB * (3 + NS)
CW = FW - 3
SW_IN = 2 + NPR + NB * (2 + NS)
SW = SW_IN - 2


def hybrid_step(nc, wts, wdt, x0, p_t, npre, npost, gpar, dtpar, s0_t, kc_t, vc_t, cs_in, sc_in, consts, masks, resets,
                xs, kout, vout, kold, vold, conv_out, scv_out, ssm_p, ssm_s):
    ctx = ExitStack()
    with ctx:
        def sem(name):
            return ctx.enter_context(nc.semaphore(name))

        def sb(name, cols, dt=F32):
            return ctx.enter_context(nc.sbuf_tensor(name, [P, cols], dt))

        RAW = [sb(f"raw{i}", UNIT) for i in range(2)]
        WHI = [sb(f"whi{i}", UNIT, F32R) for i in range(2)]
        WLO = [sb(f"wlo{i}", UNIT, F32R) for i in range(2)]
        HHI = sb("h_hi", KT * T, F32R)
        HLO = sb("h_lo", KT * T, F32R)
        YX = sb("y_or_x", 2 * KT * T)
        CST = sb("cst", NCONST)
        GP = sb("gpar_sb", NGP)
        NRM = sb("norm_weights", 2 * KT)
        DTP = sb("dt_params", 4)
        TOK = sb("tok", 288)
        TG = sb("tok_group", 72)
        FB = [sb(f"conv_in{i}", FW) for i in range(2)]
        AB = [sb(f"conv_sum{i}", CW) for i in range(2)]
        TH = [sb(f"tanh{i}", CW) for i in range(2)]
        CSI = sb("conv_state_in", 6 * 24)
        CSO = sb("conv_state_out", 6 * 27)
        SCI = sb("short_state_in", 2 * 16)
        SCO = sb("short_state_out", 2 * 18)
        RS = sb("rs", T)
        RV = sb("rs_v", T)
        RA = sb("rs_a", T)
        SQ = sb("sq", T)
        work = ExitStack()
        WK_N = 16560
        WK = work.enter_context(nc.sbuf_tensor("work", [P, WK_N], F32))
        work.close()
        at = [0]

        def cut(n, restart=None):
            if restart is not None:
                at[0] = restart
            a = WK[:, at[0]:at[0] + n]
            at[0] += n
            assert at[0] <= WK_N, at[0]
            return a

        XC = cut(6 * T).rearrange("p (t n) -> p t n", n=T)
        Z2 = cut(4 * T).rearrange("p (t n) -> p t n", n=T)
        G2 = cut(2 * T).rearrange("p (t n) -> p t n", n=T)
        SCB = cut(T)
        SBB = cut(T)
        SG2 = cut(T)
        USC = FB[0][:, 1:1 + SW_IN]
        CSUM = AB[0][:, 0:SW]
        HEAVY = at[0]
        XDT = cut(3 * GW).rearrange("p (c n) -> p c n", c=3)
        XW = cut(3 * GW).rearrange("p (c n) -> p c n", c=3)
        S1 = XW[:, 0, :]
        BT = cut(3 * P).rearrange("p (c n) -> p c n", c=3)
        BM = cut(NB * P).rearrange("p (b n) -> p b n", b=NB)
        CBM = cut(T)
        MH = [cut(T) for _ in range(6)]
        EA = [cut(P + NSM) for _ in range(3)]
        DEC = cut(HG * 9).rearrange("p (h n) -> p h n", n=9)
        S0 = cut(GW)
        YT = cut(T)
        YS = cut(T)
        LATE = at[0]
        S0T = cut(NB * GW)
        Q = cut(2 * T, HEAVY).rearrange("p (t n) -> p t n", n=T)
        QS = cut(2 * T).rearrange("p (t n) -> p t n", n=T)
        QSM = cut(4 * NSM)
        KCUR = cut(T)
        KC = cut(NB * P)
        VC = cut(NB * HD).rearrange("p (b d) -> p b d", d=HD)
        VCUR = cut(3 * HD).rearrange("p (c d) -> p c d", d=HD)
        MSK = cut(NMASK)
        MX = cut(16)
        NM = cut(16)
        DEN = cut(16)
        OS = cut(2 * NSM).rearrange("p (a n) -> p a n", n=NSM)
        PR = cut(4 * 3 * P).rearrange("p (j n) -> p j n", j=4)
        PS = cut(NB * P + NSM)
        PT = cut(4 * 3 * P).rearrange("p (j n) -> p j n", j=4)
        PTS = cut(9 * P)
        XSQ = cut(KT * T, 0)
        DT0 = cut(T, HEAVY + 2400)
        AC0 = cut(T)
        W0 = cut(T)
        DTR = cut(T)
        DTE = cut(T)
        DTU = cut(T)
        DTC = cut(T)
        RST = cut(T)
        HF = [cut(T) for _ in range(4)]
        assert at[0] <= LATE
        KTT = cut(2 * T, LATE).rearrange("p (t n) -> p t n", n=T)
        KSW = cut(2 * T).rearrange("p (t n) -> p t n", n=T)
        VTT = cut(2 * T).rearrange("p (t n) -> p t n", n=T)
        VT = cut(2 * 3 * P).rearrange("p (t n) -> p t n", t=2)
        post = ctx.enter_context(ExitStack())
        YHI = post.enter_context(nc.sbuf_tensor("yssd_hi", [P, KT * T], F32R))
        YLO = post.enter_context(nc.sbuf_tensor("yssd_lo", [P, KT * T], F32R))
        MIX = post.enter_context(nc.sbuf_tensor("mix", [P, KT * T], F32))
        MSQ = [post.enter_context(nc.sbuf_tensor(f"mix_sq{i}", [P, T], F32)) for i in range(2)]
        assert 3 * KT * T + 2 * T <= WK_N and 2 * KT * T + UNIT - KT * T <= HEAVY + 2400
        DTRAW = YX[:, KT * T:KT * T + UNIT]
        PRAW = YX[:, KT * T:KT * T + 2 * T]

        COS, SIN = CST[:, C_COS:C_COS + T], CST[:, C_SIN:C_SIN + T]
        ID, ONES = CST[:, C_ID:C_ID + P], CST[:, C_ONE:C_ONE + P]
        TRI = CST[:, C_TRI:C_TRI + T]
        TGV = TG[:, :].rearrange("p (c v h) -> p c v h", c=3, v=3)

        MAIN = [ctx.enter_context(nc.psum_tensor(f"main{i}", [P, 512], F32)) for i in range(2)]

        class Bank:

            def __init__(self, name, pre, grp, post_):
                self.t = ctx.enter_context(nc.psum_tensor(name, [P, 512], F32))
                self.full, self.free = sem(name + "_full"), sem(name + "_free")
                self.pre, self.grp, self.per = pre, grp, pre + G * grp + post_

            def in_pre(self, L, n):
                return L * self.per + (n + 1)

            def in_grp(self, L, g, n):
                return L * self.per + g * self.grp + (self.pre + n + 1)

            def in_post(self, L, n):
                return L * self.per + (self.pre + G * self.grp + n + 1)

        A0, A1 = Bank("a0", 0, 11, 0), Bank("a1", 0, 10, 0)
        YB, YO = Bank("yb", 0, 5, 0), Bank("yo", 0, 5, 0)
        T0, T1 = Bank("t0", 3, 9, 1), Bank("t1", 2, 9, 0)
        SIDE = [A0, A1, YB, YO, T0, T1]

        raw_landed = [sem(f"raw_landed{i}") for i in range(2)]
        hi_done, lo_done, lop_done = sem("hi_done"), sem("lo_done"), sem("lop_done")
        units_used, filled = sem("units_used"), sem("filled")
        bank_free = [sem(f"main_free{i}") for i in range(2)]
        const_in, layer_in, dtw_in, xres_in, p_in = (sem(n) for n in ("const_in", "layer_in", "dtw_in", "xres_in", "p_in"))
        x_first, x_final, x_stored, x_slab0 = (sem(n) for n in ("x_first", "x_final", "x_stored", "x_slab0"))
        xsq_done, xsq_sum, h_scaled, h_hi, h_lo = (sem(n) for n in ("xsq_done", "xsq_sum", "h_scaled", "h_hi", "h_lo"))
        norm_ln = sem("norm_ln")
        dt_hi, dt_lo = sem("dt_hi"), sem("dt_lo")
        dt_abs, dt_exp, dt_u, dt_ln, dt_ac, dt_wexp, dt_ready, tok_ready = (
            sem(n) for n in ("dt_abs", "dt_exp", "dt_u", "dt_ln", "dt_ac", "dt_wexp", "dt_ready", "tok_ready"))
        k_swapped, k_ready, v_ready, v_tok, k_stored, v_stored = (
            sem(n) for n in ("k_swapped", "k_ready", "v_ready", "v_tok", "k_stored", "v_stored"))
        old_copied = sem("old_copied")
        gp_in, att_in, st_in, sin_in = sem("gp_in"), sem("att_in"), sem("st_in"), sem("sin_in")
        q_swapped, q_ready, qsm_ready = sem("q_swapped"), sem("q_ready"), sem("qsm_ready")
        th_ready, th_used = sem("th_ready"), sem("th_used")
        att_max, att_exp, att_prob, smp_max, smp_exp, smp_prob = (
            sem(n) for n in ("att_max", "att_exp", "att_prob", "smp_max", "smp_exp", "smp_prob"))
        pt_ready, pts_ready, os_ready, att_done = (
            sem(n) for n in ("pt_ready", "pts_ready", "os_ready", "att_done"))
        tap_done, conv_sum, xc_ready, conv_saved, csout_stored = (
            sem(n) for n in ("tap_done", "conv_sum", "xc_ready", "conv_saved", "csout_stored"))
        tg_ready, z_ready, bt_ready, bm_ready, cb_ready, xt_ready = (
            sem(n) for n in ("tg_ready", "z_ready", "bt_ready", "bm_ready", "cb_ready", "xt_ready"))
        decay_ready, mh_ready, ea_ready, s0_ready, y_used, y_gated, y_sq = (
            sem(n) for n in ("decay_ready", "mh_ready", "ea_ready", "s0_ready", "y_used", "y_gated", "y_sq"))
        s1_ready, smp_state, smp_scaled, s1_stored, state_stored, ssd_done = (
            sem(n) for n in ("s1_ready", "smp_state", "smp_scaled", "s1_stored", "state_stored", "ssd_done"))
        c_ready, u_ready, b_ready, stap_done, sc_done, sc_saved, scout_stored = (
            sem(n) for n in ("c_ready", "u_ready", "b_ready", "stap_done", "sc_done", "sc_saved", "scout_stored"))
        y_hi, y_lo, mix_sq, mix_added, p_hi, p_lo = (
            sem(n) for n in ("y_hi", "y_lo", "mix_sq", "mix_added", "p_hi", "p_lo"))
        x_mid, x_hi, x_lo = sem("x_mid"), sem("x_hi"), sem("x_lo")

        passed = {e: sem("passed_" + e) for e in ("pe", "dve", "pool")}

        def wait_alone(eng, name, s, v):
            eng.wait_ge(s, v)
            eng.sem_inc(passed[name], 1)

        def unit(L, k):
            return L * LAYER_U + k

        def gunit(L, g, k):
            return L * LAYER_U + g * GRP_U + (PRE_U + k)

        def fill_bank(L, g, k):
            return L * (LAYER_F // 2) + g * (GRP_U // 2) + (PRE_U // 2 + k // 2 + 1)

        def gfill(L, g, k):
            return L * LAYER_F + g * GRP_U + (PRE_U + k + 1)

        def it(L, g, per=1, n=0):
            return L * (G * per) + g * per + (n + 1)

        def smp(ap, w=NS):
            return ap.rearrange("p (b t) -> p b t", t=w)

        def fsmp(ap, k):
            return smp(ap[:, k + NPR:k + NPR + NB * (k + NS)], k + NS)

        def pool_blocks(k):
            return 12 if k is not None and k >= 14 else 8

        block = ctx.enter_context(nc.Block())

        @block.sync
        def _(sp):
            def load_unit(u, s, guard=True):
                if guard:
                    sp.wait_ge(hi_done, u - 1)
                    sp.wait_ge(lo_done, u - 1)
                    sp.wait_ge(lop_done, u - 1)
                sp.dma_start(RAW[s][:, :], wts[u]).then_inc(raw_landed[s], 16)

            sp.dma_start(YX[:, 0:KT * T], x0).then_inc(x_first, 16)
            sp.dma_start(CST[:, :], consts).then_inc(const_in, 16)
            sp.wait_ge(x_first, 16)
            sp.dma_start(xs[0], YX[:, 0:KT * T]).then_inc(x_slab0, 16)
            with sp.Fori(0, DEPTH) as L:
                sp.wait_ge(x_final, L + 1)
                for k in range(2):
                    load_unit(unit(L, k), k, False)
                sp.dma_start(DTRAW, wdt[L]).then_inc(dtw_in, 16)
                sp.dma_start(NRM[:, 0:KT], npre[L]).then_inc(layer_in, 16)
                sp.dma_start(NRM[:, KT:2 * KT], npost[L]).then_inc(layer_in, 16)
                sp.dma_start(DTP[0:32, 0:2], dtpar[L]).then_inc(layer_in, 16)
                sp.dma_start(RST[0:32, :], resets).then_inc(layer_in, 16)
                for k in (2, 3):
                    load_unit(unit(L, k), k % 2)
                with sp.Fori(0, G) as g:
                    for k in range(GRP_U):
                        load_unit(gunit(L, g, k), k % 2)
                        if k == 2:
                            sp.wait_ge(smp_state, it(L, g))
                            sp.wait_ge(y_sq, it(L, g))
                            sp.wait_ge(s1_stored, L * (G * 16) + g * 16 + 16)
                            sp.wait_ge(k_stored, L * 32 + 32)
                            sp.wait_ge(v_stored, L * 128 + 128)
                            for r in range(2):
                                sp.dma_start(KCUR[64 * r:64 * r + 64, :], kout[L, g]).then_inc(att_in, 16)
                            sp.dma_start(KC[0:64, :], kc_t[L, g]).then_inc(att_in, 16)
                            sp.dma_start(VC, vc_t[L, g].rearrange("w (b d) -> w b d", d=HD)).then_inc(att_in, 16)
                            v_g = vout[L, g]
                            sp.dma_start(VCUR[:, 0:2, :], v_g[0:NPR].rearrange("(c p) d -> p c d", p=P)).then_inc(att_in, 16)
                            sp.dma_start(VCUR[0:NSM, 2, :], v_g[NPR:T]).then_inc(att_in, 16)
                            sp.dma_start(MSK, masks).then_inc(att_in, 16)
                        if k == 4:
                            sp.wait_ge(ssd_done, it(L, g))
                            sp.wait_ge(conv_saved, L * (G * 6) + g * 6 + 2)
                            sp.dma_start(GP[:, :], gpar[L, g]).then_inc(gp_in, 16)
                            sp.dma_start(CSI[:, :], cs_in[L, g]).then_inc(sin_in, 16)
                            sp.dma_start(SCI[:, :], sc_in[L, g]).then_inc(sin_in, 16)
                        if k == 14:
                            sp.wait_ge(att_done, it(L, g))
                            sp.dma_start(S0T, s0_t[L, g]).then_inc(st_in, 16)
                with sp.Fori(0, KT // 2) as m:
                    for k in range(4):
                        load_unit(L * LAYER_U + m * 4 + (OUT_U0 + k), k % 2)
                for k in range(2):
                    load_unit(unit(L, PLE_U0 + k), k)
                sp.wait_ge(y_hi, L * 8 + 8)
                sp.wait_ge(y_lo, L * 8 + 8)
                sp.wait_ge(x_slab0, 16)
                sp.wait_ge(x_stored, L * 16 + 16)
                sp.dma_start(YX[:, 0:KT * T], xs[L]).then_inc(xres_in, 16)
                sp.dma_start(PRAW, p_t[L]).then_inc(p_in, 16)
                with sp.Fori(0, KT // 2) as m:
                    for k in range(2):
                        load_unit(L * LAYER_U + m * 2 + (GATE_U0 + k), k % 2)
                sp.wait_ge(x_final, L + 2)
                sp.dma_start(xs[L + 1], YX[:, 0:KT * T]).then_inc(x_stored, 16)
            sp.wait_ge(x_stored, DEPTH * 16 + 16)

        @block.tensor
        def _(pe):
            mm, tr = nc.tensor.matmul, nc.tensor.transpose

            wait = pe.wait_ge

            def product(out, s, n, hi, lo, k, start, stop):
                w_hi, w_lo = WHI[s][:, n * BLK:(n + 1) * BLK], WLO[s][:, n * BLK:(n + 1) * BLK]
                x_hi_, x_lo_ = hi[:, k * T:(k + 1) * T], lo[:, k * T:(k + 1) * T]
                mm(out, w_hi, x_hi_, start=start, stop=False)
                mm(out, w_hi, x_lo_, start=False, stop=False)
                return mm(out, w_lo, x_hi_, start=False, stop=stop)

            def wait_unit(u):
                wait(hi_done, u + 1)
                wait(lo_done, u + 1)
                wait(lop_done, u + 1)

            def project(u, b, fb):
                wait_unit(u)
                wait(bank_free[b], fb)
                for k in range(KT):
                    last = product(MAIN[b][:, 0:T], b, k, HHI, HLO, k, k == 0, k == KT - 1)
                last.then_inc(filled, 1)
                pe.drain().then_inc(units_used, 1)

            pe.sem_inc(units_used, 2)
            for b in bank_free:
                pe.sem_inc(b, 1)
            for bk in SIDE:
                pe.sem_inc(bk.free, 1)
            wait(const_in, 16)
            with pe.Fori(0, DEPTH) as L:
                wait(xsq_sum, L + 1)
                wait(T0.free, T0.in_pre(L, 0))
                for j in range(4):
                    last = mm(T0.t[:, 0:T], ONES, XSQ[:, j * T:(j + 1) * T], start=(j == 0), stop=(j == 3))
                last.then_inc(T0.full, 1)
                for k in range(PRE_U):
                    if k == 0:
                        wait_unit(unit(L, 0))
                        wait(bank_free[0], L * (LAYER_F // 2) + 1)
                        for n in range(KT):
                            wait(h_hi, L * KT + (n + 1))
                            wait(h_lo, L * KT + (n + 1))
                            last = product(MAIN[0][:, 0:T], 0, n, HHI, HLO, n, n == 0, n == KT - 1)
                        last.then_inc(filled, 1)
                        pe.drain().then_inc(units_used, 1)
                        wait(dt_hi, L + 1)
                        wait(dt_lo, L + 1)
                        wait(T1.free, T1.in_pre(L, 0))
                        for n in range(KT):
                            w, wl = YHI[:, n * BLK:(n + 1) * BLK], YLO[:, n * BLK:(n + 1) * BLK]
                            c0 = n * T
                            mm(T1.t[:, 0:T], w, HHI[:, c0:c0 + T], start=(n == 0), stop=False)
                            mm(T1.t[:, 0:T], w, HLO[:, c0:c0 + T], start=False, stop=False)
                            last = mm(T1.t[:, 0:T], wl, HHI[:, c0:c0 + T], start=False, stop=(n == KT - 1))
                        last.then_inc(T1.full, 1)
                    else:
                        project(unit(L, k), k % 2, L * (LAYER_F // 2) + (k // 2 + 1))
                    if k == 2:
                        wait(dt_ready, L + 1)
                        wait_alone(pe, "pe", T0.free, T0.in_pre(L, 1))
                        for v, a in enumerate((DT0, AC0, W0)):
                            for c in range(3):
                                n = P if c < 2 else NSM
                                last = tr(T0.t[0:n, c * 96 + v * 32:c * 96 + v * 32 + 32], a[0:32, c * P:c * P + n], ID[0:32, 0:32])
                        last.then_inc(T0.full, 1)
                for i, bk in enumerate((T0, T1)):
                    wait(v_ready, L * 2 + (i + 1))
                    wait(bk.free, bk.in_pre(L, 2 if i == 0 else 1))
                    for c in range(3):
                        n = P if c < 2 else NSM
                        last = tr(bk.t[0:n, c * P:c * P + P], VTT[:, i, c * P:c * P + n], ID)
                    last.then_inc(bk.full, 1)

                with pe.Fori(0, G) as g:
                    def use(bk, n):
                        wait(bk.free, bk.in_grp(L, g, n))

                    def scores(j):
                        bk = (A0, A1)[j % 2]
                        a, r = j // 2, 64 * (j % 2)
                        use(bk, j // 2)
                        q, kk = Q[r:r + 64, a, :], KCUR[r:r + 64, :]
                        mm(bk.t[:, 0:P], q[:, 0:P], kk[:, 0:P], start=True, stop=True)
                        mm(bk.t[:, P:3 * P], q[:, P:2 * P], kk[:, 0:2 * P], start=True, stop=True).then_inc(bk.full, 1)

                    def turn_probs(j):
                        bk = (T0, T1)[j % 2]
                        use(bk, j // 2)
                        for c in range(3):
                            last = tr(bk.t[:, c * P:c * P + P], PR[:, j, c * P:c * P + P], ID)
                        last.then_inc(bk.full, 1)

                    def values(j):
                        bk = (YB, YO)[j // 2]
                        r = 64 * (j % 2)
                        if j % 2 == 0:
                            use(bk, 0)
                        wait(pt_ready, it(L, g, 4, j))
                        mm(bk.t[r:r + 64, 0:P], VCUR[:, 0, :], PT[:, j, 0:P], start=True, stop=True)
                        mm(bk.t[r:r + 64, P:2 * P], VCUR[:, 0, :], PT[:, j, P:2 * P], start=True, stop=False)
                        last = mm(bk.t[r:r + 64, P:2 * P], VCUR[:, 1, :], PT[:, j, 2 * P:3 * P], start=False, stop=True)
                        if j % 2:
                            last.then_inc(bk.full, 1)

                    def decay(h):
                        bk, n = ((A0, 5), (A1, 4))[h % 2]
                        use(bk, n + h // 2)
                        for c in range(3):
                            w = P if c < 2 else NSM
                            last = mm(bk.t[:, c * P:c * P + w], TGV[0:w, c, 1, h:h + 1].to_broadcast([w, P]), ID[0:w, 0:w],
                                      start=True, stop=True)
                        last.then_inc(bk.full, 1)

                    def y_pair(i):
                        use(YB, 1 + i)
                        for r in range(2):
                            h = 2 * i + r
                            wait(mh_ready, it(L, g, HG, h))
                            m = MH[h % 6]
                            for c in range(3):
                                w = P if c < 2 else NSM
                                last = mm(YB.t[64 * r:64 * r + 64, c * P:c * P + w], XDT[0:w, c, h * HD:(h + 1) * HD],
                                          m[0:w, c * P:c * P + w], start=True, stop=True)
                        last.then_inc(YB.full, 1)
                        use(YO, 1 + i)
                        cc = XC[:, 1, :]
                        mm(YO.t[:, 0:P], S0[:, i * P:(i + 1) * P], cc[:, P:2 * P], start=True, stop=True)
                        for b in range(NB):
                            last = mm(YO.t[:, P + NS * b:P + NS * b + NS], S0T[:, b * GW + i * P:b * GW + (i + 1) * P],
                                      cc[:, NPR + NS * b:NPR + NS * b + NS], start=True, stop=True)
                        last.then_inc(YO.full, 1)

                    def new_state(b, bk, n):
                        use(bk, n)
                        mm(bk.t[:, :], BM[0:NSM, b, :], XW[0:NSM, 2, :], start=True, stop=True).then_inc(bk.full, 1)

                    for k in range(GRP_U):
                        project(gunit(L, g, k), k % 2, fill_bank(L, g, k))
                        if k == 2:
                            wait(q_ready, it(L, g, 2, 1))
                            wait(att_in, L * (G * 112) + g * 112 + 112)
                            scores(0)
                            scores(1)
                        if k == 3:
                            scores(2)
                            scores(3)
                        if k in (4, 5):
                            wait(qsm_ready, it(L, g))
                            for s, bk, n in ((0, A0, 2), (1, A1, 2)) if k == 4 else ((2, A0, 3),):
                                use(bk, n)
                                keys = KC[0:64, s * 512:s * 512 + 512] if s < 2 else KCUR[0:64, NPR:T]
                                w = 512 if s < 2 else NSM
                                mm(bk.t[:, 0:w], QSM[0:64, :], keys, start=True, stop=True).then_inc(bk.full, 1)
                        if k == 6:
                            wait(att_prob, it(L, g))
                            turn_probs(0)
                            turn_probs(1)
                        if k == 7:
                            turn_probs(2)
                            turn_probs(3)
                            values(0)
                            values(1)
                        if k == 8:
                            values(2)
                            values(3)
                            wait(smp_prob, it(L, g))
                            for bk, b0 in ((T0, 0), (T1, 4)):
                                use(bk, 2)
                                for b in range(4):
                                    last = tr(bk.t[:, b * P:b * P + P], PS[:, (b0 + b) * P:(b0 + b + 1) * P], ID)
                                last.then_inc(bk.full, 1)
                        if k == 9:
                            wait_alone(pe, "pe", T0.free, T0.in_grp(L, g, 3))
                            tr(T0.t[0:NSM, 0:P], PS[:, NB * P:NB * P + NSM], ID).then_inc(T0.full, 1)
                            wait(pts_ready, it(L, g))
                            use(A1, 3)
                            o = A1.t[0:64, 0:P]
                            mm(o, VCUR[0:NSM, 2, :], PTS[0:NSM, NB * P:9 * P], start=True, stop=False, skip_group_check=True)
                            for b in range(NB):
                                mine = PTS[:, b * P:b * P + P].rearrange("p (j n) -> p j n", j=4)[:, :, NS * b:NS * b + NS]
                                last = mm(o.rearrange("p (j n) -> p j n", j=4)[:, :, NS * b:NS * b + NS], VC[:, b, :], mine,
                                          start=False, stop=(b == NB - 1), skip_group_check=True)
                            last.then_inc(A1.full, 1)
                        if k == 10:
                            wait(xc_ready, it(L, g, 6, 1) + 2)
                            use(T1, 3)
                            use(A0, 4)
                            for c in range(3):
                                w = P if c < 2 else NSM
                                last = tr(T1.t[0:w, c * P:c * P + P], XC[:, 0, c * P:c * P + w], ID)
                            last.then_inc(T1.full, 1)
                            for c in range(3):
                                w = P if c < 2 else NSM
                                last = mm(A0.t[0:w, c * P:c * P + w], XC[:, 0, c * P:c * P + w], XC[:, 1, c * P:c * P + w],
                                          start=True, stop=True)
                            last.then_inc(A0.full, 1)
                        if k in (14, 15):
                            wait(xc_ready, it(L, g, 6, 5) + 2)
                            for c in (0, 1) if k == 14 else (2,):
                                bk, n = ((T0, 4), (T1, 4), (T0, 5))[c]
                                w = P if c < 2 else NSM
                                use(bk, n)
                                for i in range(4):
                                    last = tr(bk.t[0:w, i * P:i * P + P], XC[:, 2 + i, c * P:c * P + w], ID)
                                last.then_inc(bk.full, 1)
                        if k == 15:
                            wait(xt_ready, it(L, g, 3, 1))
                            wait(bt_ready, it(L, g))
                            use(T1, 5)
                            mm(T1.t[:, :], BT[:, 0, :], XW[:, 0, :], start=True, stop=True).then_inc(T1.full, 1)
                        if 14 <= k < 18:
                            if k == 14:
                                wait(tg_ready, it(L, g))
                            decay(2 * (k - 14))
                            decay(2 * (k - 14) + 1)
                        if 16 <= k < 20:
                            if k == 16:
                                wait(xt_ready, it(L, g, 3, 2))
                                wait(s0_ready, it(L, g))
                                wait(st_in, L * (G * 16) + g * 16 + 16)
                            y_pair(k - 16)
                        if k == 17:
                            use(T0, 6)
                            mm(T0.t[:, :], BT[:, 1, :], XW[:, 1, :], start=True, stop=True).then_inc(T0.full, 1)
                        if k in (19, 20):
                            if k == 19:
                                wait(bm_ready, it(L, g))
                            for b, (bk, n) in enumerate(((T1, 6), (T0, 7), (A0, 9), (A1, 8))):
                                new_state(4 * (k - 19) + b, bk, n + (k - 19))
                        if k == 21:
                            wait(y_sq, it(L, g) + 1)
                            use(T1, 8)
                            mm(T1.t[:, 0:T], ONES, SQ[:, :], start=True, stop=True).then_inc(T1.full, 1)

                def out_tile(u, b, fb, pieces):
                    wait_unit(u)
                    wait(bank_free[b], fb)
                    for k in range(KT):
                        if pieces and k % 4 == 0:
                            wait(y_hi, L * 8 + (k // 4 + 1))
                            wait(y_lo, L * 8 + (k // 4 + 1))
                        last = product(MAIN[b][:, 0:T], 0, k, HHI, HLO, k, k == 0, False)
                    pe.drain().then_inc(units_used, 1)
                    wait_unit(u + 1)
                    for k in range(KT):
                        if pieces and k % 4 == 0:
                            wait(y_hi, L * 8 + (4 + k // 4 + 1))
                            wait(y_lo, L * 8 + (4 + k // 4 + 1))
                        last = product(MAIN[b][:, 0:T], 1, k, YHI, YLO, k, False, k == KT - 1)
                    last.then_inc(filled, 1)
                    pe.drain().then_inc(units_used, 1)

                fb0 = LAYER_F // 2
                for m in range(2):
                    out_tile(unit(L, OUT_U0 + 2 * m), m, L * fb0 + (OUT_U0 // 2 + 1), True)
                with pe.Fori(1, KT // 2) as mp:
                    for m in range(2):
                        out_tile(L * LAYER_U + mp * 4 + (OUT_U0 + 2 * m), m, L * fb0 + mp + (OUT_U0 // 2 + 1), False)
                wait(mix_added, L * KT + (KT + 2))
                wait(T0.free, T0.in_post(L, 0))
                mm(T0.t[:, 0:T], ONES, SQ[:, :], start=True, stop=True).then_inc(T0.full, 1)
                wait(p_hi, L + 1)
                wait(p_lo, L + 1)
                for s in range(2):
                    wait_unit(unit(L, PLE_U0 + s))
                    for m in range(8):
                        wait(bank_free[m % 2], L * fb0 + ((OUT_U0 + KT + 8 * s) // 2 + m // 2 + 1))
                        product(MAIN[m % 2][:, 0:T], s, 2 * m, YHI, YLO, 0, True, False)
                        product(MAIN[m % 2][:, 0:T], s, 2 * m + 1, YHI, YLO, 1, False, True).then_inc(filled, 1)
                    pe.drain().then_inc(units_used, 1)
                for m in range(2):
                    wait_unit(unit(L, GATE_U0 + m))
                    wait(bank_free[m], L * fb0 + ((OUT_U0 + 2 * KT) // 2 + 1))
                    for k in range(KT):
                        if m == 0:
                            wait(x_hi, L * KT + (k + 1))
                            wait(x_lo, L * KT + (k + 1))
                        last = product(MAIN[m][:, 0:T], m, k, HHI, HLO, k, k == 0, k == KT - 1)
                    last.then_inc(filled, 1)
                    pe.drain().then_inc(units_used, 1)
                with pe.Fori(1, KT // 2) as mp:
                    for m in range(2):
                        project(L * LAYER_U + mp * 2 + (GATE_U0 + m), m, L * fb0 + mp + ((OUT_U0 + 2 * KT) // 2 + 1))

        @block.scalar
        def _(act):
            fn = nc.scalar.activation

            def split_hi(u, s, h=None):
                act.wait_ge(units_used, u + 1)
                act.wait_ge(raw_landed[s], h)
                fn(WHI[s][:, :], RAW[s][:, :], ACT.Copy).then_inc(hi_done, 1)

            def landed(L, k, g=0, gper=0, m=0, mper=0):
                v = L * (LAYER_U // 2 * 16) + (k // 2 * 16 + 16)
                if gper:
                    v = v + g * (gper // 2 * 16)
                return v

            def swap(dst, src):
                for a, b in ((0, 32), (32, 0), (64, 96), (96, 64)):
                    last = fn(dst[a:a + 32, :], src[b:b + 32, 0:T], ACT.Copy)
                return last

            def rsqrt(bank, ready, inv, eps_col):
                act.wait_ge(bank.full, ready)
                fn(RV[:, :], bank.t[:, 0:T], ACT.Ln, scale=inv, bias=CST[:, eps_col:eps_col + 1])
                act.drain()
                fn(RS[:, :], RV[:, :], ACT.Exp, scale=-0.5).then_inc(norm_ln, 1)

            act.dma_start(kold, kc_t.rearrange("l g d (b w) -> (l g d) b w", w=P)[:, :, NS:P]).then_inc(old_copied, 16)
            act.dma_start(vold, vc_t[:, :, NS:P, :].rearrange("l g w n -> (l g) w n")).then_inc(old_copied, 16)
            act.wait_ge(const_in, 16)
            act.sem_inc(state_stored, 16)
            act.sem_inc(s1_stored, 16)
            act.sem_inc(csout_stored, 16)
            act.sem_inc(scout_stored, 16)
            with act.Fori(0, DEPTH) as L:
                act.wait_ge(x_final, L + 1)
                for j in range(4):
                    fn(XSQ[:, j * 4 * T:(j + 1) * 4 * T], YX[:, j * 4 * T:(j + 1) * 4 * T], ACT.Square).then_inc(xsq_done, 1)
                split_hi(unit(L, 0), 0, landed(L, 0))
                rsqrt(T0, T0.in_pre(L, 0), 1.0 / DM, C_EPS)
                for i in range(KT):
                    act.wait_ge(h_scaled, L * KT + (i + 1))
                    fn(HHI[:, i * T:(i + 1) * T], HF[i % 4], ACT.Copy).then_inc(h_hi, 1)
                act.wait_ge(dtw_in, L * 16 + 16)
                fn(YHI[:, 0:UNIT], DTRAW, ACT.Copy).then_inc(dt_hi, 1)
                split_hi(unit(L, 1), 1, landed(L, 1))
                act.wait_ge(layer_in, L * 64 + 64)
                fn(DTP[0:32, 2:3], DTP[0:32, 1:2], ACT.Exp)
                for k in range(PRE_U):
                    act.wait_ge(filled, L * LAYER_F + (k + 1))
                    split_hi(unit(L, k + 2), k % 2, landed(L, k + 2))
                    if k < 2:
                        swap(KSW[:, k, :], MAIN[k % 2]).then_inc(k_swapped, 1)
                    else:
                        fn(VTT[:, k - 2, :], MAIN[k % 2][:, 0:T], ACT.Copy).then_inc(v_ready, 1)
                        act.drain().then_inc(bank_free[k % 2], 1)
                    if k == 0:
                        act.wait_ge(dt_abs, L + 1)
                        fn(DTE[0:32, :], DTU[0:32, :], ACT.Exp, scale=-1.0).then_inc(dt_exp, 1)
                        act.wait_ge(dt_u, L + 1)
                        fn(DTC[0:32, :], DTU[0:32, :], ACT.Ln).then_inc(dt_ln, 1)
                    if k == 1:
                        act.wait_ge(dt_ac, L + 1)
                        fn(W0[0:32, :], DTE[0:32, :], ACT.Exp, scale=-1.0).then_inc(dt_wexp, 1)
                    if k == 2:
                        for i in range(2):
                            act.wait_ge(k_ready, L * 2 + (i + 1))
                            act.dma_start(kout[L, 2 * i:2 * i + 2].rearrange("h d n -> (h d) n"), KTT[:, i, :]).then_inc(k_stored, 16)
                        act.wait_ge(T0.full, T0.in_pre(L, 1))
                        fn(TOK[:, 0:192], T0.t[:, 0:192], ACT.Copy)
                        fn(TOK[0:NSM, 192:288], T0.t[0:NSM, 192:288], ACT.Copy).then_inc(tok_ready, 1)
                        act.drain().then_inc(T0.free, 1)
                for i, bk in enumerate((T0, T1)):
                    act.wait_ge(bk.full, bk.in_pre(L, 2 if i == 0 else 1))
                    fn(VT[:, i, 0:2 * P], bk.t[:, 0:2 * P], ACT.Copy)
                    fn(VT[0:NSM, i, 2 * P:3 * P], bk.t[0:NSM, 2 * P:3 * P], ACT.Copy).then_inc(v_tok, 1)
                    act.wait_ge(v_tok, L * 2 + (i + 1))
                    for h in range(2):
                        v_h = VT[:, i, :].rearrange("p (c h d) -> p c h d", c=3, h=2)[:, :, h, :]
                        act.dma_start(vout[L, 2 * i + h, 0:NPR].rearrange("(c p) d -> p c d", p=P), v_h[:, 0:2]).then_inc(v_stored, 16)
                        act.dma_start(vout[L, 2 * i + h, NPR:T], v_h[0:NSM, 2]).then_inc(v_stored, 16)
                    act.drain().then_inc(bk.free, 1)

                with act.Fori(0, G) as g:
                    th_n = [0]

                    def tanh_half(src, w, tag=None):
                        n = th_n[0]
                        th_n[0] += 1
                        act.wait_ge(th_used, L * 72 + g * 14 + (n + 1))
                        fn(TH[n % 2][:, 0:w], src, ACT.Tanh, scale=0.5).then_inc(th_ready, 1)

                    def decay_exp(h):
                        bk, n = ((A0, 5), (A1, 4))[h % 2]
                        m, i, r = MH[h % 6], h // 2, 64 * (h % 2)
                        act.wait_ge(bk.full, bk.in_grp(L, g, n + h // 2))
                        act.wait_ge(y_used, L * 16 + g * 4 + (i - 2 if i >= 3 else 0) + 1)
                        for c in range(2):
                            fn(m[:, c * P:(c + 1) * P], bk.t[:, c * P:(c + 1) * P], ACT.Relu, scale=-1.0, bias=TGV[:, c, 1, h:h + 1])
                        fn(m[0:NSM, NPR:T], bk.t[0:NSM, NPR:T], ACT.Relu, scale=-1.0, bias=TGV[0:NSM, 2, 1, h:h + 1])
                        fn(EA[i % 3][r:r + 64, :], bk.t[r:r + 64, P:T], ACT.Exp)
                        fn(DEC[:, h, :], bk.t[:, NPR - 1:T:4], ACT.Exp).then_inc(bk.free, 1)
                        act.drain()
                        fn(m[:, 0:NPR], m[:, 0:NPR], ACT.Exp, scale=-1.0)
                        fn(m[0:NSM, NPR:T], m[0:NSM, NPR:T], ACT.Exp, scale=-1.0).then_inc(decay_ready, 1)

                    for k in range(GRP_U):
                        b = k % 2
                        main = MAIN[b]
                        act.wait_ge(filled, gfill(L, g, k))
                        split_hi(gunit(L, g, k + 2), b, L * (LAYER_U // 2 * 16) + g * (GRP_U // 2 * 16) + ((PRE_U + k + 2) // 2 * 16 + 16))
                        if k < 2:
                            swap(QS[:, k, :], main).then_inc(q_swapped, 1)
                        if k in (2, 3) or 4 <= k < 8:
                            tanh_half(main[:, 0:T], T)
                        if k == 2:
                            act.wait_ge(q_ready, it(L, g, 2, 1))
                            for j in range(4):
                                last = fn(QSM[0:64, j * NSM:(j + 1) * NSM], Q[64 * (j % 2):64 * (j % 2) + 64, j // 2, NPR:T], ACT.Copy)
                            last.then_inc(qsm_ready, 1)
                        if 8 <= k < 14:
                            t = k - 8
                            f, s = FB[t % 2], AB[t % 2]
                            if t == 0:
                                act.wait_ge(sin_in, L * (G * 32) + g * 32 + 32)
                                act.wait_ge(gp_in, L * (G * 16) + g * 16 + 16)
                            act.wait_ge(xc_ready, L * (G * 6) + g * 6 + (t + 1))
                            act.wait_ge(conv_saved, L * (G * 6) + g * 6 + (t + 1))
                            fn(fsmp(f, 3)[:, :, 0:3], smp(CSI[:, t * 24:(t + 1) * 24], 3), ACT.Copy)
                            fn(f[:, 3:3 + NPR], main[:, 0:NPR], ACT.Copy)
                            fn(fsmp(f, 3)[:, :, 3:7], smp(main[:, NPR:T]), ACT.Copy).then_inc(bank_free[b], 1)
                            act.drain()
                            fn(s[:, :], f[:, 0:CW], ACT.Identity, scale=GP[:, G_CW + 4 * t:G_CW + 4 * t + 1],
                               bias=GP[:, G_CB + t:G_CB + t + 1]).then_inc(tap_done, 1)
                            act.wait_ge(conv_sum, it(L, g, 6, t))
                            tanh_half(s[:, :], CW)
                        if k == 5:
                            act.wait_ge(att_max, it(L, g))
                            for j in range(4):
                                for c, (c0, c1) in enumerate(((0, P), (P, 3 * P))):
                                    fn(PR[:, j, c0:c1], PR[:, j, c0:c1], ACT.Exp, scale=HD ** -0.5, bias=NM[:, 2 * j + c:2 * j + c + 1],
                                       accum_out=DEN[:, 2 * j + c:2 * j + c + 1])
                            fn(MX[:, 0:8], MX[:, 0:8], ACT.Exp).then_inc(att_exp, 1)
                        if k == 6:
                            act.wait_ge(smp_max, it(L, g))
                            fn(PS, PS, ACT.Exp, scale=HD ** -0.5, bias=NM[:, 8:9], accum_out=DEN[:, 8:9])
                            fn(MX[:, 8:9], MX[:, 8:9], ACT.Exp).then_inc(smp_exp, 1)
                        if k in (7, 8):
                            if k == 7:
                                act.wait_ge(state_stored, L * (G * 16) + g * 16 + 16)
                            for j in (0, 1) if k == 7 else (2, 3):
                                bk = (T0, T1)[j % 2]
                                act.wait_ge(bk.full, bk.in_grp(L, g, j // 2))
                                fn(PT[:, j, :], bk.t[:, 0:3 * P], ACT.Copy).then_inc(pt_ready, 1)
                                act.drain().then_inc(bk.free, 1)
                        if k == 9:
                            for bk, b0 in ((T0, 0), (T1, 4)):
                                act.wait_ge(bk.full, bk.in_grp(L, g, 2))
                                fn(PTS[:, b0 * P:(b0 + 4) * P], bk.t[:, :], ACT.Copy).then_inc(bk.free, 1)
                            act.wait_ge(T0.full, T0.in_grp(L, g, 3))
                            fn(PTS[0:NSM, NB * P:9 * P], T0.t[0:NSM, 0:P], ACT.Copy).then_inc(pts_ready, 1)
                            act.drain().then_inc(T0.free, 1)
                        if k == 10:
                            act.wait_ge(A1.full, A1.in_grp(L, g, 3))
                            for j in range(4):
                                r = 64 * (j % 2)
                                last = fn(OS[r:r + 64, j // 2, :], A1.t[0:64, j * NSM:(j + 1) * NSM], ACT.Copy)
                            last.then_inc(os_ready, 1)
                            act.drain().then_inc(A1.free, 1)
                        if k == 11:
                            act.wait_ge(att_done, it(L, g))
                            act.wait_ge(T1.full, T1.in_grp(L, g, 3))
                            fn(BT[:, 0:2, :], T1.t[:, 0:2 * P].rearrange("p (c n) -> p c n", c=2), ACT.Copy)
                            fn(BT[0:NSM, 2, :], T1.t[0:NSM, 2 * P:3 * P], ACT.Copy).then_inc(bt_ready, 1)
                            act.drain().then_inc(T1.free, 1)
                        if k in (14, 18):
                            act.wait_ge(sc_done, L * (G * 2) + g * 2 + ((k - 14) // 4 + 1))
                            act.wait_ge(sc_saved, L * (G * 2) + g * 2 + ((k - 14) // 4 + 1))
                            if k == 14:
                                act.wait_ge(conv_saved, it(L, g, 6, 4) + 2)
                            i = (k - 14) // 4
                            fn(fsmp(USC, 2)[:, :, 0:2], smp(SCI[:, i * 16:(i + 1) * 16], 2), ACT.Copy)
                            fn(SCB, main[:, 0:T], ACT.Copy).then_inc(c_ready, 1)
                            act.drain().then_inc(bank_free[b], 1)
                        if k in (16, 20):
                            i = (k - 16) // 4
                            fn(SBB, main[:, 0:T], ACT.Copy).then_inc(bank_free[b], 1)
                            act.wait_ge(u_ready, it(L, g, 2, i))
                            fn(CSUM, USC[:, 0:SW], ACT.Copy, scale=GP[:, G_SW + 3 * i:G_SW + 3 * i + 1]).then_inc(stap_done, 1)
                        if k in (17, 21):
                            tanh_half(main[:, 0:T], T)
                        if k == 16:
                            act.wait_ge(T1.full, T1.in_grp(L, g, 5))
                            fn(S0, T1.t[:, :], ACT.Copy).then_inc(s0_ready, 1)
                            act.drain().then_inc(T1.free, 1)
                        if 14 <= k < 18:
                            decay_exp(2 * (k - 14))
                            decay_exp(2 * (k - 14) + 1)
                        if k == 14:
                            act.wait_ge(conv_saved, it(L, g, 6, 5) + 2)
                            act.dma_start(conv_out[L, g], CSO[:, :]).then_inc(csout_stored, 16)
                        if k == 20:
                            act.wait_ge(s1_ready, it(L, g))
                            act.dma_start(ssm_p[L, g], S1).then_inc(s1_stored, 16)
                    rsqrt(T1, T1.in_grp(L, g, 8), 1.0 / GW, C_EPS + 1)
                    act.wait_ge(smp_state, it(L, g) + 1)
                    act.dma_start(ssm_s[L, g], S0T).then_inc(state_stored, 16)
                    act.wait_ge(sc_saved, it(L, g, 2, 1) + 1)
                    act.dma_start(scv_out[L, g], SCO[:, :]).then_inc(scout_stored, 16)

                act.wait_ge(units_used, unit(L, OUT_U0 + 2))
                act.wait_ge(sc_done, L * (G * 2) + (G * 2 + 1))
                for j in range(4):
                    c0 = (KT + 4 * j) * T
                    fn(HHI[:, 4 * j * T:4 * (j + 1) * T], YX[:, c0:c0 + 4 * T], ACT.Copy).then_inc(y_hi, 1)
                act.wait_ge(ssd_done, L * G + (G + 1))
                act.wait_ge(s1_stored, L * (G * 16) + (G * 16 + 16))
                for j in range(4):
                    fn(YHI[:, 4 * j * T:4 * (j + 1) * T], YX[:, 4 * j * T:4 * (j + 1) * T], ACT.Copy).then_inc(y_hi, 1)
                act.wait_ge(state_stored, L * (G * 16) + (G * 16 + 16))
                with act.Fori(0, KT // 2) as mp:
                    for q in range(4):
                        split_hi(L * LAYER_U + mp * 4 + (OUT_U0 + q + 2), q % 2,
                                 L * (LAYER_U // 2 * 16) + mp * 32 + ((OUT_U0 + q + 2) // 2 * 16 + 16))
                        if q % 2:
                            m = q // 2
                            act.wait_ge(filled, L * LAYER_F + mp * 2 + (OUT_U0 + m + 1))
                            act.wait_ge(mix_added, L * KT + mp * 2 + (m + 1))
                            fn(MIX[:, bass.ds((mp * 2 + m) * T, T)], MAIN[m][:, 0:T], ACT.Copy)
                            fn(MSQ[m][:, :], MAIN[m][:, 0:T], ACT.Square).then_inc(mix_sq, 1)
                            act.drain().then_inc(bank_free[m], 1)
                act.wait_ge(p_in, L * 16 + 16)
                fn(YHI[:, 0:2 * T], PRAW, ACT.Copy).then_inc(p_hi, 1)
                rsqrt(T0, T0.in_post(L, 0), 1.0 / DM, C_EPS)
                act.wait_ge(p_lo, L + 1)
                for m in range(KT + 2):
                    if m >= 2:
                        i = m - 2
                        act.wait_ge(x_mid, L * KT + (i + 1))
                        fn(HHI[:, i * T:(i + 1) * T], YX[:, i * T:(i + 1) * T], ACT.Copy).then_inc(x_hi, 1)
                    if m >= KT:
                        continue
                    if m == 8:
                        split_hi(unit(L, GATE_U0), 0, landed(L, GATE_U0))
                    act.wait_ge(filled, L * LAYER_F + (OUT_U0 + KT + m + 1))
                    c0 = (KT + m) * T
                    fn(YX[:, c0:c0 + T], MAIN[m % 2][:, 0:T], ACT.Copy, scale=0.5).then_inc(bank_free[m % 2], 1)
                split_hi(unit(L, GATE_U0 + 1), 1, landed(L, GATE_U0 + 1))
                with act.Fori(0, KT // 2 - 1) as mp:
                    for m in range(2):
                        act.wait_ge(filled, L * LAYER_F + mp * 2 + (OUT_U0 + 2 * KT + m + 1))
                        split_hi(L * LAYER_U + mp * 2 + (GATE_U0 + m + 2), m,
                                 L * (LAYER_U // 2 * 16) + mp * 16 + ((GATE_U0 + m + 2) // 2 * 16 + 16))
                        act.wait_ge(th_used, L * 72 + mp * 2 + (56 + m + 1))
                        fn(TH[m][:, 0:T], MAIN[m][:, 0:T], ACT.Tanh, scale=0.5).then_inc(th_ready, 1)
                for m in range(2):
                    act.wait_ge(filled, L * LAYER_F + (OUT_U0 + 3 * KT - 2 + m + 1))
                    act.wait_ge(th_used, L * 72 + (70 + m + 1))
                    fn(TH[m][:, 0:T], MAIN[m][:, 0:T], ACT.Tanh, scale=0.5).then_inc(th_ready, 1)
            act.wait_ge(old_copied, 32)
            act.wait_ge(k_stored, DEPTH * 32)
            act.wait_ge(v_stored, DEPTH * 128)
            act.wait_ge(csout_stored, DEPTH * G * 16 + 16)
            act.wait_ge(scout_stored, DEPTH * G * 16 + 16)
            act.wait_ge(s1_stored, DEPTH * G * 16 + 16)
            act.wait_ge(state_stored, DEPTH * G * 16 + 16)

        @block.vector
        def _(dve):
            tt, ts, stt = nc.vector.tensor_tensor, nc.vector.tensor_scalar, nc.vector.scalar_tensor_tensor

            def lo(dst, raw, hi):
                return tt(dst, raw, hi.bitcast(F32), ALU.subtract)

            def split_lo(u, s, k=None):
                n = (KT - pool_blocks(k)) * BLK
                dve.wait_ge(hi_done, u + 1)
                lo(WLO[s][:, 0:n], RAW[s][:, 0:n], WHI[s][:, 0:n]).then_inc(lo_done, 1)

            def rsqrt(bank, n, inv, eps):
                dve.wait_ge(norm_ln, n)
                ts(RV[:, :], bank.t[:, 0:T], inv, eps, ALU.mult, ALU.add).then_inc(bank.free, 1)
                tt(RA[:, :], RS[:, :], RS[:, :], ALU.mult)
                dve.drain()
                tt(RA[:, :], RA[:, :], RV[:, :], ALU.mult)
                dve.drain()
                ts(RA[:, :], RA[:, :], -0.5, 1.5, ALU.mult, ALU.add)
                dve.drain()
                tt(RS[:, :], RS[:, :], RA[:, :], ALU.mult)
                dve.drain()

            def rotate(dst, swapped, main, b):
                tt(dst, main[:, 0:T], COS, ALU.mult).then_inc(bank_free[b], 1)
                tt(swapped, swapped, SIN, ALU.mult)
                dve.drain()
                return tt(dst, dst, swapped, ALU.add)

            dve.wait_ge(x_first, 16)
            dve.sem_inc(x_final, 1)
            dve.sem_inc(th_used, 2)
            dve.sem_inc(ssd_done, 1)
            dve.sem_inc(sc_done, 1)
            dve.sem_inc(xc_ready, 2)
            dve.sem_inc(y_used, 1)
            dve.sem_inc(smp_state, 1)
            for f in FB:
                nc.vector.memset(f[:, 0:3], 0.0)
            dve.wait_ge(const_in, 16)
            with dve.Fori(0, DEPTH) as L:
                for j in range(1, 4):
                    dve.wait_ge(xsq_done, L * 4 + (j + 1))
                    last = tt(XSQ[:, 0:4 * T], XSQ[:, 0:4 * T], XSQ[:, 4 * j * T:4 * (j + 1) * T], ALU.add)
                    if j < 3:
                        dve.drain()
                last.then_inc(xsq_sum, 1)
                split_lo(unit(L, 0), 0)
                rsqrt(T0, L * 6 + 1, 1.0 / DM, EPS)
                dve.wait_ge(layer_in, L * 64 + 64)
                for i in range(KT):
                    f = HF[i % 4]
                    if i >= 4:
                        dve.wait_ge(h_lo, L * KT + (i - 3))
                    stt(f, YX[:, i * T:(i + 1) * T], NRM[:, i:i + 1], RS[:, :], ALU.mult, ALU.mult).then_inc(h_scaled, 1)
                dve.wait_ge(dt_hi, L + 1)
                lo(YLO[:, 0:UNIT], DTRAW, YHI[:, 0:UNIT]).then_inc(dt_lo, 1)
                split_lo(unit(L, 1), 1)

                def step_sizes():
                    dve.wait_ge(T1.full, T1.in_pre(L, 0))
                    ts(DTR[0:32, :], T1.t[0:32, 0:T], DTP[0:32, 0:1], None, ALU.add).then_inc(T1.free, 1)
                    dve.drain()
                    stt(DTU[0:32, :], DTR[0:32, :], -1.0, DTR[0:32, :], ALU.mult, ALU.max).then_inc(dt_abs, 1)
                    dve.wait_ge(dt_exp, L + 1)
                    ts(DTU[0:32, :], DTE[0:32, :], 1.0, None, ALU.add).then_inc(dt_u, 1)
                    dve.drain()
                    ts(W0[0:32, :], DTU[0:32, :], -1.0, None, ALU.add)
                    dve.drain()
                    tt(W0[0:32, :], DTE[0:32, :], W0[0:32, :], ALU.subtract)
                    dve.drain()
                    dve.wait_ge(dt_ln, L + 1)
                    tt(DTC[0:32, :], DTC[0:32, :], W0[0:32, :], ALU.add)
                    dve.drain()
                    stt(DT0[0:32, :], DTR[0:32, :], 0.0, DTC[0:32, :], ALU.max, ALU.add)
                    dve.drain()
                    ts(DTR[0:32, :], DT0[0:32, :], DTP[0:32, 2:3], -1.0, ALU.mult, ALU.mult)
                    dve.drain()
                    nc.vector.tensor_tensor_scan(AC0[0:32, :], RST[0:32, :], DTR[0:32, :], 0.0, ALU.mult, ALU.add)
                    dve.drain()
                    for c in range(2):
                        ts(DTE[0:32, c * P:(c + 1) * P], AC0[0:32, c * P:(c + 1) * P], AC0[0:32, (c + 1) * P - 1:(c + 1) * P],
                           None, ALU.subtract)
                    ac = smp(AC0[0:32, NPR:T])
                    tt(smp(DTE[0:32, NPR:T]), ac, ac[:, :, NS - 1:NS].to_broadcast([32, NB, NS]), ALU.subtract).then_inc(dt_ac, 1)

                for k in range(PRE_U):
                    split_lo(unit(L, k + 2), k % 2)
                    if k < 2:
                        dve.wait_ge(k_swapped, L * 2 + (k + 1))
                        rotate(KTT[:, k, :], KSW[:, k, :], MAIN[k], k).then_inc(k_ready, 1)
                    if k == 0:
                        step_sizes()
                    if k == 1:
                        dve.wait_ge(dt_wexp, L + 1)
                        tt(W0[0:32, :], W0[0:32, :], DT0[0:32, :], ALU.mult).then_inc(dt_ready, 1)

                with dve.Fori(0, G) as g:
                    th_n = [0]

                    def gate(dst, main, b):
                        n = th_n[0]
                        th_n[0] += 1
                        dve.wait_ge(th_ready, L * 72 + g * 14 + (n + 1))
                        stt(dst, TH[n % 2][:, 0:T], 1.0, main[:, 0:T], ALU.add, ALU.mult).then_inc(th_used, 1)
                        return dve.drain().then_inc(bank_free[b], 1)

                    def mask_max(j):
                        bk = (A0, A1)[j % 2]
                        dve.wait_ge(bk.full, bk.in_grp(L, g, j // 2))
                        tt(PR[:, j, :], bk.t[:, 0:3 * P], MSK[:, 0:3 * P], ALU.add).then_inc(bk.free, 1)
                        dve.drain()
                        nc.vector.reduce_max(MX[:, 2 * j:2 * j + 1], PR[:, j, 0:P], AX.X)
                        nc.vector.reduce_max(MX[:, 2 * j + 1:2 * j + 2], PR[:, j, P:3 * P], AX.X)

                    def row_stats(c0, c1, sink):
                        n = c1 - c0
                        dve.drain()
                        stt(NM[:, c0:c1].rearrange("p (j c) -> p j c", c=n if n == 1 else 2),
                            MX[:, c0:c1].rearrange("p (j c) -> p j c", c=n if n == 1 else 2), HD ** -0.5, sink, ALU.mult, ALU.max)
                        dve.drain()
                        ts(NM[:, c0:c1], NM[:, c0:c1], -1.0, None, ALU.mult)
                        dve.drain()
                        return tt(MX[:, c0:c1].rearrange("p (j c) -> p j c", c=n if n == 1 else 2),
                                  NM[:, c0:c1].rearrange("p (j c) -> p j c", c=n if n == 1 else 2), sink, ALU.add)

                    def half_over_den(c0, c1):
                        dve.drain()
                        tt(DEN[:, c0:c1], DEN[:, c0:c1], MX[:, c0:c1], ALU.add)
                        dve.drain()
                        nc.vector.reciprocal(DEN[:, c0:c1], DEN[:, c0:c1])
                        dve.drain()

                    def gated_y(i):
                        x = XC[:, 2 + i, :]
                        dve.wait_ge(YB.full, YB.in_grp(L, g, 1 + i))
                        stt(YT, x, GP[:, G_D + i:G_D + i + 1], YB.t[:, 0:T], ALU.mult, ALU.add).then_inc(YB.free, 1)
                        dve.wait_ge(YO.full, YO.in_grp(L, g, 1 + i))
                        tt(YS[:, 0:P + NSM], YO.t[:, 0:P + NSM], EA[i % 3], ALU.mult).then_inc(YO.free, 1)
                        dve.drain().then_inc(y_used, 1)
                        tt(YT[:, P:T], YT[:, P:T], YS[:, 0:P + NSM], ALU.add)
                        dve.drain()
                        tt(Z2[:, i, :], YT, Z2[:, i, :], ALU.mult).then_inc(y_gated, 1)
                        dve.drain()

                    for k in range(GRP_U):
                        b = k % 2
                        main = MAIN[b]
                        split_lo(gunit(L, g, k + 2), b, k)
                        if k < 2:
                            dve.wait_ge(q_swapped, it(L, g, 2, k))
                            rotate(Q[:, k, :], QS[:, k, :], main, b).then_inc(q_ready, 1)
                        if k in (2, 3):
                            gate(G2[:, k - 2, :], main, b)
                        if 4 <= k < 8:
                            gate(Z2[:, k - 4, :], main, b)
                        if k in (3, 4):
                            if k == 3:
                                dve.wait_ge(att_in, L * (G * 112) + g * 112 + 112)
                                dve.wait_ge(gp_in, L * (G * 16) + g * 16 + 16)
                            mask_max(2 * (k - 3))
                            mask_max(2 * (k - 3) + 1)
                        if k == 4:
                            row_stats(0, 8, GP[:, G_SK:G_SK + 4].unsqueeze(2).to_broadcast([P, 4, 2])).then_inc(att_max, 1)
                        if k == 5:
                            for s, bk, n in ((0, A0, 2), (1, A1, 2), (2, A0, 3)):
                                w = 512 if s < 2 else NSM
                                dve.wait_ge(bk.full, bk.in_grp(L, g, n))
                                tt(PS[:, s * 512:s * 512 + w], bk.t[:, 0:w], MSK[:, 3 * P + s * 512:3 * P + s * 512 + w],
                                   ALU.add).then_inc(bk.free, 1)
                            dve.drain()
                            nc.vector.reduce_max(MX[:, 8:9], PS, AX.X)
                            row_stats(8, 9, GP[:, G_SKS:G_SKS + 1].unsqueeze(2)).then_inc(smp_max, 1)
                            wait_alone(dve, "dve", att_exp, it(L, g))
                            half_over_den(0, 8)
                            for j in range(4):
                                for c, (c0, c1) in enumerate(((0, P), (P, 3 * P))):
                                    last = ts(PR[:, j, c0:c1], PR[:, j, c0:c1], DEN[:, 2 * j + c:2 * j + c + 1], 0.5,
                                              ALU.mult, ALU.mult)
                            last.then_inc(att_prob, 1)
                        if k == 6:
                            wait_alone(dve, "dve", smp_exp, it(L, g))
                            half_over_den(8, 9)
                            ts(PS, PS, DEN[:, 8:9], 0.5, ALU.mult, ALU.mult).then_inc(smp_prob, 1)
                        if 8 <= k < 14:
                            t = k - 8
                            f, s = FB[t % 2], AB[t % 2]
                            if t == 0:
                                dve.wait_ge(tok_ready, L + 1)
                                src = TOK[:, :].rearrange("p (v h) -> p v h", h=32)[:, :, bass.ds(g * HG, HG)]
                                dst = TG[:, :].rearrange("p (v h) -> p v h", h=HG)
                                nc.vector.tensor_copy(dst[:, 0:6, :], src[:, 0:6, :])
                                nc.vector.tensor_copy(dst[0:NSM, 6:9, :], src[0:NSM, 6:9, :]).then_inc(tg_ready, 1)
                            dve.wait_ge(tap_done, it(L, g, 6, t))
                            for j in range(1, 4):
                                last = stt(s[:, :], f[:, j:j + CW], GP[:, G_CW + 4 * t + j:G_CW + 4 * t + j + 1], s[:, :],
                                           ALU.mult, ALU.add)
                                if j < 3:
                                    dve.drain()
                            last.then_inc(conv_sum, 1)
                            n = th_n[0]
                            th_n[0] += 1
                            dve.wait_ge(th_ready, L * 72 + g * 14 + (n + 1))
                            th = TH[n % 2]
                            stt(XC[:, t, 0:NPR], th[:, 0:NPR], 1.0, s[:, 0:NPR], ALU.add, ALU.mult)
                            ths = th[:, NPR:NPR + 56].rearrange("p (b t) -> p b t", t=7)[:, :, 3:7]
                            ss = s[:, NPR:NPR + 56].rearrange("p (b t) -> p b t", t=7)[:, :, 3:7]
                            stt(smp(XC[:, t, NPR:T]), ths, 1.0, ss, ALU.add, ALU.mult).then_inc(th_used, 1)
                            dve.drain()
                            ts(XC[:, t, :], XC[:, t, :], 0.5, None, ALU.mult).then_inc(xc_ready, 1)
                        if k in (9, 10):
                            a = k - 9
                            bk = (YB, YO)[a]
                            dve.wait_ge(bk.full, bk.in_grp(L, g, 0))
                            if a == 0:
                                dve.wait_ge(x_stored, L * 16 + 16)
                                dve.wait_ge(x_slab0, 16)
                            tt(YX[:, bass.ds((g * 2 + KT + a) * T, NPR)], bk.t[:, 0:NPR], G2[:, a, 0:NPR], ALU.mult).then_inc(bk.free, 1)
                        if k == 10:
                            dve.wait_ge(os_ready, it(L, g))
                            for a in range(2):
                                last = tt(YX[:, bass.ds((g * 2 + KT + a) * T + NPR, NSM)], OS[:, a, :], G2[:, a, NPR:T], ALU.mult)
                            last.then_inc(att_done, 1)
                            dve.wait_ge(A0.full, A0.in_grp(L, g, 4))
                            tt(CBM[:, 0:NPR], A0.t[:, 0:NPR], TRI[:, 0:NPR], ALU.mult)
                            tt(CBM[0:NSM, NPR:T], A0.t[0:NSM, NPR:T], TRI[0:NSM, NPR:T], ALU.mult).then_inc(A0.free, 1)
                        if k in (15, 19):
                            i = (k - 15) // 4
                            dve.wait_ge(c_ready, it(L, g, 2, i))
                            tt(USC[:, 2:2 + NPR], main[:, 0:NPR], SCB[:, 0:NPR], ALU.mult)
                            tt(fsmp(USC, 2)[:, :, 2:6], smp(main[:, NPR:T]), smp(SCB[:, NPR:T]), ALU.mult).then_inc(u_ready, 1)
                            dve.drain().then_inc(bank_free[b], 1)
                        if k in (17, 21):
                            i = (k - 17) // 4
                            gate(SG2, main, b)
                            dve.wait_ge(stap_done, it(L, g, 2, i))
                            for j in (1, 2):
                                stt(CSUM, USC[:, j:j + SW], GP[:, G_SW + 3 * i + j:G_SW + 3 * i + j + 1], CSUM, ALU.mult, ALU.add)
                                dve.drain()
                            cs = CSUM[:, NPR:NPR + 48].rearrange("p (b t) -> p b t", t=6)[:, :, 2:6]
                            stt(SBB[:, 0:NPR], CSUM[:, 0:NPR], 0.5, SBB[:, 0:NPR], ALU.mult, ALU.mult)
                            stt(smp(SBB[:, NPR:T]), cs, 0.5, smp(SBB[:, NPR:T]), ALU.mult, ALU.mult)
                            dve.drain()
                            tt(YX[:, bass.ds((g * 2 + 24 + i) * T, T)], SBB, SG2, ALU.mult).then_inc(sc_done, 1)
                        if k in (14, 15):
                            for c in (0, 1) if k == 14 else (2,):
                                bk, n = ((T0, 4), (T1, 4), (T0, 5))[c]
                                w = P if c < 2 else NSM
                                dve.wait_ge(bk.full, bk.in_grp(L, g, n))
                                src = bk.t[0:w, :].rearrange("p (h d) -> p h d", d=HD)
                                for dst, v in ((XDT, 0), (XW, 2)):
                                    last = tt(dst[0:w, c, :].rearrange("p (h d) -> p h d", d=HD), src,
                                              TGV[0:w, c, v, :].unsqueeze(2).to_broadcast([w, HG, HD]), ALU.mult)
                                last.then_inc(bk.free, 1)
                                dve.drain().then_inc(xt_ready, 1)
                        if 15 <= k < 19:
                            for h in (2 * (k - 15), 2 * (k - 15) + 1):
                                m = MH[h % 6]
                                dve.wait_ge(decay_ready, it(L, g, HG, h))
                                tt(m[:, 0:NPR], m[:, 0:NPR], CBM[:, 0:NPR], ALU.mult)
                                tt(m[0:NSM, NPR:T], m[0:NSM, NPR:T], CBM[0:NSM, NPR:T], ALU.mult).then_inc(mh_ready, 1)
                        if 17 <= k < 21:
                            gated_y(k - 17)
                        if k == 18:
                            dve.wait_ge(T0.full, T0.in_grp(L, g, 6))
                            dve.wait_ge(s1_stored, L * (G * 16) + g * 16 + 16)
                            tt(S1.rearrange("p (h d) -> p h d", d=HD), S0.rearrange("p (h d) -> p h d", d=HD),
                               DEC[:, :, 0:1].to_broadcast([P, HG, HD]), ALU.mult)
                            dve.drain()
                            tt(S1, T0.t[:, :], S1, ALU.add).then_inc(T0.free, 1)
                            dve.drain().then_inc(s1_ready, 1)
                        if k in (20, 21):
                            for b_, (bk, n) in enumerate(((T1, 6), (T0, 7), (A0, 9), (A1, 8))):
                                bb = 4 * (k - 20) + b_
                                st = S0T[:, bb * GW:(bb + 1) * GW]
                                dve.wait_ge(bk.full, bk.in_grp(L, g, n + (k - 20)))
                                stv = st.rearrange("p (h d) -> p h d", d=HD)
                                tt(stv, stv, DEC[:, :, 1 + bb:2 + bb].to_broadcast([P, HG, HD]), ALU.mult)
                                dve.drain()
                                last = tt(st, bk.t[:, :], st, ALU.add).then_inc(bk.free, 1)
                    dve.drain().then_inc(smp_state, 1)
                    rsqrt(T1, L * 6 + g + 2, 1.0 / GW, 4 * EPS)
                    for i in range(4):
                        stt(YX[:, bass.ds((g * 4 + i) * T, T)], Z2[:, i, :], GP[:, G_NW + i:G_NW + i + 1], RS[:, :], ALU.mult, ALU.mult)
                    dve.drain().then_inc(ssd_done, 1)

                for j in range(8):
                    hi, lo_ = ((HHI, HLO) if j < 4 else (YHI, YLO))
                    c0, y0 = 4 * (j % 4) * T, ((KT if j < 4 else 0) + 4 * (j % 4)) * T
                    dve.wait_ge(y_hi, L * 8 + (j + 1))
                    lo(lo_[:, c0:c0 + 4 * T], YX[:, y0:y0 + 4 * T], hi[:, c0:c0 + 4 * T]).then_inc(y_lo, 1)
                with dve.Fori(0, KT // 2) as mp:
                    for q in range(4):
                        split_lo(L * LAYER_U + mp * 4 + (OUT_U0 + q + 2), q % 2)
                dve.wait_ge(p_hi, L + 1)
                lo(YLO[:, 0:2 * T], PRAW, YHI[:, 0:2 * T]).then_inc(p_lo, 1)
                rsqrt(T0, L * 6 + 6, 1.0 / DM, EPS)
                dve.wait_ge(xres_in, L * 16 + 16)
                for i in range(KT):
                    if i == 8:
                        split_lo(unit(L, GATE_U0), 0)
                    stt(MIX[:, i * T:(i + 1) * T], MIX[:, i * T:(i + 1) * T], NRM[:, KT + i:KT + i + 1], RS[:, :], ALU.mult, ALU.mult)
                    dve.drain()
                    x = YX[:, i * T:(i + 1) * T]
                    tt(x, x, MIX[:, i * T:(i + 1) * T], ALU.add).then_inc(x_mid, 1)
                split_lo(unit(L, GATE_U0 + 1), 1)

                def add_gated(mp, m):
                    dve.wait_ge(th_ready, L * 72 + mp * 2 + (56 + m + 1))
                    stt(RA[:, :], TH[m][:, 0:T], 1.0, YX[:, bass.ds((mp * 2 + KT + m) * T, T)], ALU.add, ALU.mult).then_inc(th_used, 1)
                    dve.drain().then_inc(bank_free[m], 1)
                    x = YX[:, bass.ds((mp * 2 + m) * T, T)]
                    tt(x, x, RA[:, :], ALU.add)
                    dve.drain()

                wait_alone(dve, "dve", x_lo, (L + 1) * KT)
                with dve.Fori(0, KT // 2 - 1) as mp:
                    for m in range(2):
                        split_lo(L * LAYER_U + mp * 2 + (GATE_U0 + m + 2), m)
                        add_gated(mp, m)
                for m in range(2):
                    dve.wait_ge(th_ready, L * 72 + (70 + m + 1))
                    e0, x_0 = (2 * KT - 2 + m) * T, (KT - 2 + m) * T
                    stt(RA[:, :], TH[m][:, 0:T], 1.0, YX[:, e0:e0 + T], ALU.add, ALU.mult).then_inc(th_used, 1)
                    dve.drain().then_inc(bank_free[m], 1)
                    tt(YX[:, x_0:x_0 + T], YX[:, x_0:x_0 + T], RA[:, :], ALU.add)
                    last = dve.drain()
                last.then_inc(x_final, 1)

        @block.gpsimd
        def _(pool):
            tt = nc.gpsimd.tensor_tensor

            def lo(dst, raw, hi):
                return tt(dst, raw, hi.bitcast(F32), ALU.subtract)

            def split_lo(u, s, k=None):
                n = (KT - pool_blocks(k)) * BLK
                pool.wait_ge(hi_done, u + 1)
                lo(WLO[s][:, n:UNIT], RAW[s][:, n:UNIT], WHI[s][:, n:UNIT]).then_inc(lop_done, 1)

            pool.sem_inc(conv_saved, 2)
            pool.sem_inc(sc_saved, 1)
            pool.sem_inc(x_stored, 16)
            pool.sem_inc(mix_added, 2)
            pool.sem_inc(y_sq, 1)
            pool.wait_ge(const_in, 16)
            with pool.Fori(0, DEPTH) as L:
                split_lo(unit(L, 0), 0)
                for i in range(KT):
                    pool.wait_ge(h_hi, L * KT + (i + 1))
                    lo(HLO[:, i * T:(i + 1) * T], HF[i % 4], HHI[:, i * T:(i + 1) * T]).then_inc(h_lo, 1)
                split_lo(unit(L, 1), 1)
                for k in range(PRE_U):
                    split_lo(unit(L, k + 2), k % 2)
                with pool.Fori(0, G) as g:
                    for k in range(GRP_U):
                        split_lo(gunit(L, g, k + 2), k % 2, k)
                        if 8 <= k < 14:
                            t = k - 8
                            f = FB[t % 2]
                            if t == 0:
                                pool.wait_ge(csout_stored, L * (G * 16) + g * 16 + 16)
                            wait_alone(pool, "pool", tap_done, it(L, g, 6, t))
                            nc.gpsimd.tensor_copy(CSO[:, t * 27:t * 27 + 3], f[:, NPR:NPR + 3])
                            nc.gpsimd.tensor_copy(smp(CSO[:, t * 27 + 3:(t + 1) * 27], 3), fsmp(f, 3)[:, :, 4:7]).then_inc(conv_saved, 1)
                        if k == 12:
                            pool.wait_ge(bt_ready, it(L, g))
                            tt(BM[0:NSM, :, :], BT[0:NSM, 2:3, :].to_broadcast([NSM, NB, P]),
                               CST[0:NSM, C_SEQ:C_SEQ + NB].unsqueeze(2).to_broadcast([NSM, NB, P]), ALU.mult).then_inc(bm_ready, 1)
                        if k in (16, 20):
                            i = (k - 16) // 4
                            if i == 0:
                                pool.wait_ge(scout_stored, L * (G * 16) + g * 16 + 16)
                            wait_alone(pool, "pool", u_ready, it(L, g, 2, i))
                            nc.gpsimd.tensor_copy(SCO[:, i * 18:i * 18 + 2], USC[:, NPR:NPR + 2])
                            nc.gpsimd.tensor_copy(smp(SCO[:, i * 18 + 2:(i + 1) * 18], 2), fsmp(USC, 2)[:, :, 4:6]).then_inc(sc_saved, 1)
                        if 18 <= k < 22:
                            i = k - 18
                            pool.wait_ge(y_gated, it(L, g, 4, i))
                            if i == 0:
                                tt(SQ[:, :], Z2[:, 0, :], Z2[:, 0, :], ALU.mult)
                            else:
                                tt(CBM, Z2[:, i, :], Z2[:, i, :], ALU.mult)
                                pool.drain()
                                tt(SQ[:, :], SQ[:, :], CBM, ALU.add)
                            if i < 3:
                                pool.drain()
                            else:
                                pool.drain().then_inc(y_sq, 1)
                wait_alone(pool, "pool", ssd_done, L * G + (G + 1))
                nc.gpsimd.memset(SQ[:, :], 0.0)
                pool.drain()
                with pool.Fori(0, KT // 2) as mp:
                    for q in range(4):
                        split_lo(L * LAYER_U + mp * 4 + (OUT_U0 + q + 2), q % 2)
                        if q % 2:
                            m = q // 2
                            pool.wait_ge(mix_sq, L * KT + mp * 2 + (m + 1))
                            tt(SQ[:, :], SQ[:, :], MSQ[m][:, :], ALU.add).then_inc(mix_added, 1)
                            pool.drain()
                split_lo(unit(L, GATE_U0), 0)
                for i in range(KT):
                    pool.wait_ge(x_hi, L * KT + (i + 1))
                    lo(HLO[:, i * T:(i + 1) * T], YX[:, i * T:(i + 1) * T], HHI[:, i * T:(i + 1) * T]).then_inc(x_lo, 1)
                split_lo(unit(L, GATE_U0 + 1), 1)
                with pool.Fori(0, KT // 2 - 1) as mp:
                    for m in range(2):
                        split_lo(L * LAYER_U + mp * 2 + (GATE_U0 + m + 2), m)


_INS = ["wts", "wdt", "x0", "p_t", "npre", "npost", "gpar", "dtpar", "s0_t", "kc_t", "vc_t", "cs_in", "sc_in",
        "consts", "masks", "resets"]
_OUTS = [("xs", (DEPTH + 1, P, KT * T)), ("kout", (DEPTH, G, HD, T)), ("vout", (DEPTH, G, T, HD)),
         ("kold", (DEPTH * G * HD, NB, P - NS)), ("vold", (DEPTH * G, P - NS, NB * HD)),
         ("conv_out", (DEPTH, G, P, 6 * 27)), ("scv_out", (DEPTH, G, P, 2 * 18)),
         ("ssm_p", (DEPTH, G, P, GW)), ("ssm_s", (DEPTH, G, P, NB * GW))]


def shape_constants():
    import numpy as np

    f = np.float32
    half = HD // 2
    inv = np.exp(f(-np.log(10000.0)) * np.arange(half, dtype=f) * f(2.0 / HD))
    pos = np.concatenate([np.arange(NPR), np.tile(1024 + np.arange(NS), NB)]).astype(f)
    ang = pos[None, :] * inv[np.arange(P) % half][:, None]
    sign = np.where(np.arange(P) % HD < half, -1.0, 1.0).astype(f)[:, None]
    c = np.zeros((P, NCONST), f)
    c[:, C_COS:C_COS + T] = np.cos(ang)
    c[:, C_SIN:C_SIN + T] = np.sin(ang) * sign
    c[:, C_ID:C_ID + P] = np.eye(P)
    s, l = np.arange(P)[:, None], np.arange(P)[None, :]
    for n in range(2):
        c[:, C_TRI + n * P:C_TRI + (n + 1) * P] = s <= l
    c[:NSM, C_TRI + NPR:C_TRI + T] = ((s <= l) & (s // NS == l // NS))[:NSM, :NSM]
    c[:, C_ONE:C_ONE + P] = 1.0
    c[:NSM, C_SEQ:C_SEQ + NB] = np.arange(NSM)[:, None] // NS == np.arange(NB)[None, :]
    c[:, C_EPS], c[:, C_EPS + 1] = EPS, 4 * EPS
    m = np.zeros((P, NMASK), f)
    t = np.arange(P)[:, None]
    key = np.arange(2 * P)[None, :]
    m[:, 0:P] = np.where(key[:, :P] <= t, 0, -1e30)
    m[:, P:3 * P] = np.where((key <= P + t) & (key > t), 0, -1e30)
    b, tok = (t // NS) % NB, t % NS
    col = np.arange(NB * P)[None, :]
    m[:, 3 * P:3 * P + NB * P] = np.where((col // P == b) & (col % P > tok), 0, -1e30)
    new = np.arange(NSM)[None, :]
    m[:, 3 * P + NB * P:] = np.where((new // NS == b) & (new % NS <= tok), 0, -1e30)
    r = np.ones((32, T), f)
    r[:, [0, P]] = 0
    r[:, NPR::NS] = 0
    return c, m, r


def kernel(**inputs):
    import concourse.bacc as _bacc
    import numpy as np
    from concourse.bass_utils import run_bass_kernel_spmd as _run

    i = {k: np.asarray(v) for k, v in inputs.items()}
    D = DEPTH

    z0, xbc0 = 0, 2048
    x_0, b_0, c_0 = xbc0, xbc0 + 2048, xbc0 + 2048 + 512
    dt0 = xbc0 + 3072
    q0 = dt0 + 32
    k0, v0 = q0 + 1024, q0 + 1024 + 256
    ga0 = v0 + 256
    sb0 = ga0 + 1024
    scc0, sh0, sg0 = sb0 + 1024, sb0 + 2048, sb0 + 3072
    starts = [k0, k0 + P, v0, v0 + P]
    for g in range(G):
        starts += [q0 + g * 256, q0 + g * 256 + P, ga0 + g * 256, ga0 + g * 256 + P]
        starts += [z0 + g * 512 + n * P for n in range(4)]
        starts += [b_0 + g * P, c_0 + g * P] + [x_0 + g * 512 + n * P for n in range(4)]
        for n in range(2):
            starts += [w + (2 * g + n) * P for w in (scc0, sh0, sb0, sg0)]
    w_in, w_out, ple, gate = i["w_in"], i["w_out"], i["ple_proj"], i["ple_gate"]
    wts = np.empty((D, LAYER_U, P, KT, P), np.float32)
    for u, c in enumerate(starts):
        wts[:, u] = w_in[:, :, c:c + P].reshape(D, KT, P, P).transpose(0, 2, 1, 3)
    for m in range(KT):
        w = w_out[:, :, m * P:(m + 1) * P].reshape(D, 2, KT, P, P).transpose(0, 1, 3, 2, 4)
        wts[:, OUT_U0 + 2 * m] = w[:, 1]
        wts[:, OUT_U0 + 2 * m + 1] = w[:, 0]
        wts[:, GATE_U0 + m] = gate[:, :, m * P:(m + 1) * P].reshape(D, KT, P, P).transpose(0, 2, 1, 3)
    pl = ple.reshape(D, 2, P, KT, P).transpose(0, 2, 3, 1, 4).reshape(D, P, 2, KT, P)
    wts[:, PLE_U0:PLE_U0 + 2] = pl.transpose(0, 2, 1, 3, 4)
    wdt = np.zeros((D, P, KT, P), np.float32)
    wdt[:, :, :, 0:32] = w_in[:, :, dt0:dt0 + 32].reshape(D, KT, P, 32).transpose(0, 2, 1, 3)

    def tokens(prompt, sample):
        a = np.concatenate([prompt[..., 0, :, :], sample.reshape(*sample.shape[:-3], NSM, sample.shape[-1])], axis=-2)
        n = a.shape[-1] // P
        a = a.reshape(*a.shape[:-1], n, P)
        a = np.moveaxis(a, (-1, -2, -3), (-3, -2, -1))
        return a.reshape(*a.shape[:-2], n * T)

    def conv_groups(w):
        lead = w.shape[:-1]
        x, b, c = w[..., :2048], w[..., 2048:2560], w[..., 2560:]
        return np.concatenate([b.reshape(*lead, G, 1, P), c.reshape(*lead, G, 1, P), x.reshape(*lead, G, 4, P)], axis=-2)

    gpar = np.zeros((D, G, P, NGP), np.float32)
    gpar[..., G_CW:G_CW + 24] = conv_groups(i["ssd_conv_w"]).transpose(0, 2, 4, 3, 1).reshape(D, G, P, 24)
    gpar[..., G_CB:G_CB + 6] = conv_groups(i["ssd_conv_b"]).transpose(0, 1, 3, 2)
    gpar[..., G_D:G_D + 4] = np.repeat(i["ssd_d"].reshape(D, G, 4, 2), HD, axis=3).transpose(0, 1, 3, 2)
    gpar[..., G_NW:G_NW + 4] = i["ssd_norm"].reshape(D, G, 4, P).transpose(0, 1, 3, 2)
    gpar[..., G_SW:G_SW + 6] = i["sc_conv_w"].reshape(D, 3, G, 2, P).transpose(0, 2, 4, 3, 1).reshape(D, G, P, 6)
    sinks = i["attn_sinks"].reshape(D, G, 4)
    gpar[..., G_SK:G_SK + 4] = sinks[:, :, None, :]
    gpar[..., G_SKS] = np.repeat(sinks, NSM, axis=2)
    consts, masks, resets = shape_constants()
    cs = conv_groups(i["state_ssd_conv"])
    sc = i["state_sc_conv"].reshape(D, NB, 2, G, 2, P)
    arrays = {
        "wts": wts.reshape(NUNITS, P, UNIT), "wdt": wdt.reshape(D, P, UNIT),
        "x0": tokens(i["x_prompt"], i["x_sample"]), "p_t": tokens(i["p_prompt"], i["p_sample"]),
        "npre": i["norm_pre"].reshape(D, KT, P).transpose(0, 2, 1), "npost": i["norm_post"].reshape(D, KT, P).transpose(0, 2, 1),
        "gpar": gpar, "dtpar": np.stack([i["ssd_dt_bias"], i["ssd_a_log"]], axis=-1),
        "s0_t": i["state_ssm"].reshape(D, NB, G, HG, HD, NST).transpose(0, 2, 5, 1, 3, 4).reshape(D, G, P, NB * GW),
        "kc_t": i["cache_k"].transpose(0, 3, 4, 1, 2).reshape(D, G, HD, NB * P),
        "vc_t": i["cache_v"].transpose(0, 3, 2, 1, 4).reshape(D, G, P, NB * HD),
        "cs_in": cs.transpose(0, 3, 5, 4, 1, 2).reshape(D, G, P, 6 * 24),
        "sc_in": sc.transpose(0, 3, 5, 4, 1, 2).reshape(D, G, P, 2 * 16),
        "consts": consts, "masks": masks, "resets": resets,
    }
    nc = _bacc.Bacc("TRN2", target_bir_lowering=False, num_devices=1)
    args = []
    for n in _INS:
        arrays[n] = np.ascontiguousarray(arrays[n])
        args.append(nc.dram_tensor(n, arrays[n].shape, F32, kind="ExternalInput").ap())
    for n, shape in _OUTS:
        args.append(nc.dram_tensor(n, shape, F32, kind="ExternalOutput").ap())
    hybrid_step(nc, *args)
    r = _run(nc, [arrays], core_ids=[0])
    o = {n: np.asarray(r.results[0][n]) for n, _ in _OUTS}

    y = o["xs"][DEPTH].reshape(P, KT, T).transpose(2, 1, 0).reshape(T, DM)
    k, v = o["kout"], o["vout"]
    pk = k[..., P:NPR].transpose(0, 3, 1, 2)[:, None]
    pv = v[:, :, P:NPR].transpose(0, 2, 1, 3)[:, None]
    k_new = k[..., NPR:].reshape(D, G, HD, NB, NS).transpose(0, 3, 4, 1, 2)
    v_new = v[:, :, NPR:].reshape(D, G, NB, NS, HD).transpose(0, 2, 3, 1, 4)
    k_old = o["kold"].reshape(D, G, HD, NB, P - NS).transpose(0, 3, 4, 1, 2)
    v_old = o["vold"].reshape(D, G, P - NS, NB, HD).transpose(0, 3, 2, 1, 4)
    co = o["conv_out"].reshape(D, G, P, 6, 9, 3).transpose(0, 4, 5, 1, 3, 2)
    co = np.concatenate([co[..., 2:, :].reshape(D, 9, 3, 2048), co[..., 0, :].reshape(D, 9, 3, 512),
                         co[..., 1, :].reshape(D, 9, 3, 512)], axis=-1)
    so = o["scv_out"].reshape(D, G, P, 2, 9, 2).transpose(0, 4, 5, 1, 3, 2).reshape(D, 9, 2, 1024)
    sp = o["ssm_p"].reshape(D, G, NST, HG, HD).transpose(0, 1, 3, 4, 2).reshape(D, 1, 32, HD, NST)
    ss = o["ssm_s"].reshape(D, G, NST, NB, HG, HD).transpose(0, 3, 1, 4, 5, 2).reshape(D, NB, 32, HD, NST)
    out = (y[None, :NPR], y[NPR:].reshape(NB, NS, DM), co[:, :1], sp, pk, pv, so[:, :1],
           co[:, 1:], ss, np.concatenate([k_old, k_new], axis=2), np.concatenate([v_old, v_new], axis=2), so[:, 1:])
    return tuple(np.ascontiguousarray(a) for a in out)
```

```python
from contextlib import ExitStack

import concourse.bass as bass
from concourse import mybir

F32 = mybir.dt.float32
F32R = mybir.dt.float32r
ALU = mybir.AluOpType
ACT = mybir.ActivationFunctionType
AX = mybir.AxisListType

P = 128
DEPTH = 2
DM = 2048
KT = DM // P
NPR = 256
NB, NS = 8, 4
NSM = NB * NS
T = NPR + NSM
G = 4
HG = 8
HD = 64
NST = 128
GW = HG * HD
EPS = 1e-6
BLK = P
UNIT = KT * BLK

NEW_STATES = {19: ((0, "T1", 5), (1, "A0", 8)), 20: ((2, "A1", 7), (3, "T0", 6), (4, "T1", 6)),
              21: ((5, "A0", 9), (6, "A1", 8), (7, "T0", 7))}

PRE_U = 4
GRP_U = 22
OUT_U0 = PRE_U + G * GRP_U
OUT_U = 2 * KT
PLE_U0 = OUT_U0 + OUT_U
GATE_U0 = PLE_U0 + 2
LAYER_U = GATE_U0 + KT
LAYER_F = OUT_U0 + 3 * KT
NUNITS = DEPTH * LAYER_U

C_COS, C_SIN = 0, T
C_ID = 2 * T
C_TRI = C_ID + P
C_ONE = C_TRI + T
C_SEQ = C_ONE + P
C_EPS = C_SEQ + NB
NCONST = C_EPS + 2
NMASK = 3 * P + NB * P + NSM

G_CW, G_CB = 0, 24
G_D, G_NW = 30, 34
G_SW = 38
G_SK, G_SKS = 44, 48
NGP = 49

FW = 3 + NPR + NB * (3 + NS)
CW = FW - 3
SW_IN = 2 + NPR + NB * (2 + NS)
SW = SW_IN - 2


def hybrid_step(nc, wts, wdt, x0, p_t, npre, npost, gpar, dtpar, s0_t, kc_t, vc_t, cs_in, sc_in, consts, masks, resets,
                xs, kout, vout, kold, vold, conv_out, scv_out, ssm_p, ssm_s):
    ctx = ExitStack()
    with ctx:
        def sem(name):
            return ctx.enter_context(nc.semaphore(name))

        def sb(name, cols, dt=F32):
            return ctx.enter_context(nc.sbuf_tensor(name, [P, cols], dt))

        RAW = [sb(f"raw{i}", UNIT) for i in range(2)]
        WHI = [sb(f"whi{i}", UNIT, F32R) for i in range(2)]
        WLO = [sb(f"wlo{i}", UNIT, F32R) for i in range(2)]
        HHI = sb("h_hi", KT * T, F32R)
        HLO = sb("h_lo", KT * T, F32R)
        YX = sb("y_or_x", 2 * KT * T)
        CST = sb("cst", NCONST)
        GP = sb("gpar_sb", NGP)
        NRM = sb("norm_weights", 2 * KT)
        DTP = sb("dt_params", 4)
        TOK = sb("tok", 288)
        TG = sb("tok_group", 72)
        FB = [sb(f"conv_in{i}", FW) for i in range(2)]
        AB = [sb(f"conv_sum{i}", CW) for i in range(2)]
        TH = [sb(f"tanh{i}", CW) for i in range(2)]
        CSI = sb("conv_state_in", 6 * 24)
        CSO = sb("conv_state_out", 6 * 27)
        SCI = sb("short_state_in", 2 * 16)
        SCO = sb("short_state_out", 2 * 18)
        RS = sb("rs", T)
        RV = sb("rs_v", T)
        RA = sb("rs_a", T)
        SQ = sb("sq", T)
        B3 = sb("b3", P, F32R)
        BM3 = sb("b3_masked", NB * P, F32R)[:, :].rearrange("p (b n) -> p b n", b=NB)
        X3 = sb("x3", GW, F32R)
        SQI = sb("sq_tile", T)
        work = ExitStack()
        WK_N = 15408
        WK = work.enter_context(nc.sbuf_tensor("work", [P, WK_N], F32))
        work.close()
        at = [0]

        def cut(n, restart=None):
            if restart is not None:
                at[0] = restart
            a = WK[:, at[0]:at[0] + n]
            at[0] += n
            assert at[0] <= WK_N, at[0]
            return a

        XC = cut(6 * T).rearrange("p (t n) -> p t n", n=T)
        Z2 = cut(4 * T).rearrange("p (t n) -> p t n", n=T)
        G2 = cut(2 * T).rearrange("p (t n) -> p t n", n=T)
        SCB = cut(T)
        SBB = cut(T)
        SG2 = cut(T)
        USC = FB[0][:, 1:1 + SW_IN]
        CSUM = AB[0][:, 0:SW]
        HEAVY = at[0]
        XDT = cut(3 * GW).rearrange("p (c n) -> p c n", c=3)
        XW = cut(3 * GW).rearrange("p (c n) -> p c n", c=3)
        S1 = XW[:, 0, :]
        BT = cut(2 * P).rearrange("p (c n) -> p c n", c=2)
        CBM = cut(T)
        MH = [cut(T) for _ in range(6)]
        EA = [cut(P + NSM) for _ in range(3)]
        DEC = cut(HG * 9).rearrange("p (h n) -> p h n", n=9)
        S0 = cut(GW)
        YT = cut(T)
        YS = cut(T)
        LATE = at[0]
        S0T = cut(NB * GW)
        Q = cut(2 * T, HEAVY).rearrange("p (t n) -> p t n", n=T)
        QS = cut(2 * T).rearrange("p (t n) -> p t n", n=T)
        QSM = cut(4 * NSM)
        KCUR = cut(T)
        KC = cut(NB * P)
        VC = cut(NB * HD).rearrange("p (b d) -> p b d", d=HD)
        VCUR = cut(3 * HD).rearrange("p (c d) -> p c d", d=HD)
        MSK = cut(NMASK)
        MX = cut(16)
        NM = cut(16)
        DEN = cut(16)
        OS = cut(2 * NSM).rearrange("p (a n) -> p a n", n=NSM)
        PR = cut(4 * 3 * P).rearrange("p (j n) -> p j n", j=4)
        PS = cut(NB * P + NSM)
        PT = cut(4 * 3 * P).rearrange("p (j n) -> p j n", j=4)
        PTS = cut(9 * P)
        XSQ = cut(KT * T, 0)
        DT0 = cut(T, HEAVY + 2400)
        AC0 = cut(T)
        W0 = cut(T)
        DTR = cut(T)
        DTE = cut(T)
        DTU = cut(T)
        DTC = cut(T)
        RST = cut(T)
        HF = [cut(T) for _ in range(4)]
        assert at[0] <= LATE
        KTT = cut(2 * T, LATE).rearrange("p (t n) -> p t n", n=T)
        KSW = cut(2 * T).rearrange("p (t n) -> p t n", n=T)
        VTT = cut(2 * T).rearrange("p (t n) -> p t n", n=T)
        VT = cut(2 * 3 * P).rearrange("p (t n) -> p t n", t=2)
        post = ctx.enter_context(ExitStack())
        YHI = post.enter_context(nc.sbuf_tensor("yssd_hi", [P, KT * T], F32R))
        YLO = post.enter_context(nc.sbuf_tensor("yssd_lo", [P, KT * T], F32R))
        MIX = post.enter_context(nc.sbuf_tensor("mix", [P, KT * T], F32))
        MSQ = [post.enter_context(nc.sbuf_tensor(f"mix_sq{i}", [P, T], F32)) for i in range(2)]
        assert 3 * KT * T + 2 * T <= WK_N and 2 * KT * T + UNIT - KT * T <= HEAVY + 2400
        DTRAW = YX[:, KT * T:KT * T + UNIT]
        PRAW = YX[:, KT * T:KT * T + 2 * T]

        COS, SIN = CST[:, C_COS:C_COS + T], CST[:, C_SIN:C_SIN + T]
        ID, ONES = CST[:, C_ID:C_ID + P], CST[:, C_ONE:C_ONE + P]
        TRI = CST[:, C_TRI:C_TRI + T]
        TGV = TG[:, :].rearrange("p (c v h) -> p c v h", c=3, v=3)

        MAIN = [ctx.enter_context(nc.psum_tensor(f"main{i}", [P, 512], F32)) for i in range(2)]

        class Bank:

            def __init__(self, name, pre, grp, post_):
                self.t = ctx.enter_context(nc.psum_tensor(name, [P, 512], F32))
                self.full, self.free = sem(name + "_full"), sem(name + "_free")
                self.pre, self.grp, self.per = pre, grp, pre + G * grp + post_

            def in_pre(self, L, n):
                return L * self.per + (n + 1)

            def in_grp(self, L, g, n):
                return L * self.per + g * self.grp + (self.pre + n + 1)

            def in_post(self, L, n):
                return L * self.per + (self.pre + G * self.grp + n + 1)

        A0, A1 = Bank("a0", 0, 10, 0), Bank("a1", 0, 9, 0)
        YB, YO = Bank("yb", 0, 7, 0), Bank("yo", 0, 7, 0)
        T0, T1 = Bank("t0", 3, 8, 1), Bank("t1", 2, 8, 0)
        BANKS = {"A0": A0, "A1": A1, "T0": T0, "T1": T1}
        SIDE = [A0, A1, YB, YO, T0, T1]

        raw_landed = [sem(f"raw_landed{i}") for i in range(2)]
        hi_done, lo_done, lop_done = sem("hi_done"), sem("lo_done"), sem("lop_done")
        units_used, filled = sem("units_used"), sem("filled")
        bank_free = [sem(f"main_free{i}") for i in range(2)]
        const_in, layer_in, dtw_in, xres_in, p_in = (sem(n) for n in ("const_in", "layer_in", "dtw_in", "xres_in", "p_in"))
        x_first, x_final, x_stored, x_slab0 = (sem(n) for n in ("x_first", "x_final", "x_stored", "x_slab0"))
        xsq_done, xsq_sum, h_scaled, h_hi, h_lo = (sem(n) for n in ("xsq_done", "xsq_sum", "h_scaled", "h_hi", "h_lo"))
        norm_ln = sem("norm_ln")
        dt_hi, dt_lo = sem("dt_hi"), sem("dt_lo")
        dt_abs, dt_exp, dt_u, dt_ln, dt_ac, dt_wexp, dt_ready, tok_ready = (
            sem(n) for n in ("dt_abs", "dt_exp", "dt_u", "dt_ln", "dt_ac", "dt_wexp", "dt_ready", "tok_ready"))
        k_swapped, k_ready, v_ready, v_tok, k_stored, v_stored = (
            sem(n) for n in ("k_swapped", "k_ready", "v_ready", "v_tok", "k_stored", "v_stored"))
        old_copied = sem("old_copied")
        gp_in, att_in, msk_in, sin_in = sem("gp_in"), sem("att_in"), sem("msk_in"), sem("sin_in")
        st_in = [sem(f"st_in{i}") for i in range(4)]
        b3_ready, x3_hi, x3_ready = sem("b3_ready"), sem("x3_hi"), sem("x3_ready")
        q_swapped, q_ready, qsm_ready = sem("q_swapped"), sem("q_ready"), sem("qsm_ready")
        th_ready, th_used = sem("th_ready"), sem("th_used")
        att_max, att_exp, att_prob, smp_max, smp_exp, smp_prob = (
            sem(n) for n in ("att_max", "att_exp", "att_prob", "smp_max", "smp_exp", "smp_prob"))
        pt_ready, pts_ready, os_ready, att_done = (
            sem(n) for n in ("pt_ready", "pts_ready", "os_ready", "att_done"))
        tap_done, conv_sum, xc_ready, conv_saved, csout_stored = (
            sem(n) for n in ("tap_done", "conv_sum", "xc_ready", "conv_saved", "csout_stored"))
        tg_ready, bt_ready, bm_ready, xt_ready = (
            sem(n) for n in ("tg_ready", "bt_ready", "bm_ready", "xt_ready"))
        decay_ready, mh_ready, ea_ready, s0_ready, y_used, y_gated, y_sq = (
            sem(n) for n in ("decay_ready", "mh_ready", "ea_ready", "s0_ready", "y_used", "y_gated", "y_sq"))
        s1_ready, smp_state, s1_stored, state_stored, ssd_done = (
            sem(n) for n in ("s1_ready", "smp_state", "s1_stored", "state_stored", "ssd_done"))
        c_ready, u_ready, stap_done, sc_done, sc_saved, scout_stored = (
            sem(n) for n in ("c_ready", "u_ready", "stap_done", "sc_done", "sc_saved", "scout_stored"))
        y_hi, y_lo, mix_sq, mix_added, p_hi, p_lo = (
            sem(n) for n in ("y_hi", "y_lo", "mix_sq", "mix_added", "p_hi", "p_lo"))
        x_mid, x_hi, x_lo = sem("x_mid"), sem("x_hi"), sem("x_lo")

        passed = {e: sem("passed_" + e) for e in ("pe", "dve", "pool")}

        def wait_alone(eng, name, s, v):
            eng.wait_ge(s, v)
            eng.sem_inc(passed[name], 1)

        def unit(L, k):
            return L * LAYER_U + k

        def gunit(L, g, k):
            return L * LAYER_U + g * GRP_U + (PRE_U + k)

        def fill_bank(L, g, k):
            return L * (LAYER_F // 2) + g * (GRP_U // 2) + (PRE_U // 2 + k // 2 + 1)

        def gfill(L, g, k):
            return L * LAYER_F + g * GRP_U + (PRE_U + k + 1)

        def it(L, g, per=1, n=0):
            return L * (G * per) + g * per + (n + 1)

        def smp(ap, w=NS):
            return ap.rearrange("p (b t) -> p b t", t=w)

        def fsmp(ap, k):
            return smp(ap[:, k + NPR:k + NPR + NB * (k + NS)], k + NS)

        def pool_blocks(k):
            return 12 if k is not None and k >= 14 else 8

        block = ctx.enter_context(nc.Block())

        @block.sync
        def _(sp):
            def load_unit(u, s, guard=True):
                if guard:
                    sp.wait_ge(hi_done, u - 1)
                    sp.wait_ge(lo_done, u - 1)
                    sp.wait_ge(lop_done, u - 1)
                sp.dma_start(RAW[s][:, :], wts[u]).then_inc(raw_landed[s], 16)

            sp.dma_start(YX[:, 0:KT * T], x0).then_inc(x_first, 16)
            sp.dma_start(CST[:, :], consts).then_inc(const_in, 16)
            sp.wait_ge(x_first, 16)
            sp.dma_start(xs[0], YX[:, 0:KT * T]).then_inc(x_slab0, 16)
            with sp.Fori(0, DEPTH) as L:
                sp.wait_ge(x_final, L + 1)
                for k in range(2):
                    load_unit(unit(L, k), k, False)
                sp.dma_start(DTRAW, wdt[L]).then_inc(dtw_in, 16)
                sp.dma_start(NRM[:, 0:KT], npre[L]).then_inc(layer_in, 16)
                sp.dma_start(NRM[:, KT:2 * KT], npost[L]).then_inc(layer_in, 16)
                sp.dma_start(DTP[0:32, 0:2], dtpar[L]).then_inc(layer_in, 16)
                sp.dma_start(RST[0:32, :], resets).then_inc(layer_in, 16)
                for k in (2, 3):
                    load_unit(unit(L, k), k % 2)
                with sp.Fori(0, G) as g:
                    for k in range(GRP_U):
                        load_unit(gunit(L, g, k), k % 2)
                        if k == 3:
                            sp.wait_ge(smp_state, it(L, g))
                            sp.wait_ge(y_sq, it(L, g))
                            sp.wait_ge(s1_stored, L * (G * 16) + g * 16 + 16)
                            sp.wait_ge(k_stored, L * 32 + 32)
                            sp.wait_ge(v_stored, L * 128 + 128)
                            for r in range(2):
                                sp.dma_start(KCUR[64 * r:64 * r + 64, :], kout[L, g]).then_inc(att_in, 16)
                            sp.dma_start(KC[0:64, :], kc_t[L, g]).then_inc(att_in, 16)
                            sp.dma_start(VC, vc_t[L, g].rearrange("w (b d) -> w b d", d=HD)).then_inc(att_in, 16)
                            v_g = vout[L, g]
                            sp.dma_start(VCUR[:, 0:2, :], v_g[0:NPR].rearrange("(c p) d -> p c d", p=P)).then_inc(att_in, 16)
                            sp.dma_start(VCUR[0:NSM, 2, :], v_g[NPR:T]).then_inc(att_in, 16)
                            sp.dma_start(MSK, masks).then_inc(msk_in, 16)
                        if k == 4:
                            sp.wait_ge(ssd_done, it(L, g))
                            sp.wait_ge(conv_saved, L * (G * 6) + g * 6 + 2)
                            sp.dma_start(GP[:, :], gpar[L, g]).then_inc(gp_in, 16)
                            sp.dma_start(CSI[:, :], cs_in[L, g]).then_inc(sin_in, 16)
                            sp.dma_start(SCI[:, :], sc_in[L, g]).then_inc(sin_in, 16)
                        if 15 <= k < 19:
                            i = k - 15
                            if i == 0:
                                sp.wait_ge(att_done, it(L, g))
                            sp.dma_start(S0T.rearrange("p (b n) -> p b n", b=NB)[:, :, i * P:(i + 1) * P],
                                         s0_t[L, g].rearrange("p (b n) -> p b n", b=NB)[:, :, i * P:(i + 1) * P]).then_inc(st_in[i], 16)
                with sp.Fori(0, KT // 2) as m:
                    for k in range(4):
                        load_unit(L * LAYER_U + m * 4 + (OUT_U0 + k), k % 2)
                for k in range(2):
                    load_unit(unit(L, PLE_U0 + k), k)
                sp.wait_ge(y_hi, L * 8 + 8)
                sp.wait_ge(y_lo, L * 8 + 8)
                sp.wait_ge(x_slab0, 16)
                sp.wait_ge(x_stored, L * 16 + 16)
                sp.dma_start(YX[:, 0:KT * T], xs[L]).then_inc(xres_in, 16)
                sp.dma_start(PRAW, p_t[L]).then_inc(p_in, 16)
                with sp.Fori(0, KT // 2) as m:
                    for k in range(2):
                        load_unit(L * LAYER_U + m * 2 + (GATE_U0 + k), k % 2)
                sp.wait_ge(x_final, L + 2)
                sp.dma_start(xs[L + 1], YX[:, 0:KT * T]).then_inc(x_stored, 16)
            sp.wait_ge(x_stored, DEPTH * 16 + 16)

        @block.tensor
        def _(pe):
            mm, tr = nc.tensor.matmul, nc.tensor.transpose

            wait = pe.wait_ge

            def product(out, s, n, hi, lo, k, start, stop):
                w_hi, w_lo = WHI[s][:, n * BLK:(n + 1) * BLK], WLO[s][:, n * BLK:(n + 1) * BLK]
                x_hi_, x_lo_ = hi[:, k * T:(k + 1) * T], lo[:, k * T:(k + 1) * T]
                mm(out, w_hi, x_hi_, start=start, stop=False)
                mm(out, w_hi, x_lo_, start=False, stop=False)
                return mm(out, w_lo, x_hi_, start=False, stop=stop)

            def wait_unit(u):
                wait(hi_done, u + 1)
                wait(lo_done, u + 1)
                wait(lop_done, u + 1)

            def project(u, b, fb):
                wait_unit(u)
                wait(bank_free[b], fb)
                for k in range(KT):
                    last = product(MAIN[b][:, 0:T], b, k, HHI, HLO, k, k == 0, k == KT - 1)
                last.then_inc(filled, 1)
                pe.drain().then_inc(units_used, 1)

            pe.sem_inc(units_used, 2)
            for b in bank_free:
                pe.sem_inc(b, 1)
            for bk in SIDE:
                pe.sem_inc(bk.free, 1)
            wait(const_in, 16)
            with pe.Fori(0, DEPTH) as L:
                wait(xsq_sum, L + 1)
                wait(T0.free, T0.in_pre(L, 0))
                for j in range(4):
                    last = mm(T0.t[:, 0:T], ONES, XSQ[:, j * T:(j + 1) * T], start=(j == 0), stop=(j == 3))
                last.then_inc(T0.full, 1)
                for k in range(PRE_U):
                    if k == 0:
                        wait_unit(unit(L, 0))
                        wait(bank_free[0], L * (LAYER_F // 2) + 1)
                        for n in range(KT):
                            wait(h_hi, L * KT + (n + 1))
                            wait(h_lo, L * KT + (n + 1))
                            last = product(MAIN[0][:, 0:T], 0, n, HHI, HLO, n, n == 0, n == KT - 1)
                        last.then_inc(filled, 1)
                        pe.drain().then_inc(units_used, 1)
                        wait(dt_hi, L + 1)
                        wait(dt_lo, L + 1)
                        wait(T1.free, T1.in_pre(L, 0))
                        for n in range(KT):
                            w, wl = YHI[:, n * BLK:(n + 1) * BLK], YLO[:, n * BLK:(n + 1) * BLK]
                            c0 = n * T
                            mm(T1.t[:, 0:T], w, HHI[:, c0:c0 + T], start=(n == 0), stop=False)
                            mm(T1.t[:, 0:T], w, HLO[:, c0:c0 + T], start=False, stop=False)
                            last = mm(T1.t[:, 0:T], wl, HHI[:, c0:c0 + T], start=False, stop=(n == KT - 1))
                        last.then_inc(T1.full, 1)
                    else:
                        project(unit(L, k), k % 2, L * (LAYER_F // 2) + (k // 2 + 1))
                    if k == 2:
                        wait(dt_ready, L + 1)
                        wait_alone(pe, "pe", T0.free, T0.in_pre(L, 1))
                        for v, a in enumerate((DT0, AC0, W0)):
                            for c in range(3):
                                n = P if c < 2 else NSM
                                last = tr(T0.t[0:n, c * 96 + v * 32:c * 96 + v * 32 + 32], a[0:32, c * P:c * P + n], ID[0:32, 0:32])
                        last.then_inc(T0.full, 1)
                for i, bk in enumerate((T0, T1)):
                    wait(v_ready, L * 2 + (i + 1))
                    wait(bk.free, bk.in_pre(L, 2 if i == 0 else 1))
                    for c in range(3):
                        n = P if c < 2 else NSM
                        last = tr(bk.t[0:n, c * P:c * P + P], VTT[:, i, c * P:c * P + n], ID)
                    last.then_inc(bk.full, 1)

                with pe.Fori(0, G) as g:
                    def use(bk, n):
                        wait(bk.free, bk.in_grp(L, g, n))

                    def scores(j):
                        bk = (A0, A1, T0, T1)[j]
                        a, r = j // 2, 64 * (j % 2)
                        use(bk, 0)
                        q, kk = Q[r:r + 64, a, :], KCUR[r:r + 64, :]
                        mm(bk.t[:, 0:P], q[:, 0:P], kk[:, 0:P], start=True, stop=True)
                        mm(bk.t[:, P:3 * P], q[:, P:2 * P], kk[:, 0:2 * P], start=True, stop=True).then_inc(bk.full, 1)

                    def turn_probs(j):
                        bk, n = ((T0, 1), (T1, 1), (A0, 2), (A1, 1))[j]
                        use(bk, n)
                        for c in range(3):
                            last = tr(bk.t[:, c * P:c * P + P], PR[:, j, c * P:c * P + P], ID)
                        last.then_inc(bk.full, 1)

                    def values(j):
                        bk, n = ((T1, 2), (A0, 3))[j // 2]
                        r = 64 * (j % 2)
                        if j % 2 == 0:
                            use(bk, n)
                        mm(bk.t[r:r + 64, 0:P], VCUR[:, 0, :], PT[:, j, 0:P], start=True, stop=True)
                        mm(bk.t[r:r + 64, P:2 * P], VCUR[:, 0, :], PT[:, j, P:2 * P], start=True, stop=False)
                        last = mm(bk.t[r:r + 64, P:2 * P], VCUR[:, 1, :], PT[:, j, 2 * P:3 * P], start=False, stop=True)
                        if j % 2:
                            last.then_inc(bk.full, 1)

                    def decay(h):
                        bk, n = ((A0, 4), (A1, 3))[h % 2]
                        use(bk, n + h // 2)
                        for c in range(3):
                            w = P if c < 2 else NSM
                            last = mm(bk.t[:, c * P:c * P + w], TGV[0:w, c, 1, h:h + 1].to_broadcast([w, P]), ID[0:w, 0:w],
                                      start=True, stop=True)
                        last.then_inc(bk.full, 1)

                    def y_pair(i):
                        use(YB, 3 + i)
                        for r in range(2):
                            h = 2 * i + r
                            wait(mh_ready, it(L, g, HG, h))
                            m = MH[h % 6]
                            for c in range(3):
                                w = P if c < 2 else NSM
                                last = mm(YB.t[64 * r:64 * r + 64, c * P:c * P + w], XDT[0:w, c, h * HD:(h + 1) * HD],
                                          m[0:w, c * P:c * P + w], start=True, stop=True)
                        last.then_inc(YB.full, 1)
                        use(YO, 3 + i)
                        cc = XC[:, 1, :]
                        mm(YO.t[:, 0:P], S0[:, i * P:(i + 1) * P], cc[:, P:2 * P], start=True, stop=True)
                        for b in range(NB):
                            last = mm(YO.t[:, P + NS * b:P + NS * b + NS], S0T[:, b * GW + i * P:b * GW + (i + 1) * P],
                                      cc[:, NPR + NS * b:NPR + NS * b + NS], start=True, stop=True)
                        last.then_inc(YO.full, 1)

                    def new_state(b, bk, n):
                        use(bk, n)
                        mm(bk.t[:, :], BM3[0:3 * NSM, b, :], X3[0:3 * NSM, :], start=True, stop=True).then_inc(bk.full, 1)

                    for k in range(GRP_U):
                        project(gunit(L, g, k), k % 2, fill_bank(L, g, k))
                        if k == 2:
                            wait(q_ready, it(L, g, 2, 1))
                            wait(att_in, L * (G * 96) + g * 96 + 96)
                            scores(0)
                            scores(1)
                        if k == 3:
                            scores(2)
                            scores(3)
                        if k == 4:
                            wait(qsm_ready, it(L, g))
                            for s, bk, n in ((0, YB, 0), (1, YO, 0), (2, A0, 1)):
                                use(bk, n)
                                keys = KC[0:64, s * 512:s * 512 + 512] if s < 2 else KCUR[0:64, NPR:T]
                                w = 512 if s < 2 else NSM
                                mm(bk.t[:, 0:w], QSM[0:64, :], keys, start=True, stop=True).then_inc(bk.full, 1)
                        if k == 7:
                            wait(att_prob, it(L, g))
                            for j in range(4):
                                turn_probs(j)
                        if k == 8:
                            wait(smp_prob, it(L, g))
                            for bk, b0 in ((YB, 0), (YO, 4)):
                                use(bk, 1)
                                for b in range(4):
                                    last = tr(bk.t[:, b * P:b * P + P], PS[:, (b0 + b) * P:(b0 + b + 1) * P], ID)
                                last.then_inc(bk.full, 1)
                        if k == 9:
                            wait_alone(pe, "pe", T0.free, T0.in_grp(L, g, 2))
                            tr(T0.t[0:NSM, 0:P], PS[:, NB * P:NB * P + NSM], ID).then_inc(T0.full, 1)
                            wait(pt_ready, it(L, g, 4, 3))
                            for j in range(4):
                                values(j)
                        if k == 10:
                            wait(pts_ready, it(L, g))
                            use(A1, 2)
                            o = A1.t[0:64, 0:P]
                            mm(o, VCUR[0:NSM, 2, :], PTS[0:NSM, NB * P:9 * P], start=True, stop=False, skip_group_check=True)
                            for b in range(NB):
                                mine = PTS[:, b * P:b * P + P].rearrange("p (j n) -> p j n", j=4)[:, :, NS * b:NS * b + NS]
                                last = mm(o.rearrange("p (j n) -> p j n", j=4)[:, :, NS * b:NS * b + NS], VC[:, b, :], mine,
                                          start=False, stop=(b == NB - 1), skip_group_check=True)
                            last.then_inc(A1.full, 1)
                            wait(xc_ready, it(L, g, 6, 1) + 2)
                            use(YB, 2)
                            use(YO, 2)
                            for c in range(3):
                                w = P if c < 2 else NSM
                                last = tr(YB.t[0:w, c * P:c * P + P], XC[:, 0, c * P:c * P + w], ID)
                            last.then_inc(YB.full, 1)
                            for c in range(3):
                                w = P if c < 2 else NSM
                                last = mm(YO.t[0:w, c * P:c * P + w], XC[:, 0, c * P:c * P + w], XC[:, 1, c * P:c * P + w],
                                          start=True, stop=True)
                            last.then_inc(YO.full, 1)
                        if k in (14, 15):
                            wait(xc_ready, it(L, g, 6, 5) + 2)
                            for c in (0, 1) if k == 14 else (2,):
                                bk, n = ((T0, 3), (T1, 3), (T0, 4))[c]
                                w = P if c < 2 else NSM
                                use(bk, n)
                                for i in range(4):
                                    last = tr(bk.t[0:w, i * P:i * P + P], XC[:, 2 + i, c * P:c * P + w], ID)
                                last.then_inc(bk.full, 1)
                        if k == 15:
                            wait(xt_ready, it(L, g, 3, 1))
                            wait(bt_ready, it(L, g))
                            use(T1, 4)
                            mm(T1.t[:, :], BT[:, 0, :], XW[:, 0, :], start=True, stop=True).then_inc(T1.full, 1)
                        if 14 <= k < 18:
                            if k == 14:
                                wait(tg_ready, it(L, g))
                            decay(2 * (k - 14))
                            decay(2 * (k - 14) + 1)
                        if 16 <= k < 20:
                            if k == 16:
                                wait(xt_ready, it(L, g, 3, 2))
                                wait(s0_ready, it(L, g))
                            wait(st_in[k - 16], L * (G * 16) + g * 16 + 16)
                            y_pair(k - 16)
                        if k == 17:
                            use(T0, 5)
                            mm(T0.t[:, :], BT[:, 1, :], XW[:, 1, :], start=True, stop=True).then_inc(T0.full, 1)
                        if k == 21:
                            wait(y_sq, it(L, g) + 1)
                            use(T1, 7)
                            mm(T1.t[:, 0:T], ONES, SQ[:, :], start=True, stop=True).then_inc(T1.full, 1)
                        if k >= 19:
                            if k == 19:
                                wait(bm_ready, it(L, g))
                                wait(x3_ready, it(L, g))
                            for b, bk, n in NEW_STATES[k]:
                                new_state(b, BANKS[bk], n)

                def out_tile(u, b, fb, pieces):
                    wait_unit(u)
                    wait(bank_free[b], fb)
                    for k in range(KT):
                        if pieces and k % 4 == 0:
                            wait(y_hi, L * 8 + (k // 4 + 1))
                            wait(y_lo, L * 8 + (k // 4 + 1))
                        last = product(MAIN[b][:, 0:T], 0, k, HHI, HLO, k, k == 0, False)
                    pe.drain().then_inc(units_used, 1)
                    wait_unit(u + 1)
                    for k in range(KT):
                        if pieces and k % 4 == 0:
                            wait(y_hi, L * 8 + (4 + k // 4 + 1))
                            wait(y_lo, L * 8 + (4 + k // 4 + 1))
                        last = product(MAIN[b][:, 0:T], 1, k, YHI, YLO, k, False, k == KT - 1)
                    last.then_inc(filled, 1)
                    pe.drain().then_inc(units_used, 1)

                fb0 = LAYER_F // 2
                for m in range(2):
                    out_tile(unit(L, OUT_U0 + 2 * m), m, L * fb0 + (OUT_U0 // 2 + 1), True)
                with pe.Fori(1, KT // 2) as mp:
                    for m in range(2):
                        out_tile(L * LAYER_U + mp * 4 + (OUT_U0 + 2 * m), m, L * fb0 + mp + (OUT_U0 // 2 + 1), False)
                wait(mix_added, L * KT + (KT + 2))
                wait(T0.free, T0.in_post(L, 0))
                mm(T0.t[:, 0:T], ONES, SQ[:, :], start=True, stop=True).then_inc(T0.full, 1)
                wait(p_hi, L + 1)
                wait(p_lo, L + 1)
                for s in range(2):
                    wait_unit(unit(L, PLE_U0 + s))
                    for m in range(8):
                        wait(bank_free[m % 2], L * fb0 + ((OUT_U0 + KT + 8 * s) // 2 + m // 2 + 1))
                        product(MAIN[m % 2][:, 0:T], s, 2 * m, YHI, YLO, 0, True, False)
                        product(MAIN[m % 2][:, 0:T], s, 2 * m + 1, YHI, YLO, 1, False, True).then_inc(filled, 1)
                    pe.drain().then_inc(units_used, 1)
                for m in range(2):
                    wait_unit(unit(L, GATE_U0 + m))
                    wait(bank_free[m], L * fb0 + ((OUT_U0 + 2 * KT) // 2 + 1))
                    for k in range(KT):
                        if m == 0:
                            wait(x_hi, L * KT + (k + 1))
                            wait(x_lo, L * KT + (k + 1))
                        last = product(MAIN[m][:, 0:T], m, k, HHI, HLO, k, k == 0, k == KT - 1)
                    last.then_inc(filled, 1)
                    pe.drain().then_inc(units_used, 1)
                with pe.Fori(1, KT // 2) as mp:
                    for m in range(2):
                        project(L * LAYER_U + mp * 2 + (GATE_U0 + m), m, L * fb0 + mp + ((OUT_U0 + 2 * KT) // 2 + 1))

        @block.scalar
        def _(act):
            fn = nc.scalar.activation

            def split_hi(u, s, h=None):
                act.wait_ge(units_used, u + 1)
                act.wait_ge(raw_landed[s], h)
                fn(WHI[s][:, :], RAW[s][:, :], ACT.Copy).then_inc(hi_done, 1)

            def landed(L, k, g=0, gper=0, m=0, mper=0):
                v = L * (LAYER_U // 2 * 16) + (k // 2 * 16 + 16)
                if gper:
                    v = v + g * (gper // 2 * 16)
                return v

            def swap(dst, src):
                for a, b in ((0, 32), (32, 0), (64, 96), (96, 64)):
                    last = fn(dst[a:a + 32, :], src[b:b + 32, 0:T], ACT.Copy)
                return last

            def rsqrt(bank, ready, inv, eps_col):
                act.wait_ge(bank.full, ready)
                fn(RV[:, :], bank.t[:, 0:T], ACT.Ln, scale=inv, bias=CST[:, eps_col:eps_col + 1])
                act.drain()
                fn(RS[:, :], RV[:, :], ACT.Exp, scale=-0.5).then_inc(norm_ln, 1)

            act.dma_start(kold, kc_t.rearrange("l g d (b w) -> (l g d) b w", w=P)[:, :, NS:P]).then_inc(old_copied, 16)
            act.dma_start(vold, vc_t[:, :, NS:P, :].rearrange("l g w n -> (l g) w n")).then_inc(old_copied, 16)
            act.wait_ge(const_in, 16)
            act.sem_inc(state_stored, 16)
            act.sem_inc(s1_stored, 16)
            act.sem_inc(csout_stored, 16)
            act.sem_inc(scout_stored, 16)
            with act.Fori(0, DEPTH) as L:
                act.wait_ge(x_final, L + 1)
                for j in range(4):
                    fn(XSQ[:, j * 4 * T:(j + 1) * 4 * T], YX[:, j * 4 * T:(j + 1) * 4 * T], ACT.Square).then_inc(xsq_done, 1)
                split_hi(unit(L, 0), 0, landed(L, 0))
                rsqrt(T0, T0.in_pre(L, 0), 1.0 / DM, C_EPS)
                for i in range(KT):
                    act.wait_ge(h_scaled, L * KT + (i + 1))
                    fn(HHI[:, i * T:(i + 1) * T], HF[i % 4], ACT.Copy).then_inc(h_hi, 1)
                act.wait_ge(dtw_in, L * 16 + 16)
                fn(YHI[:, 0:UNIT], DTRAW, ACT.Copy).then_inc(dt_hi, 1)
                split_hi(unit(L, 1), 1, landed(L, 1))
                act.wait_ge(layer_in, L * 64 + 64)
                fn(DTP[0:32, 2:3], DTP[0:32, 1:2], ACT.Exp)
                for k in range(PRE_U):
                    act.wait_ge(filled, L * LAYER_F + (k + 1))
                    split_hi(unit(L, k + 2), k % 2, landed(L, k + 2))
                    if k < 2:
                        swap(KSW[:, k, :], MAIN[k % 2]).then_inc(k_swapped, 1)
                    else:
                        fn(VTT[:, k - 2, :], MAIN[k % 2][:, 0:T], ACT.Copy).then_inc(v_ready, 1)
                        act.drain().then_inc(bank_free[k % 2], 1)
                    if k == 0:
                        act.wait_ge(dt_abs, L + 1)
                        fn(DTE[0:32, :], DTU[0:32, :], ACT.Exp, scale=-1.0).then_inc(dt_exp, 1)
                        act.wait_ge(dt_u, L + 1)
                        fn(DTC[0:32, :], DTU[0:32, :], ACT.Ln).then_inc(dt_ln, 1)
                    if k == 1:
                        act.wait_ge(dt_ac, L + 1)
                        fn(W0[0:32, :], DTE[0:32, :], ACT.Exp, scale=-1.0).then_inc(dt_wexp, 1)
                    if k == 2:
                        for i in range(2):
                            act.wait_ge(k_ready, L * 2 + (i + 1))
                            act.dma_start(kout[L, 2 * i:2 * i + 2].rearrange("h d n -> (h d) n"), KTT[:, i, :]).then_inc(k_stored, 16)
                        act.wait_ge(T0.full, T0.in_pre(L, 1))
                        fn(TOK[:, 0:192], T0.t[:, 0:192], ACT.Copy)
                        fn(TOK[0:NSM, 192:288], T0.t[0:NSM, 192:288], ACT.Copy).then_inc(tok_ready, 1)
                        act.drain().then_inc(T0.free, 1)
                for i, bk in enumerate((T0, T1)):
                    act.wait_ge(bk.full, bk.in_pre(L, 2 if i == 0 else 1))
                    fn(VT[:, i, 0:2 * P], bk.t[:, 0:2 * P], ACT.Copy)
                    fn(VT[0:NSM, i, 2 * P:3 * P], bk.t[0:NSM, 2 * P:3 * P], ACT.Copy).then_inc(v_tok, 1)
                    act.wait_ge(v_tok, L * 2 + (i + 1))
                    for h in range(2):
                        v_h = VT[:, i, :].rearrange("p (c h d) -> p c h d", c=3, h=2)[:, :, h, :]
                        act.dma_start(vout[L, 2 * i + h, 0:NPR].rearrange("(c p) d -> p c d", p=P), v_h[:, 0:2]).then_inc(v_stored, 16)
                        act.dma_start(vout[L, 2 * i + h, NPR:T], v_h[0:NSM, 2]).then_inc(v_stored, 16)
                    act.drain().then_inc(bk.free, 1)

                with act.Fori(0, G) as g:
                    th_n = [0]

                    def tanh_half(src, w, tag=None):
                        n = th_n[0]
                        th_n[0] += 1
                        act.wait_ge(th_used, L * 72 + g * 14 + (n + 1))
                        fn(TH[n % 2][:, 0:w], src, ACT.Tanh, scale=0.5).then_inc(th_ready, 1)

                    def decay_exp(h):
                        bk, n = ((A0, 4), (A1, 3))[h % 2]
                        m, i, r = MH[h % 6], h // 2, 64 * (h % 2)
                        act.wait_ge(bk.full, bk.in_grp(L, g, n + h // 2))
                        act.wait_ge(y_used, L * 16 + g * 4 + (i - 2 if i >= 3 else 0) + 1)
                        for c in range(2):
                            fn(m[:, c * P:(c + 1) * P], bk.t[:, c * P:(c + 1) * P], ACT.Relu, scale=-1.0, bias=TGV[:, c, 1, h:h + 1])
                        fn(m[0:NSM, NPR:T], bk.t[0:NSM, NPR:T], ACT.Relu, scale=-1.0, bias=TGV[0:NSM, 2, 1, h:h + 1])
                        fn(EA[i % 3][r:r + 64, :], bk.t[r:r + 64, P:T], ACT.Exp)
                        fn(DEC[:, h, :], bk.t[:, NPR - 1:T:4], ACT.Exp).then_inc(bk.free, 1)
                        act.drain()
                        fn(m[:, 0:NPR], m[:, 0:NPR], ACT.Exp, scale=-1.0)
                        fn(m[0:NSM, NPR:T], m[0:NSM, NPR:T], ACT.Exp, scale=-1.0).then_inc(decay_ready, 1)

                    for k in range(GRP_U):
                        b = k % 2
                        main = MAIN[b]
                        act.wait_ge(filled, gfill(L, g, k))
                        if k < 2:
                            swap(QS[:, k, :], main).then_inc(q_swapped, 1)
                        if k in (2, 3, 6, 20) or 14 <= k < 18:
                            tanh_half(main[:, 0:T], T)
                        if k in (4, 18):
                            i = k // 18
                            if k == 4:
                                act.wait_ge(sin_in, L * (G * 32) + g * 32 + 32)
                                act.wait_ge(gp_in, L * (G * 16) + g * 16 + 16)
                            else:
                                act.wait_ge(conv_saved, it(L, g, 6, 4) + 2)
                                act.wait_ge(xc_ready, it(L, g, 6, 4) + 2)
                            act.wait_ge(sc_done, L * (G * 2) + g * 2 + (i + 1))
                            act.wait_ge(sc_saved, L * (G * 2) + g * 2 + (i + 1))
                            fn(fsmp(USC, 2)[:, :, 0:2], smp(SCI[:, i * 16:(i + 1) * 16], 2), ACT.Copy)
                            fn(SCB, main[:, 0:T], ACT.Copy).then_inc(c_ready, 1)
                            act.drain().then_inc(bank_free[b], 1)
                        if 8 <= k < 14:
                            t = k - 8
                            f, s = FB[t % 2], AB[t % 2]
                            if t == 0:
                                act.wait_ge(sc_done, it(L, g, 2, 0) + 1)
                                act.wait_ge(sc_saved, it(L, g, 2, 0) + 1)
                            act.wait_ge(xc_ready, L * (G * 6) + g * 6 + (t + 1))
                            act.wait_ge(conv_saved, L * (G * 6) + g * 6 + (t + 1))
                            fn(fsmp(f, 3)[:, :, 0:3], smp(CSI[:, t * 24:(t + 1) * 24], 3), ACT.Copy)
                            fn(f[:, 3:3 + NPR], main[:, 0:NPR], ACT.Copy)
                            fn(fsmp(f, 3)[:, :, 3:7], smp(main[:, NPR:T]), ACT.Copy).then_inc(bank_free[b], 1)
                            act.drain()
                            fn(s[:, :], f[:, 0:CW], ACT.Identity, scale=GP[:, G_CW + 4 * t:G_CW + 4 * t + 1],
                               bias=GP[:, G_CB + t:G_CB + t + 1]).then_inc(tap_done, 1)
                        split_hi(gunit(L, g, k + 2), b, L * (LAYER_U // 2 * 16) + g * (GRP_U // 2 * 16) + ((PRE_U + k + 2) // 2 * 16 + 16))
                        if k == 2:
                            act.wait_ge(q_ready, it(L, g, 2, 1))
                            for j in range(4):
                                last = fn(QSM[0:64, j * NSM:(j + 1) * NSM], Q[64 * (j % 2):64 * (j % 2) + 64, j // 2, NPR:T], ACT.Copy)
                            last.then_inc(qsm_ready, 1)
                        if 8 <= k < 14:
                            act.wait_ge(conv_sum, it(L, g, 6, t))
                            tanh_half(s[:, :], CW)
                        if k in (5, 19):
                            i = k // 19
                            act.wait_ge(u_ready, it(L, g, 2, i))
                            fn(CSUM, USC[:, 0:SW], ACT.Copy, scale=GP[:, G_SW + 3 * i:G_SW + 3 * i + 1]).then_inc(stap_done, 1)
                        if k == 5:
                            act.wait_ge(att_max, it(L, g))
                            for j in range(4):
                                for c, (c0, c1) in enumerate(((0, P), (P, 3 * P))):
                                    fn(PR[:, j, c0:c1], PR[:, j, c0:c1], ACT.Exp, scale=HD ** -0.5, bias=NM[:, 2 * j + c:2 * j + c + 1],
                                       accum_out=DEN[:, 2 * j + c:2 * j + c + 1])
                            fn(MX[:, 0:8], MX[:, 0:8], ACT.Exp).then_inc(att_exp, 1)
                        if k == 6:
                            act.wait_ge(smp_max, it(L, g))
                            fn(PS, PS, ACT.Exp, scale=HD ** -0.5, bias=NM[:, 8:9], accum_out=DEN[:, 8:9])
                            fn(MX[:, 8:9], MX[:, 8:9], ACT.Exp).then_inc(smp_exp, 1)
                        if k == 8:
                            act.wait_ge(state_stored, L * (G * 16) + g * 16 + 16)
                            for j, (bk, n) in enumerate(((T0, 1), (T1, 1), (A0, 2), (A1, 1))):
                                act.wait_ge(bk.full, bk.in_grp(L, g, n))
                                fn(PT[:, j, :], bk.t[:, 0:3 * P], ACT.Copy).then_inc(pt_ready, 1)
                                act.drain().then_inc(bk.free, 1)
                        if k == 9:
                            for bk, b0 in ((YB, 0), (YO, 4)):
                                act.wait_ge(bk.full, bk.in_grp(L, g, 1))
                                fn(PTS[:, b0 * P:(b0 + 4) * P], bk.t[:, :], ACT.Copy).then_inc(bk.free, 1)
                            act.wait_ge(T0.full, T0.in_grp(L, g, 2))
                            fn(PTS[0:NSM, NB * P:9 * P], T0.t[0:NSM, 0:P], ACT.Copy).then_inc(pts_ready, 1)
                            act.drain().then_inc(T0.free, 1)
                        if k == 10:
                            act.wait_ge(A1.full, A1.in_grp(L, g, 2))
                            for j in range(4):
                                r = 64 * (j % 2)
                                last = fn(OS[r:r + 64, j // 2, :], A1.t[0:64, j * NSM:(j + 1) * NSM], ACT.Copy)
                            last.then_inc(os_ready, 1)
                            act.drain().then_inc(A1.free, 1)
                        if k == 12:
                            act.wait_ge(att_done, it(L, g))
                            act.wait_ge(YB.full, YB.in_grp(L, g, 2))
                            fn(BT[:, 0:2, :], YB.t[:, 0:2 * P].rearrange("p (c n) -> p c n", c=2), ACT.Copy)
                            for q in range(2):
                                last = fn(B3[q * NSM:(q + 1) * NSM, :], YB.t[0:NSM, 2 * P:3 * P], ACT.Copy)
                            last.then_inc(bt_ready, 1)
                        if k == 15:
                            act.wait_ge(T1.full, T1.in_grp(L, g, 4))
                            fn(S0, T1.t[:, :], ACT.Copy).then_inc(s0_ready, 1)
                            act.drain().then_inc(T1.free, 1)
                        if 14 <= k < 18:
                            decay_exp(2 * (k - 14))
                            decay_exp(2 * (k - 14) + 1)
                        if k == 16:
                            act.wait_ge(xt_ready, it(L, g, 3, 2))
                            for q in (0, 2):
                                last = fn(X3[q * NSM:(q + 1) * NSM, :], XW[0:NSM, 2, :], ACT.Copy)
                            last.then_inc(x3_hi, 1)
                        if k == 14:
                            act.wait_ge(conv_saved, it(L, g, 6, 5) + 2)
                            act.dma_start(conv_out[L, g], CSO[:, :]).then_inc(csout_stored, 16)
                        if k == 20:
                            act.wait_ge(s1_ready, it(L, g))
                            act.dma_start(ssm_p[L, g], S1).then_inc(s1_stored, 16)
                    rsqrt(T1, T1.in_grp(L, g, 7), 1.0 / GW, C_EPS + 1)
                    act.wait_ge(smp_state, it(L, g) + 1)
                    act.dma_start(ssm_s[L, g], S0T).then_inc(state_stored, 16)
                    act.wait_ge(sc_saved, it(L, g, 2, 1) + 1)
                    act.dma_start(scv_out[L, g], SCO[:, :]).then_inc(scout_stored, 16)

                act.wait_ge(units_used, unit(L, OUT_U0 + 2))
                act.wait_ge(sc_done, L * (G * 2) + (G * 2 + 1))
                for j in range(4):
                    c0 = (KT + 4 * j) * T
                    fn(HHI[:, 4 * j * T:4 * (j + 1) * T], YX[:, c0:c0 + 4 * T], ACT.Copy).then_inc(y_hi, 1)
                act.wait_ge(ssd_done, L * G + (G + 1))
                act.wait_ge(s1_stored, L * (G * 16) + (G * 16 + 16))
                for j in range(4):
                    fn(YHI[:, 4 * j * T:4 * (j + 1) * T], YX[:, 4 * j * T:4 * (j + 1) * T], ACT.Copy).then_inc(y_hi, 1)
                act.wait_ge(state_stored, L * (G * 16) + (G * 16 + 16))
                with act.Fori(0, KT // 2) as mp:
                    for q in range(4):
                        split_hi(L * LAYER_U + mp * 4 + (OUT_U0 + q + 2), q % 2,
                                 L * (LAYER_U // 2 * 16) + mp * 32 + ((OUT_U0 + q + 2) // 2 * 16 + 16))
                        if q % 2:
                            m = q // 2
                            act.wait_ge(filled, L * LAYER_F + mp * 2 + (OUT_U0 + m + 1))
                            act.wait_ge(mix_added, L * KT + mp * 2 + (m + 1))
                            fn(MIX[:, bass.ds((mp * 2 + m) * T, T)], MAIN[m][:, 0:T], ACT.Copy)
                            fn(MSQ[m][:, :], MAIN[m][:, 0:T], ACT.Square).then_inc(mix_sq, 1)
                            act.drain().then_inc(bank_free[m], 1)
                act.wait_ge(p_in, L * 16 + 16)
                fn(YHI[:, 0:2 * T], PRAW, ACT.Copy).then_inc(p_hi, 1)
                rsqrt(T0, T0.in_post(L, 0), 1.0 / DM, C_EPS)
                act.wait_ge(p_lo, L + 1)
                for m in range(KT + 2):
                    if m >= 2:
                        i = m - 2
                        act.wait_ge(x_mid, L * KT + (i + 1))
                        fn(HHI[:, i * T:(i + 1) * T], YX[:, i * T:(i + 1) * T], ACT.Copy).then_inc(x_hi, 1)
                    if m >= KT:
                        continue
                    if m == 8:
                        split_hi(unit(L, GATE_U0), 0, landed(L, GATE_U0))
                    act.wait_ge(filled, L * LAYER_F + (OUT_U0 + KT + m + 1))
                    c0 = (KT + m) * T
                    fn(YX[:, c0:c0 + T], MAIN[m % 2][:, 0:T], ACT.Copy, scale=0.5).then_inc(bank_free[m % 2], 1)
                split_hi(unit(L, GATE_U0 + 1), 1, landed(L, GATE_U0 + 1))
                with act.Fori(0, KT // 2 - 1) as mp:
                    for m in range(2):
                        act.wait_ge(filled, L * LAYER_F + mp * 2 + (OUT_U0 + 2 * KT + m + 1))
                        split_hi(L * LAYER_U + mp * 2 + (GATE_U0 + m + 2), m,
                                 L * (LAYER_U // 2 * 16) + mp * 16 + ((GATE_U0 + m + 2) // 2 * 16 + 16))
                        act.wait_ge(th_used, L * 72 + mp * 2 + (56 + m + 1))
                        fn(TH[m][:, 0:T], MAIN[m][:, 0:T], ACT.Tanh, scale=0.5).then_inc(th_ready, 1)
                for m in range(2):
                    act.wait_ge(filled, L * LAYER_F + (OUT_U0 + 3 * KT - 2 + m + 1))
                    act.wait_ge(th_used, L * 72 + (70 + m + 1))
                    fn(TH[m][:, 0:T], MAIN[m][:, 0:T], ACT.Tanh, scale=0.5).then_inc(th_ready, 1)
            act.wait_ge(old_copied, 32)
            act.wait_ge(k_stored, DEPTH * 32)
            act.wait_ge(v_stored, DEPTH * 128)
            act.wait_ge(csout_stored, DEPTH * G * 16 + 16)
            act.wait_ge(scout_stored, DEPTH * G * 16 + 16)
            act.wait_ge(s1_stored, DEPTH * G * 16 + 16)
            act.wait_ge(state_stored, DEPTH * G * 16 + 16)

        @block.vector
        def _(dve):
            tt, ts, stt = nc.vector.tensor_tensor, nc.vector.tensor_scalar, nc.vector.scalar_tensor_tensor

            def lo(dst, raw, hi):
                return tt(dst, raw, hi.bitcast(F32), ALU.subtract)

            def split_lo(u, s, k=None):
                n = (KT - pool_blocks(k)) * BLK
                dve.wait_ge(hi_done, u + 1)
                lo(WLO[s][:, 0:n], RAW[s][:, 0:n], WHI[s][:, 0:n]).then_inc(lo_done, 1)

            def rsqrt(bank, n, inv, eps):
                dve.wait_ge(norm_ln, n)
                ts(RV[:, :], bank.t[:, 0:T], inv, eps, ALU.mult, ALU.add).then_inc(bank.free, 1)
                tt(RA[:, :], RS[:, :], RS[:, :], ALU.mult)
                dve.drain()
                tt(RA[:, :], RA[:, :], RV[:, :], ALU.mult)
                dve.drain()
                ts(RA[:, :], RA[:, :], -0.5, 1.5, ALU.mult, ALU.add)
                dve.drain()
                tt(RS[:, :], RS[:, :], RA[:, :], ALU.mult)
                dve.drain()

            def rotate(dst, swapped, main, b):
                tt(dst, main[:, 0:T], COS, ALU.mult).then_inc(bank_free[b], 1)
                tt(swapped, swapped, SIN, ALU.mult)
                dve.drain()
                return tt(dst, dst, swapped, ALU.add)

            dve.wait_ge(x_first, 16)
            dve.sem_inc(x_final, 1)
            dve.sem_inc(th_used, 2)
            dve.sem_inc(ssd_done, 1)
            dve.sem_inc(sc_done, 1)
            dve.sem_inc(xc_ready, 2)
            dve.sem_inc(y_used, 1)
            dve.sem_inc(smp_state, 1)
            for f in FB:
                nc.vector.memset(f[:, 0:3], 0.0)
            dve.wait_ge(const_in, 16)
            with dve.Fori(0, DEPTH) as L:
                for j in range(1, 4):
                    dve.wait_ge(xsq_done, L * 4 + (j + 1))
                    last = tt(XSQ[:, 0:4 * T], XSQ[:, 0:4 * T], XSQ[:, 4 * j * T:4 * (j + 1) * T], ALU.add)
                    if j < 3:
                        dve.drain()
                last.then_inc(xsq_sum, 1)
                split_lo(unit(L, 0), 0)
                rsqrt(T0, L * 6 + 1, 1.0 / DM, EPS)
                dve.wait_ge(layer_in, L * 64 + 64)
                for i in range(KT):
                    f = HF[i % 4]
                    if i >= 4:
                        dve.wait_ge(h_lo, L * KT + (i - 3))
                    stt(f, YX[:, i * T:(i + 1) * T], NRM[:, i:i + 1], RS[:, :], ALU.mult, ALU.mult).then_inc(h_scaled, 1)
                dve.wait_ge(dt_hi, L + 1)
                lo(YLO[:, 0:UNIT], DTRAW, YHI[:, 0:UNIT]).then_inc(dt_lo, 1)
                split_lo(unit(L, 1), 1)

                def step_sizes():
                    dve.wait_ge(T1.full, T1.in_pre(L, 0))
                    ts(DTR[0:32, :], T1.t[0:32, 0:T], DTP[0:32, 0:1], None, ALU.add).then_inc(T1.free, 1)
                    dve.drain()
                    stt(DTU[0:32, :], DTR[0:32, :], -1.0, DTR[0:32, :], ALU.mult, ALU.max).then_inc(dt_abs, 1)
                    dve.wait_ge(dt_exp, L + 1)
                    ts(DTU[0:32, :], DTE[0:32, :], 1.0, None, ALU.add).then_inc(dt_u, 1)
                    dve.drain()
                    ts(W0[0:32, :], DTU[0:32, :], -1.0, None, ALU.add)
                    dve.drain()
                    tt(W0[0:32, :], DTE[0:32, :], W0[0:32, :], ALU.subtract)
                    dve.drain()
                    dve.wait_ge(dt_ln, L + 1)
                    tt(DTC[0:32, :], DTC[0:32, :], W0[0:32, :], ALU.add)
                    dve.drain()
                    stt(DT0[0:32, :], DTR[0:32, :], 0.0, DTC[0:32, :], ALU.max, ALU.add)
                    dve.drain()
                    ts(DTR[0:32, :], DT0[0:32, :], DTP[0:32, 2:3], -1.0, ALU.mult, ALU.mult)
                    dve.drain()
                    nc.vector.tensor_tensor_scan(AC0[0:32, :], RST[0:32, :], DTR[0:32, :], 0.0, ALU.mult, ALU.add)
                    dve.drain()
                    for c in range(2):
                        ts(DTE[0:32, c * P:(c + 1) * P], AC0[0:32, c * P:(c + 1) * P], AC0[0:32, (c + 1) * P - 1:(c + 1) * P],
                           None, ALU.subtract)
                    ac = smp(AC0[0:32, NPR:T])
                    tt(smp(DTE[0:32, NPR:T]), ac, ac[:, :, NS - 1:NS].to_broadcast([32, NB, NS]), ALU.subtract).then_inc(dt_ac, 1)

                for k in range(PRE_U):
                    split_lo(unit(L, k + 2), k % 2)
                    if k < 2:
                        dve.wait_ge(k_swapped, L * 2 + (k + 1))
                        rotate(KTT[:, k, :], KSW[:, k, :], MAIN[k], k).then_inc(k_ready, 1)
                    if k == 0:
                        step_sizes()
                    if k == 1:
                        dve.wait_ge(dt_wexp, L + 1)
                        tt(W0[0:32, :], W0[0:32, :], DT0[0:32, :], ALU.mult).then_inc(dt_ready, 1)

                with dve.Fori(0, G) as g:
                    th_n = [0]

                    def gate(dst, main, b):
                        n = th_n[0]
                        th_n[0] += 1
                        dve.wait_ge(th_ready, L * 72 + g * 14 + (n + 1))
                        stt(dst, TH[n % 2][:, 0:T], 1.0, main[:, 0:T], ALU.add, ALU.mult).then_inc(th_used, 1)
                        return dve.drain().then_inc(bank_free[b], 1)

                    def mask_max(j):
                        bk = (A0, A1, T0, T1)[j]
                        dve.wait_ge(bk.full, bk.in_grp(L, g, 0))
                        tt(PR[:, j, :], bk.t[:, 0:3 * P], MSK[:, 0:3 * P], ALU.add).then_inc(bk.free, 1)
                        dve.drain()
                        nc.vector.reduce_max(MX[:, 2 * j:2 * j + 1], PR[:, j, 0:P], AX.X)
                        nc.vector.reduce_max(MX[:, 2 * j + 1:2 * j + 2], PR[:, j, P:3 * P], AX.X)

                    def row_stats(c0, c1, sink):
                        n = c1 - c0
                        dve.drain()
                        stt(NM[:, c0:c1].rearrange("p (j c) -> p j c", c=n if n == 1 else 2),
                            MX[:, c0:c1].rearrange("p (j c) -> p j c", c=n if n == 1 else 2), HD ** -0.5, sink, ALU.mult, ALU.max)
                        dve.drain()
                        ts(NM[:, c0:c1], NM[:, c0:c1], -1.0, None, ALU.mult)
                        dve.drain()
                        return tt(MX[:, c0:c1].rearrange("p (j c) -> p j c", c=n if n == 1 else 2),
                                  NM[:, c0:c1].rearrange("p (j c) -> p j c", c=n if n == 1 else 2), sink, ALU.add)

                    def half_over_den(c0, c1):
                        dve.drain()
                        tt(DEN[:, c0:c1], DEN[:, c0:c1], MX[:, c0:c1], ALU.add)
                        dve.drain()
                        nc.vector.reciprocal(DEN[:, c0:c1], DEN[:, c0:c1])
                        dve.drain()

                    def gated_y(i):
                        x = XC[:, 2 + i, :]
                        dve.wait_ge(YB.full, YB.in_grp(L, g, 3 + i))
                        stt(YT, x, GP[:, G_D + i:G_D + i + 1], YB.t[:, 0:T], ALU.mult, ALU.add).then_inc(YB.free, 1)
                        dve.wait_ge(YO.full, YO.in_grp(L, g, 3 + i))
                        tt(YS[:, 0:P + NSM], YO.t[:, 0:P + NSM], EA[i % 3], ALU.mult).then_inc(YO.free, 1)
                        dve.drain().then_inc(y_used, 1)
                        tt(YT[:, P:T], YT[:, P:T], YS[:, 0:P + NSM], ALU.add)
                        dve.drain()
                        tt(Z2[:, i, :], YT, Z2[:, i, :], ALU.mult).then_inc(y_gated, 1)
                        dve.drain()

                    for k in range(GRP_U):
                        b = k % 2
                        main = MAIN[b]
                        if k < 2:
                            dve.wait_ge(q_swapped, it(L, g, 2, k))
                            rotate(Q[:, k, :], QS[:, k, :], main, b).then_inc(q_ready, 1)
                        if k in (2, 3):
                            gate(G2[:, k - 2, :], main, b)
                        if k in (6, 20):
                            gate(SG2, main, b)
                        if 14 <= k < 18:
                            gate(Z2[:, k - 14, :], main, b)
                        if k in (5, 19):
                            i = k // 19
                            dve.wait_ge(c_ready, it(L, g, 2, i))
                            dve.wait_ge(filled, gfill(L, g, k))
                            tt(USC[:, 2:2 + NPR], main[:, 0:NPR], SCB[:, 0:NPR], ALU.mult)
                            tt(fsmp(USC, 2)[:, :, 2:6], smp(main[:, NPR:T]), smp(SCB[:, NPR:T]), ALU.mult).then_inc(u_ready, 1)
                            dve.drain().then_inc(bank_free[b], 1)
                        if k in (7, 21):
                            i = k // 21
                            dve.wait_ge(filled, gfill(L, g, k))
                            cs = CSUM[:, NPR:NPR + 48].rearrange("p (b t) -> p b t", t=6)[:, :, 2:6]
                            stt(SBB[:, 0:NPR], CSUM[:, 0:NPR], 0.5, main[:, 0:NPR], ALU.mult, ALU.mult)
                            stt(smp(SBB[:, NPR:T]), cs, 0.5, smp(main[:, NPR:T]), ALU.mult, ALU.mult)
                            dve.drain().then_inc(bank_free[b], 1)
                            if k == 7:
                                dve.wait_ge(x_stored, L * 16 + 16)
                                dve.wait_ge(x_slab0, 16)
                            tt(YX[:, bass.ds((g * 2 + 24 + i) * T, T)], SBB, SG2, ALU.mult).then_inc(sc_done, 1)
                        if 8 <= k < 14:
                            t = k - 8
                            f, s = FB[t % 2], AB[t % 2]
                            dve.wait_ge(tap_done, it(L, g, 6, t))
                            for j in range(1, 4):
                                last = stt(s[:, :], f[:, j:j + CW], GP[:, G_CW + 4 * t + j:G_CW + 4 * t + j + 1], s[:, :],
                                           ALU.mult, ALU.add)
                                if j < 3:
                                    dve.drain()
                            last.then_inc(conv_sum, 1)
                        split_lo(gunit(L, g, k + 2), b, k)
                        if k in (3, 4):
                            if k == 3:
                                dve.wait_ge(msk_in, L * (G * 16) + g * 16 + 16)
                                dve.wait_ge(gp_in, L * (G * 16) + g * 16 + 16)
                            mask_max(2 * (k - 3))
                            mask_max(2 * (k - 3) + 1)
                        if k == 4:
                            row_stats(0, 8, GP[:, G_SK:G_SK + 4].unsqueeze(2).to_broadcast([P, 4, 2])).then_inc(att_max, 1)
                        if k == 5:
                            for s, bk, n in ((0, YB, 0), (1, YO, 0), (2, A0, 1)):
                                w = 512 if s < 2 else NSM
                                dve.wait_ge(bk.full, bk.in_grp(L, g, n))
                                if s == 0:
                                    dve.wait_ge(state_stored, L * (G * 16) + g * 16 + 16)
                                tt(PS[:, s * 512:s * 512 + w], bk.t[:, 0:w], MSK[:, 3 * P + s * 512:3 * P + s * 512 + w],
                                   ALU.add).then_inc(bk.free, 1)
                            dve.drain()
                            nc.vector.reduce_max(MX[:, 8:9], PS, AX.X)
                            row_stats(8, 9, GP[:, G_SKS:G_SKS + 1].unsqueeze(2)).then_inc(smp_max, 1)
                        if k == 6:
                            wait_alone(dve, "dve", att_exp, it(L, g))
                            half_over_den(0, 8)
                            for j in range(4):
                                for c, (c0, c1) in enumerate(((0, P), (P, 3 * P))):
                                    last = ts(PR[:, j, c0:c1], PR[:, j, c0:c1], DEN[:, 2 * j + c:2 * j + c + 1], 0.5,
                                              ALU.mult, ALU.mult)
                            last.then_inc(att_prob, 1)
                        if k == 7:
                            wait_alone(dve, "dve", smp_exp, it(L, g))
                            half_over_den(8, 9)
                            ts(PS, PS, DEN[:, 8:9], 0.5, ALU.mult, ALU.mult).then_inc(smp_prob, 1)
                        if k in (6, 20):
                            i = k // 20
                            dve.wait_ge(stap_done, it(L, g, 2, i))
                            for j in (1, 2):
                                stt(CSUM, USC[:, j:j + SW], GP[:, G_SW + 3 * i + j:G_SW + 3 * i + j + 1], CSUM, ALU.mult, ALU.add)
                                dve.drain()
                        if 8 <= k < 14:
                            if t == 0:
                                dve.wait_ge(tok_ready, L + 1)
                                src = TOK[:, :].rearrange("p (v h) -> p v h", h=32)[:, :, bass.ds(g * HG, HG)]
                                dst = TG[:, :].rearrange("p (v h) -> p v h", h=HG)
                                nc.vector.tensor_copy(dst[:, 0:6, :], src[:, 0:6, :])
                                nc.vector.tensor_copy(dst[0:NSM, 6:9, :], src[0:NSM, 6:9, :]).then_inc(tg_ready, 1)
                            n = th_n[0]
                            th_n[0] += 1
                            dve.wait_ge(th_ready, L * 72 + g * 14 + (n + 1))
                            th = TH[n % 2]
                            stt(XC[:, t, 0:NPR], th[:, 0:NPR], 1.0, AB[t % 2][:, 0:NPR], ALU.add, ALU.mult)
                            ths = th[:, NPR:NPR + 56].rearrange("p (b t) -> p b t", t=7)[:, :, 3:7]
                            ss = AB[t % 2][:, NPR:NPR + 56].rearrange("p (b t) -> p b t", t=7)[:, :, 3:7]
                            stt(smp(XC[:, t, NPR:T]), ths, 1.0, ss, ALU.add, ALU.mult).then_inc(th_used, 1)
                            dve.drain()
                            ts(XC[:, t, :], XC[:, t, :], 0.5, None, ALU.mult).then_inc(xc_ready, 1)
                        if k == 10:
                            for a, (bk, n) in enumerate(((T1, 2), (A0, 3))):
                                dve.wait_ge(bk.full, bk.in_grp(L, g, n))
                                tt(YX[:, bass.ds((g * 2 + KT + a) * T, NPR)], bk.t[:, 0:NPR], G2[:, a, 0:NPR], ALU.mult).then_inc(bk.free, 1)
                        if k == 11:
                            dve.wait_ge(os_ready, it(L, g))
                            for a in range(2):
                                last = tt(YX[:, bass.ds((g * 2 + KT + a) * T + NPR, NSM)], OS[:, a, :], G2[:, a, NPR:T], ALU.mult)
                            last.then_inc(att_done, 1)
                            dve.drain()
                            dve.wait_ge(YO.full, YO.in_grp(L, g, 2))
                            tt(CBM[:, 0:NPR], YO.t[:, 0:NPR], TRI[:, 0:NPR], ALU.mult)
                            tt(CBM[0:NSM, NPR:T], YO.t[0:NSM, NPR:T], TRI[0:NSM, NPR:T], ALU.mult).then_inc(YO.free, 1)
                        if k == 12:
                            dve.wait_ge(bt_ready, it(L, g))
                            lo(B3[2 * NSM:3 * NSM, :], YB.t[0:NSM, 2 * P:3 * P], B3[0:NSM, :]).then_inc(b3_ready, 1)
                            dve.drain().then_inc(YB.free, 1)
                        if k in (14, 15):
                            for c in (0, 1) if k == 14 else (2,):
                                bk, n = ((T0, 3), (T1, 3), (T0, 4))[c]
                                w = P if c < 2 else NSM
                                dve.wait_ge(bk.full, bk.in_grp(L, g, n))
                                src = bk.t[0:w, :].rearrange("p (h d) -> p h d", d=HD)
                                for dst, v in ((XDT, 0), (XW, 2)):
                                    last = tt(dst[0:w, c, :].rearrange("p (h d) -> p h d", d=HD), src,
                                              TGV[0:w, c, v, :].unsqueeze(2).to_broadcast([w, HG, HD]), ALU.mult)
                                last.then_inc(bk.free, 1)
                                dve.drain().then_inc(xt_ready, 1)
                        if 15 <= k < 19:
                            for h in (2 * (k - 15), 2 * (k - 15) + 1):
                                m = MH[h % 6]
                                dve.wait_ge(decay_ready, it(L, g, HG, h))
                                tt(m[:, 0:NPR], m[:, 0:NPR], CBM[:, 0:NPR], ALU.mult)
                                tt(m[0:NSM, NPR:T], m[0:NSM, NPR:T], CBM[0:NSM, NPR:T], ALU.mult).then_inc(mh_ready, 1)
                        if k == 17:
                            dve.wait_ge(x3_hi, it(L, g))
                            lo(X3[NSM:2 * NSM, :], XW[0:NSM, 2, :], X3[0:NSM, :]).then_inc(x3_ready, 1)
                        if 16 <= k < 20:
                            gated_y(k - 16)
                        if k == 18:
                            dve.wait_ge(T0.full, T0.in_grp(L, g, 5))
                            dve.wait_ge(s1_stored, L * (G * 16) + g * 16 + 16)
                            tt(S1.rearrange("p (h d) -> p h d", d=HD), S0.rearrange("p (h d) -> p h d", d=HD),
                               DEC[:, :, 0:1].to_broadcast([P, HG, HD]), ALU.mult)
                            dve.drain()
                            tt(S1, T0.t[:, :], S1, ALU.add).then_inc(T0.free, 1)
                            dve.drain().then_inc(s1_ready, 1)
                        if k >= 19:
                            for b_, name, n in NEW_STATES[k]:
                                bk = BANKS[name]
                                st = S0T[:, b_ * GW:(b_ + 1) * GW]
                                dve.wait_ge(bk.full, bk.in_grp(L, g, n))
                                stv = st.rearrange("p (h d) -> p h d", d=HD)
                                tt(stv, stv, DEC[:, :, 1 + b_:2 + b_].to_broadcast([P, HG, HD]), ALU.mult)
                                dve.drain()
                                tt(st, bk.t[:, :], st, ALU.add).then_inc(bk.free, 1)
                    dve.drain().then_inc(smp_state, 1)
                    rsqrt(T1, L * 6 + g + 2, 1.0 / GW, 4 * EPS)
                    for i in range(4):
                        stt(YX[:, bass.ds((g * 4 + i) * T, T)], Z2[:, i, :], GP[:, G_NW + i:G_NW + i + 1], RS[:, :], ALU.mult, ALU.mult)
                    dve.drain().then_inc(ssd_done, 1)

                for j in range(8):
                    hi, lo_ = ((HHI, HLO) if j < 4 else (YHI, YLO))
                    c0, y0 = 4 * (j % 4) * T, ((KT if j < 4 else 0) + 4 * (j % 4)) * T
                    dve.wait_ge(y_hi, L * 8 + (j + 1))
                    lo(lo_[:, c0:c0 + 4 * T], YX[:, y0:y0 + 4 * T], hi[:, c0:c0 + 4 * T]).then_inc(y_lo, 1)
                with dve.Fori(0, KT // 2) as mp:
                    for q in range(4):
                        split_lo(L * LAYER_U + mp * 4 + (OUT_U0 + q + 2), q % 2)
                dve.wait_ge(p_hi, L + 1)
                lo(YLO[:, 0:2 * T], PRAW, YHI[:, 0:2 * T]).then_inc(p_lo, 1)
                rsqrt(T0, L * 6 + 6, 1.0 / DM, EPS)
                dve.wait_ge(xres_in, L * 16 + 16)
                for i in range(KT):
                    if i == 8:
                        split_lo(unit(L, GATE_U0), 0)
                    stt(MIX[:, i * T:(i + 1) * T], MIX[:, i * T:(i + 1) * T], NRM[:, KT + i:KT + i + 1], RS[:, :], ALU.mult, ALU.mult)
                    dve.drain()
                    x = YX[:, i * T:(i + 1) * T]
                    tt(x, x, MIX[:, i * T:(i + 1) * T], ALU.add).then_inc(x_mid, 1)
                split_lo(unit(L, GATE_U0 + 1), 1)

                def add_gated(mp, m):
                    dve.wait_ge(th_ready, L * 72 + mp * 2 + (56 + m + 1))
                    stt(RA[:, :], TH[m][:, 0:T], 1.0, YX[:, bass.ds((mp * 2 + KT + m) * T, T)], ALU.add, ALU.mult).then_inc(th_used, 1)
                    dve.drain().then_inc(bank_free[m], 1)
                    x = YX[:, bass.ds((mp * 2 + m) * T, T)]
                    tt(x, x, RA[:, :], ALU.add)
                    dve.drain()

                wait_alone(dve, "dve", x_lo, (L + 1) * KT)
                with dve.Fori(0, KT // 2 - 1) as mp:
                    for m in range(2):
                        split_lo(L * LAYER_U + mp * 2 + (GATE_U0 + m + 2), m)
                        add_gated(mp, m)
                for m in range(2):
                    dve.wait_ge(th_ready, L * 72 + (70 + m + 1))
                    e0, x_0 = (2 * KT - 2 + m) * T, (KT - 2 + m) * T
                    stt(RA[:, :], TH[m][:, 0:T], 1.0, YX[:, e0:e0 + T], ALU.add, ALU.mult).then_inc(th_used, 1)
                    dve.drain().then_inc(bank_free[m], 1)
                    tt(YX[:, x_0:x_0 + T], YX[:, x_0:x_0 + T], RA[:, :], ALU.add)
                    last = dve.drain()
                last.then_inc(x_final, 1)

        @block.gpsimd
        def _(pool):
            tt = nc.gpsimd.tensor_tensor

            def lo(dst, raw, hi):
                return tt(dst, raw, hi.bitcast(F32), ALU.subtract)

            def split_lo(u, s, k=None):
                n = (KT - pool_blocks(k)) * BLK
                pool.wait_ge(hi_done, u + 1)
                lo(WLO[s][:, n:UNIT], RAW[s][:, n:UNIT], WHI[s][:, n:UNIT]).then_inc(lop_done, 1)

            pool.sem_inc(conv_saved, 2)
            pool.sem_inc(sc_saved, 1)
            pool.sem_inc(x_stored, 16)
            pool.sem_inc(mix_added, 2)
            pool.sem_inc(y_sq, 1)
            pool.wait_ge(const_in, 16)
            with pool.Fori(0, DEPTH) as L:
                split_lo(unit(L, 0), 0)
                for i in range(KT):
                    pool.wait_ge(h_hi, L * KT + (i + 1))
                    lo(HLO[:, i * T:(i + 1) * T], HF[i % 4], HHI[:, i * T:(i + 1) * T]).then_inc(h_lo, 1)
                split_lo(unit(L, 1), 1)
                for k in range(PRE_U):
                    split_lo(unit(L, k + 2), k % 2)
                with pool.Fori(0, G) as g:
                    for k in range(GRP_U):
                        split_lo(gunit(L, g, k + 2), k % 2, k)
                        if 8 <= k < 14:
                            t = k - 8
                            f = FB[t % 2]
                            if t == 0:
                                pool.wait_ge(csout_stored, L * (G * 16) + g * 16 + 16)
                            wait_alone(pool, "pool", tap_done, it(L, g, 6, t))
                            nc.gpsimd.tensor_copy(CSO[:, t * 27:t * 27 + 3], f[:, NPR:NPR + 3])
                            nc.gpsimd.tensor_copy(smp(CSO[:, t * 27 + 3:(t + 1) * 27], 3), fsmp(f, 3)[:, :, 4:7]).then_inc(conv_saved, 1)
                        if k == 13:
                            pool.wait_ge(b3_ready, it(L, g))
                            w = 3 * NSM
                            tt(BM3[0:w, :, :], B3[0:w, :].bitcast(F32).unsqueeze(1).to_broadcast([w, NB, P]),
                               CST[0:w, C_SEQ:C_SEQ + NB].unsqueeze(2).to_broadcast([w, NB, P]), ALU.mult).then_inc(bm_ready, 1)
                        if k in (6, 20):
                            i = k // 20
                            if i == 0:
                                pool.wait_ge(scout_stored, L * (G * 16) + g * 16 + 16)
                            wait_alone(pool, "pool", u_ready, it(L, g, 2, i))
                            nc.gpsimd.tensor_copy(SCO[:, i * 18:i * 18 + 2], USC[:, NPR:NPR + 2])
                            nc.gpsimd.tensor_copy(smp(SCO[:, i * 18 + 2:(i + 1) * 18], 2), fsmp(USC, 2)[:, :, 4:6]).then_inc(sc_saved, 1)
                        if 17 <= k < 21:
                            i = k - 17
                            pool.wait_ge(y_gated, it(L, g, 4, i))
                            if i == 0:
                                tt(SQ[:, :], Z2[:, 0, :], Z2[:, 0, :], ALU.mult)
                            else:
                                tt(SQI[:, :], Z2[:, i, :], Z2[:, i, :], ALU.mult)
                                pool.drain()
                                tt(SQ[:, :], SQ[:, :], SQI[:, :], ALU.add)
                            if i < 3:
                                pool.drain()
                            else:
                                pool.drain().then_inc(y_sq, 1)
                wait_alone(pool, "pool", ssd_done, L * G + (G + 1))
                nc.gpsimd.memset(SQ[:, :], 0.0)
                pool.drain()
                with pool.Fori(0, KT // 2) as mp:
                    for q in range(4):
                        split_lo(L * LAYER_U + mp * 4 + (OUT_U0 + q + 2), q % 2)
                        if q % 2:
                            m = q // 2
                            pool.wait_ge(mix_sq, L * KT + mp * 2 + (m + 1))
                            tt(SQ[:, :], SQ[:, :], MSQ[m][:, :], ALU.add).then_inc(mix_added, 1)
                            pool.drain()
                split_lo(unit(L, GATE_U0), 0)
                for i in range(KT):
                    pool.wait_ge(x_hi, L * KT + (i + 1))
                    lo(HLO[:, i * T:(i + 1) * T], YX[:, i * T:(i + 1) * T], HHI[:, i * T:(i + 1) * T]).then_inc(x_lo, 1)
                split_lo(unit(L, GATE_U0 + 1), 1)
                with pool.Fori(0, KT // 2 - 1) as mp:
                    for m in range(2):
                        split_lo(L * LAYER_U + mp * 2 + (GATE_U0 + m + 2), m)


_INS = ["wts", "wdt", "x0", "p_t", "npre", "npost", "gpar", "dtpar", "s0_t", "kc_t", "vc_t", "cs_in", "sc_in",
        "consts", "masks", "resets"]
_OUTS = [("xs", (DEPTH + 1, P, KT * T)), ("kout", (DEPTH, G, HD, T)), ("vout", (DEPTH, G, T, HD)),
         ("kold", (DEPTH * G * HD, NB, P - NS)), ("vold", (DEPTH * G, P - NS, NB * HD)),
         ("conv_out", (DEPTH, G, P, 6 * 27)), ("scv_out", (DEPTH, G, P, 2 * 18)),
         ("ssm_p", (DEPTH, G, P, GW)), ("ssm_s", (DEPTH, G, P, NB * GW))]


def shape_constants():
    import numpy as np

    f = np.float32
    half = HD // 2
    inv = np.exp(f(-np.log(10000.0)) * np.arange(half, dtype=f) * f(2.0 / HD))
    pos = np.concatenate([np.arange(NPR), np.tile(1024 + np.arange(NS), NB)]).astype(f)
    ang = pos[None, :] * inv[np.arange(P) % half][:, None]
    sign = np.where(np.arange(P) % HD < half, -1.0, 1.0).astype(f)[:, None]
    c = np.zeros((P, NCONST), f)
    c[:, C_COS:C_COS + T] = np.cos(ang)
    c[:, C_SIN:C_SIN + T] = np.sin(ang) * sign
    c[:, C_ID:C_ID + P] = np.eye(P)
    s, l = np.arange(P)[:, None], np.arange(P)[None, :]
    for n in range(2):
        c[:, C_TRI + n * P:C_TRI + (n + 1) * P] = s <= l
    c[:NSM, C_TRI + NPR:C_TRI + T] = ((s <= l) & (s // NS == l // NS))[:NSM, :NSM]
    c[:, C_ONE:C_ONE + P] = 1.0
    c[:3 * NSM, C_SEQ:C_SEQ + NB] = np.arange(3 * NSM)[:, None] % NSM // NS == np.arange(NB)[None, :]
    c[:, C_EPS], c[:, C_EPS + 1] = EPS, 4 * EPS
    m = np.zeros((P, NMASK), f)
    t = np.arange(P)[:, None]
    key = np.arange(2 * P)[None, :]
    m[:, 0:P] = np.where(key[:, :P] <= t, 0, -1e30)
    m[:, P:3 * P] = np.where((key <= P + t) & (key > t), 0, -1e30)
    b, tok = (t // NS) % NB, t % NS
    col = np.arange(NB * P)[None, :]
    m[:, 3 * P:3 * P + NB * P] = np.where((col // P == b) & (col % P > tok), 0, -1e30)
    new = np.arange(NSM)[None, :]
    m[:, 3 * P + NB * P:] = np.where((new // NS == b) & (new % NS <= tok), 0, -1e30)
    r = np.ones((32, T), f)
    r[:, [0, P]] = 0
    r[:, NPR::NS] = 0
    return c, m, r


def kernel(**inputs):
    import concourse.bacc as _bacc
    import numpy as np
    from concourse.bass_utils import run_bass_kernel_spmd as _run

    i = {k: np.asarray(v) for k, v in inputs.items()}
    D = DEPTH

    z0, xbc0 = 0, 2048
    x_0, b_0, c_0 = xbc0, xbc0 + 2048, xbc0 + 2048 + 512
    dt0 = xbc0 + 3072
    q0 = dt0 + 32
    k0, v0 = q0 + 1024, q0 + 1024 + 256
    ga0 = v0 + 256
    sb0 = ga0 + 1024
    scc0, sh0, sg0 = sb0 + 1024, sb0 + 2048, sb0 + 3072
    starts = [k0, k0 + P, v0, v0 + P]
    for g in range(G):
        starts += [q0 + g * 256, q0 + g * 256 + P, ga0 + g * 256, ga0 + g * 256 + P]
        short = [[w + (2 * g + n) * P for w in (scc0, sh0, sg0, sb0)] for n in range(2)]
        starts += short[0] + [b_0 + g * P, c_0 + g * P] + [x_0 + g * 512 + n * P for n in range(4)]
        starts += [z0 + g * 512 + n * P for n in range(4)] + short[1]
    w_in, w_out, ple, gate = i["w_in"], i["w_out"], i["ple_proj"], i["ple_gate"]
    wts = np.empty((D, LAYER_U, P, KT, P), np.float32)
    for u, c in enumerate(starts):
        wts[:, u] = w_in[:, :, c:c + P].reshape(D, KT, P, P).transpose(0, 2, 1, 3)
    for m in range(KT):
        w = w_out[:, :, m * P:(m + 1) * P].reshape(D, 2, KT, P, P).transpose(0, 1, 3, 2, 4)
        wts[:, OUT_U0 + 2 * m] = w[:, 1]
        wts[:, OUT_U0 + 2 * m + 1] = w[:, 0]
        wts[:, GATE_U0 + m] = gate[:, :, m * P:(m + 1) * P].reshape(D, KT, P, P).transpose(0, 2, 1, 3)
    pl = ple.reshape(D, 2, P, KT, P).transpose(0, 2, 3, 1, 4).reshape(D, P, 2, KT, P)
    wts[:, PLE_U0:PLE_U0 + 2] = pl.transpose(0, 2, 1, 3, 4)
    wdt = np.zeros((D, P, KT, P), np.float32)
    wdt[:, :, :, 0:32] = w_in[:, :, dt0:dt0 + 32].reshape(D, KT, P, 32).transpose(0, 2, 1, 3)

    def tokens(prompt, sample):
        a = np.concatenate([prompt[..., 0, :, :], sample.reshape(*sample.shape[:-3], NSM, sample.shape[-1])], axis=-2)
        n = a.shape[-1] // P
        a = a.reshape(*a.shape[:-1], n, P)
        a = np.moveaxis(a, (-1, -2, -3), (-3, -2, -1))
        return a.reshape(*a.shape[:-2], n * T)

    def conv_groups(w):
        lead = w.shape[:-1]
        x, b, c = w[..., :2048], w[..., 2048:2560], w[..., 2560:]
        return np.concatenate([b.reshape(*lead, G, 1, P), c.reshape(*lead, G, 1, P), x.reshape(*lead, G, 4, P)], axis=-2)

    gpar = np.zeros((D, G, P, NGP), np.float32)
    gpar[..., G_CW:G_CW + 24] = conv_groups(i["ssd_conv_w"]).transpose(0, 2, 4, 3, 1).reshape(D, G, P, 24)
    gpar[..., G_CB:G_CB + 6] = conv_groups(i["ssd_conv_b"]).transpose(0, 1, 3, 2)
    gpar[..., G_D:G_D + 4] = np.repeat(i["ssd_d"].reshape(D, G, 4, 2), HD, axis=3).transpose(0, 1, 3, 2)
    gpar[..., G_NW:G_NW + 4] = i["ssd_norm"].reshape(D, G, 4, P).transpose(0, 1, 3, 2)
    gpar[..., G_SW:G_SW + 6] = i["sc_conv_w"].reshape(D, 3, G, 2, P).transpose(0, 2, 4, 3, 1).reshape(D, G, P, 6)
    sinks = i["attn_sinks"].reshape(D, G, 4)
    gpar[..., G_SK:G_SK + 4] = sinks[:, :, None, :]
    gpar[..., G_SKS] = np.repeat(sinks, NSM, axis=2)
    consts, masks, resets = shape_constants()
    cs = conv_groups(i["state_ssd_conv"])
    sc = i["state_sc_conv"].reshape(D, NB, 2, G, 2, P)
    arrays = {
        "wts": wts.reshape(NUNITS, P, UNIT), "wdt": wdt.reshape(D, P, UNIT),
        "x0": tokens(i["x_prompt"], i["x_sample"]), "p_t": tokens(i["p_prompt"], i["p_sample"]),
        "npre": i["norm_pre"].reshape(D, KT, P).transpose(0, 2, 1), "npost": i["norm_post"].reshape(D, KT, P).transpose(0, 2, 1),
        "gpar": gpar, "dtpar": np.stack([i["ssd_dt_bias"], i["ssd_a_log"]], axis=-1),
        "s0_t": i["state_ssm"].reshape(D, NB, G, HG, HD, NST).transpose(0, 2, 5, 1, 3, 4).reshape(D, G, P, NB * GW),
        "kc_t": i["cache_k"].transpose(0, 3, 4, 1, 2).reshape(D, G, HD, NB * P),
        "vc_t": i["cache_v"].transpose(0, 3, 2, 1, 4).reshape(D, G, P, NB * HD),
        "cs_in": cs.transpose(0, 3, 5, 4, 1, 2).reshape(D, G, P, 6 * 24),
        "sc_in": sc.transpose(0, 3, 5, 4, 1, 2).reshape(D, G, P, 2 * 16),
        "consts": consts, "masks": masks, "resets": resets,
    }
    nc = _bacc.Bacc("TRN2", target_bir_lowering=False, num_devices=1)
    args = []
    for n in _INS:
        arrays[n] = np.ascontiguousarray(arrays[n])
        args.append(nc.dram_tensor(n, arrays[n].shape, F32, kind="ExternalInput").ap())
    for n, shape in _OUTS:
        args.append(nc.dram_tensor(n, shape, F32, kind="ExternalOutput").ap())
    hybrid_step(nc, *args)
    r = _run(nc, [arrays], core_ids=[0])
    o = {n: np.asarray(r.results[0][n]) for n, _ in _OUTS}

    y = o["xs"][DEPTH].reshape(P, KT, T).transpose(2, 1, 0).reshape(T, DM)
    k, v = o["kout"], o["vout"]
    pk = k[..., P:NPR].transpose(0, 3, 1, 2)[:, None]
    pv = v[:, :, P:NPR].transpose(0, 2, 1, 3)[:, None]
    k_new = k[..., NPR:].reshape(D, G, HD, NB, NS).transpose(0, 3, 4, 1, 2)
    v_new = v[:, :, NPR:].reshape(D, G, NB, NS, HD).transpose(0, 2, 3, 1, 4)
    k_old = o["kold"].reshape(D, G, HD, NB, P - NS).transpose(0, 3, 4, 1, 2)
    v_old = o["vold"].reshape(D, G, P - NS, NB, HD).transpose(0, 3, 2, 1, 4)
    co = o["conv_out"].reshape(D, G, P, 6, 9, 3).transpose(0, 4, 5, 1, 3, 2)
    co = np.concatenate([co[..., 2:, :].reshape(D, 9, 3, 2048), co[..., 0, :].reshape(D, 9, 3, 512),
                         co[..., 1, :].reshape(D, 9, 3, 512)], axis=-1)
    so = o["scv_out"].reshape(D, G, P, 2, 9, 2).transpose(0, 4, 5, 1, 3, 2).reshape(D, 9, 2, 1024)
    sp = o["ssm_p"].reshape(D, G, NST, HG, HD).transpose(0, 1, 3, 4, 2).reshape(D, 1, 32, HD, NST)
    ss = o["ssm_s"].reshape(D, G, NST, NB, HG, HD).transpose(0, 3, 1, 4, 5, 2).reshape(D, NB, 32, HD, NST)
    out = (y[None, :NPR], y[NPR:].reshape(NB, NS, DM), co[:, :1], sp, pk, pv, so[:, :1],
           co[:, 1:], ss, np.concatenate([k_old, k_new], axis=2), np.concatenate([v_old, v_new], axis=2), so[:, 1:])
    return tuple(np.ascontiguousarray(a) for a in out)
```

```python
from contextlib import ExitStack

import concourse.bass as bass
from concourse import mybir

F32 = mybir.dt.float32
F32R = mybir.dt.float32r
ALU = mybir.AluOpType
ACT = mybir.ActivationFunctionType
AX = mybir.AxisListType

P = 128
DEPTH = 2
DM = 2048
KT = DM // P
NPR = 256
NB, NS = 8, 4
NSM = NB * NS
T = NPR + NSM
G = 4
HG = 8
HD = 64
NST = 128
GW = HG * HD
EPS = 1e-6
BLK = P
UNIT = KT * BLK

NEW_STATES = {19: ((0, "T1", 5), (1, "A0", 8), (2, "A1", 7)), 20: ((3, "T0", 6), (4, "T1", 6), (5, "A0", 9)),
              21: ((6, "A1", 8), (7, "T0", 7))}

PRE_U = 4
GRP_U = 22
OUT_U0 = PRE_U + G * GRP_U
OUT_U = 2 * KT
PLE_U0 = OUT_U0 + OUT_U
GATE_U0 = PLE_U0 + 2
LAYER_U = GATE_U0 + KT
LAYER_F = OUT_U0 + 3 * KT
NUNITS = DEPTH * LAYER_U

C_COS, C_SIN = 0, T
C_ID = 2 * T
C_TRI = C_ID + P
C_ONE = C_TRI + T
C_SEQ = C_ONE + P
C_SEL = C_SEQ + NB
C_EPS = C_SEL + 32
NCONST = C_EPS + 2
NMASK = 3 * P + NB * P + NSM

G_CW, G_CB = 0, 24
G_D, G_NW = 30, 34
G_SW = 38
G_SK, G_SKS = 44, 48
NGP = 49

FW = 3 + NPR + NB * (3 + NS)
CW = FW - 3
SW_IN = 2 + NPR + NB * (2 + NS)
SW = SW_IN - 2


def hybrid_step(nc, wts, wdt, x0, p_t, npre, npost, gpar, dtpar, s0_t, kc_t, vc_t, cs_in, sc_in, consts, masks, resets,
                xs, kout, vout, kold, vold, conv_out, scv_out, ssm_p, ssm_s):
    ctx = ExitStack()
    with ctx:
        def sem(name):
            return ctx.enter_context(nc.semaphore(name))

        def sb(name, cols, dt=F32):
            return ctx.enter_context(nc.sbuf_tensor(name, [P, cols], dt))

        RAW = [sb(f"raw{i}", UNIT) for i in range(2)]
        WHI = [sb(f"whi{i}", UNIT, F32R) for i in range(2)]
        WLO = [sb(f"wlo{i}", UNIT, F32R) for i in range(2)]
        HHI = sb("h_hi", KT * T, F32R)
        HLO = sb("h_lo", KT * T, F32R)
        YX = sb("y_or_x", 2 * KT * T)
        CST = sb("cst", NCONST)
        GP = sb("gpar_sb", NGP)
        NRM = sb("norm_weights", 2 * KT)
        DTP = sb("dt_params", 4)
        TOK = sb("tok", 288)
        TG = sb("tok_group", 72)
        FB = [sb(f"conv_in{i}", FW) for i in range(2)]
        AB = [sb(f"conv_sum{i}", CW) for i in range(2)]
        TH = [sb(f"tanh{i}", CW) for i in range(2)]
        CSI = sb("conv_state_in", 6 * 24)
        CSO = sb("conv_state_out", 6 * 27)
        SCI = sb("short_state_in", 2 * 16)
        SCO = sb("short_state_out", 2 * 18)
        RS = sb("rs", T)
        RV = sb("rs_v", T)
        RA = sb("rs_a", T)
        SQ = sb("sq", T)
        B3 = sb("b3", P, F32R)
        BM3 = sb("b3_masked", NB * P, F32R)[:, :].rearrange("p (b n) -> p b n", b=NB)
        X3 = sb("x3", GW, F32R)
        ONE = sb("ln_warm", 1)
        AC3 = sb("decay3", T, F32R)
        SEL = sb("select", HG, F32R)
        work = ExitStack()
        WK_N = 15408
        WK = work.enter_context(nc.sbuf_tensor("work", [P, WK_N], F32))
        work.close()
        at = [0]

        def cut(n, restart=None):
            if restart is not None:
                at[0] = restart
            a = WK[:, at[0]:at[0] + n]
            at[0] += n
            assert at[0] <= WK_N, at[0]
            return a

        XC = cut(6 * T).rearrange("p (t n) -> p t n", n=T)
        Z2 = cut(4 * T).rearrange("p (t n) -> p t n", n=T)
        G2 = cut(2 * T).rearrange("p (t n) -> p t n", n=T)
        SCB = cut(T)
        SBB = cut(T)
        SG2 = cut(T)
        USC = FB[0][:, 1:1 + SW_IN]
        CSUM = AB[0][:, 0:SW]
        HEAVY = at[0]
        XDT = cut(3 * GW).rearrange("p (c n) -> p c n", c=3)
        XW = cut(3 * GW).rearrange("p (c n) -> p c n", c=3)
        S1 = XW[:, 0, :]
        BT = cut(2 * P).rearrange("p (c n) -> p c n", c=2)
        CBM = cut(T)
        MH = [cut(T) for _ in range(6)]
        EA = [cut(P + NSM) for _ in range(3)]
        DEC = cut(HG * 9).rearrange("p (h n) -> p h n", n=9)
        S0 = cut(GW)
        YT = cut(T)
        YS = cut(T)
        LATE = at[0]
        S0T = cut(NB * GW)
        Q = cut(2 * T, HEAVY).rearrange("p (t n) -> p t n", n=T)
        QS = cut(2 * T).rearrange("p (t n) -> p t n", n=T)
        QSM = cut(4 * NSM)
        KCUR = cut(T)
        KC = cut(NB * P)
        VC = cut(NB * HD).rearrange("p (b d) -> p b d", d=HD)
        VCUR = cut(3 * HD).rearrange("p (c d) -> p c d", d=HD)
        MSK = cut(NMASK)
        MX = cut(16)
        NM = cut(16)
        DEN = cut(16)
        OS = cut(2 * NSM).rearrange("p (a n) -> p a n", n=NSM)
        PR = cut(4 * 3 * P).rearrange("p (j n) -> p j n", j=4)
        PS = cut(NB * P + NSM)
        PT = cut(4 * 3 * P).rearrange("p (j n) -> p j n", j=4)
        PTS = cut(9 * P)
        XSQ = cut(KT * T, 0)
        DT0 = cut(T, HEAVY + 2400)
        AC0 = cut(T)
        W0 = cut(T)
        DTR = cut(T)
        DTE = cut(T)
        DTU = cut(T)
        DTC = cut(T)
        RST = cut(T)
        HF = [cut(T) for _ in range(6)]
        assert at[0] <= LATE
        KTT = cut(2 * T, LATE).rearrange("p (t n) -> p t n", n=T)
        KSW = cut(2 * T).rearrange("p (t n) -> p t n", n=T)
        VTT = cut(2 * T).rearrange("p (t n) -> p t n", n=T)
        VT = cut(2 * 3 * P).rearrange("p (t n) -> p t n", t=2)
        post = ctx.enter_context(ExitStack())
        YHI = post.enter_context(nc.sbuf_tensor("yssd_hi", [P, KT * T], F32R))
        YLO = post.enter_context(nc.sbuf_tensor("yssd_lo", [P, KT * T], F32R))
        MIX = post.enter_context(nc.sbuf_tensor("mix", [P, KT * T], F32))
        MSQ = [post.enter_context(nc.sbuf_tensor(f"mix_sq{i}", [P, T], F32)) for i in range(2)]
        assert 3 * KT * T + 2 * T <= WK_N and 2 * KT * T + UNIT - KT * T <= HEAVY + 2400
        DTRAW = YX[:, KT * T:KT * T + UNIT]
        PRAW = YX[:, KT * T:KT * T + 2 * T]

        COS, SIN = CST[:, C_COS:C_COS + T], CST[:, C_SIN:C_SIN + T]
        ID, ONES = CST[:, C_ID:C_ID + P], CST[:, C_ONE:C_ONE + P]
        TRI = CST[:, C_TRI:C_TRI + T]
        TGV = TG[:, :].rearrange("p (c v h) -> p c v h", c=3, v=3)

        MAIN = [ctx.enter_context(nc.psum_tensor(f"main{i}", [P, 512], F32)) for i in range(2)]

        class Bank:

            def __init__(self, name, pre, grp, post_):
                self.t = ctx.enter_context(nc.psum_tensor(name, [P, 512], F32))
                self.full, self.free = sem(name + "_full"), sem(name + "_free")
                self.pre, self.grp, self.per = pre, grp, pre + G * grp + post_

            def in_pre(self, L, n):
                return L * self.per + (n + 1)

            def in_grp(self, L, g, n):
                return L * self.per + g * self.grp + (self.pre + n + 1)

            def in_post(self, L, n):
                return L * self.per + (self.pre + G * self.grp + n + 1)

        A0, A1 = Bank("a0", 0, 10, 0), Bank("a1", 0, 9, 0)
        YB, YO = Bank("yb", 0, 7, 0), Bank("yo", 0, 7, 0)
        T0, T1 = Bank("t0", 3, 8, 1), Bank("t1", 2, 8, 0)
        BANKS = {"A0": A0, "A1": A1, "T0": T0, "T1": T1}
        SIDE = [A0, A1, YB, YO, T0, T1]

        raw_landed = [sem(f"raw_landed{i}") for i in range(2)]
        hi_done, lo_done, lop_done = sem("hi_done"), sem("lo_done"), sem("lop_done")
        units_used, e_filled = sem("units_used"), sem("e_filled")
        bank_free = [sem(f"main_free{i}") for i in range(2)]
        const_in, layer_in, dtw_in, xres_in, p_in = (sem(n) for n in ("const_in", "layer_in", "dtw_in", "xres_in", "p_in"))
        x_first = [sem(f"x_first{j}") for j in range(4)]
        x_most, x_final, x_stored, x_slab0 = (sem(n) for n in ("x_most", "x_final", "x_stored", "x_slab0"))
        x_out, x_sq, x_added = sem("x_out"), sem("x_sq"), sem("x_added")
        xsq_done, xsq_sum, h_scaled, h_hi, h_lo = (sem(n) for n in ("xsq_done", "xsq_sum", "h_scaled", "h_hi", "h_lo"))
        h_lo_dve = sem("h_lo_dve")
        ac_ready, ac_hi, ac_rest, ac_mid, ac_lo = (sem(n) for n in ("ac_ready", "ac_hi", "ac_rest", "ac_mid", "ac_lo"))
        norm_read, norm_ln = sem("norm_read"), sem("norm_ln")
        dt_hi, dt_lo = sem("dt_hi"), sem("dt_lo")
        dt_abs, dt_exp, dt_u, dt_ln, dt_ac, dt_wexp, dt_ready, tok_ready = (
            sem(n) for n in ("dt_abs", "dt_exp", "dt_u", "dt_ln", "dt_ac", "dt_wexp", "dt_ready", "tok_ready"))
        k_swapped, k_ready, v_ready, v_tok, k_stored, v_stored = (
            sem(n) for n in ("k_swapped", "k_ready", "v_ready", "v_tok", "k_stored", "v_stored"))
        old_copied = sem("old_copied")
        gp_in, att_in, msk_in, sin_in = sem("gp_in"), sem("att_in"), sem("msk_in"), sem("sin_in")
        st_in = [sem(f"st_in{i}") for i in range(4)]
        b3_ready, x3_hi, x3_ready = sem("b3_ready"), sem("x3_hi"), sem("x3_ready")
        q_swapped, q_ready, qsm_ready = sem("q_swapped"), sem("q_ready"), sem("qsm_ready")
        th_ready, th_used = sem("th_ready"), sem("th_used")
        att_max, att_exp, att_prob, smp_max, smp_exp, smp_prob = (
            sem(n) for n in ("att_max", "att_exp", "att_prob", "smp_max", "smp_exp", "smp_prob"))
        pt_ready, pts_ready, os_ready, att_done = (
            sem(n) for n in ("pt_ready", "pts_ready", "os_ready", "att_done"))
        tap_done, conv_sum, xc_ready, conv_saved, csout_stored = (
            sem(n) for n in ("tap_done", "conv_sum", "xc_ready", "conv_saved", "csout_stored"))
        tg_ready, bt_ready, bm_ready, xt_ready = (
            sem(n) for n in ("tg_ready", "bt_ready", "bm_ready", "xt_ready"))
        decay_ready, mh_ready, s0_ready, y_used, y_gated, y_sq = (
            sem(n) for n in ("decay_ready", "mh_ready", "s0_ready", "y_used", "y_gated", "y_sq"))
        s1_ready, smp_state, s1_stored, state_stored, ssd_done = (
            sem(n) for n in ("s1_ready", "smp_state", "s1_stored", "state_stored", "ssd_done"))
        c_ready, u_ready, stap_done, sc_done, sc_saved, scout_stored = (
            sem(n) for n in ("c_ready", "u_ready", "stap_done", "sc_done", "sc_saved", "scout_stored"))
        y_lop = sem("y_lop")
        y_hi, y_lo, mix_sq, mix_added, p_hi, p_lo = (
            sem(n) for n in ("y_hi", "y_lo", "mix_sq", "mix_added", "p_hi", "p_lo"))
        x_mid, x_hi, x_lo = sem("x_mid"), sem("x_hi"), sem("x_lo")

        passed = {e: sem("passed_" + e) for e in ("pe", "dve", "pool")}

        def wait_alone(eng, name, s, v):
            eng.wait_ge(s, v)
            eng.sem_inc(passed[name], 1)

        def unit(L, k):
            return L * LAYER_U + k

        def gunit(L, g, k):
            return L * LAYER_U + g * GRP_U + (PRE_U + k)

        def fill_bank(L, g, k):
            return L * (LAYER_F // 2) + g * (GRP_U // 2) + (PRE_U // 2 + k // 2 + 1)

        def used(u):
            return u + 3

        def it(L, g, per=1, n=0):
            return L * (G * per) + g * per + (n + 1)

        def smp(ap, w=NS):
            return ap.rearrange("p (b t) -> p b t", t=w)

        def fsmp(ap, k):
            return smp(ap[:, k + NPR:k + NPR + NB * (k + NS)], k + NS)

        def pool_blocks(k):
            return 8 if k is None or k < 14 else 16 if k < 21 else 12

        def h_rest(L, i):
            if i % 3 == 2:
                return h_lo_dve, L * (KT // 3) + (i // 3 + 1)
            return h_lo, L * (KT - KT // 3) + (2 * (i // 3) + i % 3 + 1)

        def y_split(j):
            return (4 <= j < 8 or (j >= 8 and j % 2 == 0)), (j % 4 if j < 8 else 4 + (j - 8) // 2)

        def y_pair_at(j):
            c = 2 * (j % 8) * T
            return c, c + (KT * T if j < 8 else 0)

        block = ctx.enter_context(nc.Block())

        @block.sync
        def _(sp):
            def load_unit(u, s):
                for split in (hi_done, lo_done, lop_done):
                    sp.wait_ge(split, u + 1)
                sp.dma_start(RAW[s][:, :], wts[u]).then_inc(raw_landed[s], 16)

            for j in range(4):
                c0 = j * 4 * T
                sp.dma_start(YX[:, c0:c0 + 4 * T], x0[:, c0:c0 + 4 * T]).then_inc(x_first[j], 16)
            sp.dma_start(CST[:, :], consts).then_inc(const_in, 16)
            with sp.Fori(0, DEPTH) as L:
                for k in range(2):
                    load_unit(unit(L, k), k)
                sp.wait_ge(x_final, L + 1)
                sp.dma_start(DTRAW, wdt[L]).then_inc(dtw_in, 16)
                sp.dma_start(NRM[:, 0:KT], npre[L]).then_inc(layer_in, 16)
                sp.dma_start(NRM[:, KT:2 * KT], npost[L]).then_inc(layer_in, 16)
                sp.dma_start(DTP[0:32, 0:2], dtpar[L]).then_inc(layer_in, 16)
                sp.dma_start(RST[0:32, :], resets).then_inc(layer_in, 16)
                for k in (2, 3):
                    load_unit(unit(L, k), k % 2)
                with sp.Fori(0, G) as g:
                    for k in range(GRP_U):
                        load_unit(gunit(L, g, k), k % 2)
                        if k == 3:
                            sp.wait_ge(smp_state, it(L, g))
                            sp.wait_ge(y_sq, it(L, g))
                            sp.wait_ge(s1_stored, L * (G * 16) + g * 16 + 16)
                            sp.wait_ge(k_stored, L * 32 + 32)
                            sp.wait_ge(v_stored, L * 128 + 128)
                            for r in range(2):
                                sp.dma_start(KCUR[64 * r:64 * r + 64, :], kout[L, g]).then_inc(att_in, 16)
                            sp.dma_start(KC[0:64, :], kc_t[L, g]).then_inc(att_in, 16)
                            sp.dma_start(VC, vc_t[L, g].rearrange("w (b d) -> w b d", d=HD)).then_inc(att_in, 16)
                            v_g = vout[L, g]
                            sp.dma_start(VCUR[:, 0:2, :], v_g[0:NPR].rearrange("(c p) d -> p c d", p=P)).then_inc(att_in, 16)
                            sp.dma_start(VCUR[0:NSM, 2, :], v_g[NPR:T]).then_inc(att_in, 16)
                            sp.dma_start(MSK, masks).then_inc(msk_in, 16)
                        if k == 4:
                            sp.wait_ge(ssd_done, it(L, g))
                            sp.wait_ge(conv_saved, L * (G * 6) + g * 6 + 2)
                            sp.dma_start(GP[:, :], gpar[L, g]).then_inc(gp_in, 16)
                            sp.dma_start(CSI[:, :], cs_in[L, g]).then_inc(sin_in, 16)
                            sp.dma_start(SCI[:, :], sc_in[L, g]).then_inc(sin_in, 16)
                        if 15 <= k < 19:
                            i = k - 15
                            if i == 0:
                                sp.wait_ge(att_done, it(L, g))
                            sp.dma_start(S0T.rearrange("p (b n) -> p b n", b=NB)[:, :, i * P:(i + 1) * P],
                                         s0_t[L, g].rearrange("p (b n) -> p b n", b=NB)[:, :, i * P:(i + 1) * P]).then_inc(st_in[i], 16)
                for k in range(4):
                    load_unit(unit(L, OUT_U0 + k), k % 2)
                sp.wait_ge(y_hi, L * 16 + 16)
                sp.wait_ge(y_lo, L * 8 + 8)
                sp.wait_ge(y_lop, L * 8 + 8)
                sp.wait_ge(x_slab0, 16)
                sp.wait_ge(x_stored, L * 32 + 32)
                sp.dma_start(PRAW, p_t[L]).then_inc(p_in, 16)
                sp.dma_start(YX[:, 0:2 * T], xs[L][:, 0:2 * T]).then_inc(xres_in, 16)
                with sp.Fori(1, KT // 2) as m:
                    for k in range(4):
                        load_unit(L * LAYER_U + m * 4 + (OUT_U0 + k), k % 2)
                    sp.dma_start(YX[:, bass.ds(m * (2 * T), 2 * T)], xs[L][:, bass.ds(m * (2 * T), 2 * T)]).then_inc(xres_in, 16)
                for k in range(2):
                    load_unit(unit(L, PLE_U0 + k), k)
                with sp.Fori(0, KT // 2) as m:
                    for k in range(2):
                        load_unit(L * LAYER_U + m * 2 + (GATE_U0 + k), k % 2)

        @block.tensor
        def _(pe):
            mm, tr = nc.tensor.matmul, nc.tensor.transpose

            wait = pe.wait_ge

            def product(out, s, n, hi, lo, k, start, stop):
                w_hi, w_lo = WHI[s][:, n * BLK:(n + 1) * BLK], WLO[s][:, n * BLK:(n + 1) * BLK]
                x_hi_, x_lo_ = hi[:, k * T:(k + 1) * T], lo[:, k * T:(k + 1) * T]
                mm(out, w_hi, x_hi_, start=start, stop=False)
                mm(out, w_hi, x_lo_, start=False, stop=False)
                return mm(out, w_lo, x_hi_, start=False, stop=stop)

            def wait_unit(u):
                for split in (hi_done, lo_done, lop_done):
                    wait(split, u + 3)

            def project(u, b, fb):
                wait_unit(u)
                wait(bank_free[b], fb)
                for k in range(KT):
                    last = product(MAIN[b][:, 0:T], b, k, HHI, HLO, k, k == 0, k == KT - 1)
                last.then_inc(units_used, 1)

            pe.sem_inc(units_used, 2)
            for b in bank_free:
                pe.sem_inc(b, 1)
            for bk in SIDE:
                pe.sem_inc(bk.free, 1)
            wait(const_in, 16)
            with pe.Fori(0, DEPTH) as L:
                wait(xsq_sum, L + 1)
                wait(T0.free, T0.in_pre(L, 0))
                mm(T0.t[:, 0:T], ONES, SQ[:, :], start=True, stop=True).then_inc(T0.full, 1)
                for k in range(PRE_U):
                    if k == 0:
                        wait_unit(unit(L, 0))
                        wait(bank_free[0], L * (LAYER_F // 2) + 1)
                        for n in range(KT):
                            wait(h_hi, L * KT + (n + 1))
                            wait(*h_rest(L, n))
                            last = product(MAIN[0][:, 0:T], 0, n, HHI, HLO, n, n == 0, n == KT - 1)
                        last.then_inc(units_used, 1)
                    else:
                        project(unit(L, k), k % 2, L * (LAYER_F // 2) + (k // 2 + 1))
                    if k == 0:
                        wait(dt_hi, L + 1)
                        wait(dt_lo, L + 1)
                        wait(T1.free, T1.in_pre(L, 0))
                        for n in range(KT):
                            w, wl = YHI[:, n * BLK:(n + 1) * BLK], YLO[:, n * BLK:(n + 1) * BLK]
                            c0 = n * T
                            mm(T1.t[:, 0:T], w, HHI[:, c0:c0 + T], start=(n == 0), stop=False)
                            mm(T1.t[:, 0:T], w, HLO[:, c0:c0 + T], start=False, stop=False)
                            last = mm(T1.t[:, 0:T], wl, HHI[:, c0:c0 + T], start=False, stop=(n == KT - 1))
                        last.then_inc(T1.full, 1)
                    if k == 3:
                        wait(dt_ready, L + 1)
                        wait_alone(pe, "pe", T0.free, T0.in_pre(L, 1))
                        for v, a in enumerate((DT0, AC0, W0)):
                            for c in range(3):
                                n = P if c < 2 else NSM
                                last = tr(T0.t[0:n, c * 96 + v * 32:c * 96 + v * 32 + 32], a[0:32, c * P:c * P + n], ID[0:32, 0:32])
                        last.then_inc(T0.full, 1)
                for i, bk in enumerate((T0, T1)):
                    wait(v_ready, L * 2 + (i + 1))
                    wait(bk.free, bk.in_pre(L, 2 if i == 0 else 1))
                    for c in range(3):
                        n = P if c < 2 else NSM
                        last = tr(bk.t[0:n, c * P:c * P + P], VTT[:, i, c * P:c * P + n], ID)
                    last.then_inc(bk.full, 1)

                with pe.Fori(0, G) as g:
                    def use(bk, n):
                        wait(bk.free, bk.in_grp(L, g, n))

                    def scores(j):
                        bk = (A0, A1, T0, T1)[j]
                        a, r = j // 2, 64 * (j % 2)
                        use(bk, 0)
                        q, kk = Q[r:r + 64, a, :], KCUR[r:r + 64, :]
                        mm(bk.t[:, 0:P], q[:, 0:P], kk[:, 0:P], start=True, stop=True)
                        mm(bk.t[:, P:3 * P], q[:, P:2 * P], kk[:, 0:2 * P], start=True, stop=True).then_inc(bk.full, 1)

                    def turn_probs(j):
                        bk, n = ((T0, 1), (T1, 1), (A0, 2), (A1, 1))[j]
                        use(bk, n)
                        for c in range(3):
                            last = tr(bk.t[:, c * P:c * P + P], PR[:, j, c * P:c * P + P], ID)
                        last.then_inc(bk.full, 1)

                    def values(j):
                        bk, n = ((T1, 2), (A0, 3))[j // 2]
                        r = 64 * (j % 2)
                        if j % 2 == 0:
                            use(bk, n)
                        mm(bk.t[r:r + 64, 0:P], VCUR[:, 0, :], PT[:, j, 0:P], start=True, stop=True)
                        mm(bk.t[r:r + 64, P:2 * P], VCUR[:, 0, :], PT[:, j, P:2 * P], start=True, stop=False)
                        last = mm(bk.t[r:r + 64, P:2 * P], VCUR[:, 1, :], PT[:, j, 2 * P:3 * P], start=False, stop=True)
                        if j % 2:
                            last.then_inc(bk.full, 1)

                    def decay(h):
                        bk, n = ((A0, 4), (A1, 3))[h % 2]
                        use(bk, n + h // 2)
                        mm(bk.t[:, 0:T], SEL[0:96, h:h + 1].to_broadcast([96, P]), AC3[0:96, :], start=True, stop=True).then_inc(bk.full, 1)

                    def y_pair(i):
                        use(YB, 3 + i)
                        for r in range(2):
                            h = 2 * i + r
                            wait(mh_ready, it(L, g, HG, h))
                            m = MH[h % 6]
                            for c in range(3):
                                w = P if c < 2 else NSM
                                last = mm(YB.t[64 * r:64 * r + 64, c * P:c * P + w], XDT[0:w, c, h * HD:(h + 1) * HD],
                                          m[0:w, c * P:c * P + w], start=True, stop=True)
                        last.then_inc(YB.full, 1)
                        use(YO, 3 + i)
                        cc = XC[:, 1, :]
                        mm(YO.t[:, 0:P], S0[:, i * P:(i + 1) * P], cc[:, P:2 * P], start=True, stop=True)
                        for b in range(NB):
                            last = mm(YO.t[:, P + NS * b:P + NS * b + NS], S0T[:, b * GW + i * P:b * GW + (i + 1) * P],
                                      cc[:, NPR + NS * b:NPR + NS * b + NS], start=True, stop=True)
                        last.then_inc(YO.full, 1)

                    def new_state(b, bk, n):
                        use(bk, n)
                        mm(bk.t[:, :], BM3[0:3 * NSM, b, :], X3[0:3 * NSM, :], start=True, stop=True).then_inc(bk.full, 1)

                    for k in range(GRP_U):
                        project(gunit(L, g, k), k % 2, fill_bank(L, g, k))
                        if k == 2:
                            wait(q_ready, it(L, g, 2, 1))
                            wait(att_in, L * (G * 96) + g * 96 + 96)
                            scores(0)
                            scores(1)
                        if k == 3:
                            scores(2)
                            scores(3)
                        if k == 4:
                            wait(qsm_ready, it(L, g))
                            for s, bk, n in ((0, YB, 0), (1, YO, 0), (2, A0, 1)):
                                use(bk, n)
                                keys = KC[0:64, s * 512:s * 512 + 512] if s < 2 else KCUR[0:64, NPR:T]
                                w = 512 if s < 2 else NSM
                                mm(bk.t[:, 0:w], QSM[0:64, :], keys, start=True, stop=True).then_inc(bk.full, 1)
                        if k == 7:
                            wait(att_prob, it(L, g))
                            for j in range(4):
                                turn_probs(j)
                        if k == 8:
                            wait(smp_prob, it(L, g))
                            for bk, b0 in ((YB, 0), (YO, 4)):
                                use(bk, 1)
                                for b in range(4):
                                    last = tr(bk.t[:, b * P:b * P + P], PS[:, (b0 + b) * P:(b0 + b + 1) * P], ID)
                                last.then_inc(bk.full, 1)
                        if k == 9:
                            wait_alone(pe, "pe", T0.free, T0.in_grp(L, g, 2))
                            tr(T0.t[0:NSM, 0:P], PS[:, NB * P:NB * P + NSM], ID).then_inc(T0.full, 1)
                            wait(pt_ready, it(L, g, 4, 3))
                            for j in range(4):
                                values(j)
                        if k == 10:
                            wait(pts_ready, it(L, g))
                            use(A1, 2)
                            o = A1.t[0:64, 0:P]
                            mm(o, VCUR[0:NSM, 2, :], PTS[0:NSM, NB * P:9 * P], start=True, stop=False, skip_group_check=True)
                            for b in range(NB):
                                mine = PTS[:, b * P:b * P + P].rearrange("p (j n) -> p j n", j=4)[:, :, NS * b:NS * b + NS]
                                last = mm(o.rearrange("p (j n) -> p j n", j=4)[:, :, NS * b:NS * b + NS], VC[:, b, :], mine,
                                          start=False, stop=(b == NB - 1), skip_group_check=True)
                            last.then_inc(A1.full, 1)
                            wait(xc_ready, it(L, g, 6, 1) + 2)
                            use(YB, 2)
                            use(YO, 2)
                            for c in range(3):
                                w = P if c < 2 else NSM
                                last = tr(YB.t[0:w, c * P:c * P + P], XC[:, 0, c * P:c * P + w], ID)
                            last.then_inc(YB.full, 1)
                            for c in range(3):
                                w = P if c < 2 else NSM
                                last = mm(YO.t[0:w, c * P:c * P + w], XC[:, 0, c * P:c * P + w], XC[:, 1, c * P:c * P + w],
                                          start=True, stop=True)
                            last.then_inc(YO.full, 1)
                        if k in (14, 15):
                            wait(xc_ready, it(L, g, 6, 5) + 2)
                            for c in (0, 1) if k == 14 else (2,):
                                bk, n = ((T0, 3), (T1, 3), (T0, 4))[c]
                                w = P if c < 2 else NSM
                                use(bk, n)
                                for i in range(4):
                                    last = tr(bk.t[0:w, i * P:i * P + P], XC[:, 2 + i, c * P:c * P + w], ID)
                                last.then_inc(bk.full, 1)
                        if k == 15:
                            wait(xt_ready, it(L, g, 3, 1))
                            wait(bt_ready, it(L, g))
                            use(T1, 4)
                            mm(T1.t[:, :], BT[:, 0, :], XW[:, 0, :], start=True, stop=True).then_inc(T1.full, 1)
                        if 14 <= k < 18:
                            if k == 14:
                                wait(tg_ready, it(L, g))
                                wait(ac_lo, L + 1)
                            decay(2 * (k - 14))
                            decay(2 * (k - 14) + 1)
                        if 16 <= k < 20:
                            if k == 16:
                                wait(xt_ready, it(L, g, 3, 2))
                                wait(s0_ready, it(L, g))
                            wait(st_in[k - 16], L * (G * 16) + g * 16 + 16)
                            y_pair(k - 16)
                        if k == 17:
                            use(T0, 5)
                            mm(T0.t[:, :], BT[:, 1, :], XW[:, 1, :], start=True, stop=True).then_inc(T0.full, 1)
                        if k >= 19:
                            if k == 19:
                                wait(bm_ready, it(L, g))
                                wait(x3_ready, it(L, g))
                            for b, bk, n in NEW_STATES[k]:
                                new_state(b, BANKS[bk], n)
                        if k == 21:
                            wait(y_sq, it(L, g) + 1)
                            use(T1, 7)
                            mm(T1.t[:, 0:T], ONES, SQ[:, :], start=True, stop=True).then_inc(T1.full, 1)

                def wait_pair(j):
                    wait(y_hi, L * KT + (j + 1))
                    by_dve, n = y_split(j)
                    wait(y_lo if by_dve else y_lop, L * 8 + (n + 1))

                def out_tile(u, b, fb, pieces):
                    wait_unit(u)
                    wait(bank_free[b], fb)
                    for k in range(KT):
                        if pieces and k % 2 == 0:
                            wait_pair(k // 2)
                        last = product(MAIN[b][:, 0:T], 0, k, HHI, HLO, k, k == 0, False)
                    last.then_inc(units_used, 1)
                    wait_unit(u + 1)
                    for k in range(KT):
                        if pieces and k % 2 == 0:
                            wait_pair((KT + k) // 2)
                        last = product(MAIN[b][:, 0:T], 1, k, YHI, YLO, k, False, k == KT - 1)
                    last.then_inc(units_used, 1)

                fb0 = LAYER_F // 2
                for m in range(2):
                    out_tile(unit(L, OUT_U0 + 2 * m), m, L * fb0 + (OUT_U0 // 2 + 1), True)
                with pe.Fori(1, KT // 2) as mp:
                    for m in range(2):
                        out_tile(L * LAYER_U + mp * 4 + (OUT_U0 + 2 * m), m, L * fb0 + mp + (OUT_U0 // 2 + 1), False)
                wait(p_hi, L + 1)
                wait(p_lo, L + 1)
                for s in range(2):
                    wait_unit(unit(L, PLE_U0 + s))
                    for m in range(8):
                        wait(bank_free[m % 2], L * fb0 + ((OUT_U0 + KT + 8 * s) // 2 + m // 2 + 1))
                        if s == 0 and m == 2:
                            wait(mix_added, L * KT + (KT + 2))
                            wait(T0.free, T0.in_post(L, 0))
                            mm(T0.t[:, 0:T], ONES, SQ[:, :], start=True, stop=True).then_inc(T0.full, 1)
                        product(MAIN[m % 2][:, 0:T], s, 2 * m, HHI, HLO, KT - 2, True, False)
                        product(MAIN[m % 2][:, 0:T], s, 2 * m + 1, HHI, HLO, KT - 1, False, True).then_inc(e_filled, 1)
                    pe.drain().then_inc(units_used, 1)
                for m in range(2):
                    wait_unit(unit(L, GATE_U0 + m))
                    wait(bank_free[m], L * fb0 + ((OUT_U0 + 2 * KT) // 2 + 1))
                    for k in range(KT):
                        if m == 0 and k % 2 == 0:
                            wait(x_hi, L * (KT // 2) + (k // 2 + 1))
                            wait(x_lo, L * (KT // 2) + (k // 2 + 1))
                        last = product(MAIN[m][:, 0:T], m, k, HHI, HLO, k, k == 0, k == KT - 1)
                    last.then_inc(units_used, 1)
                with pe.Fori(1, KT // 2) as mp:
                    for m in range(2):
                        project(L * LAYER_U + mp * 2 + (GATE_U0 + m), m, L * fb0 + mp + ((OUT_U0 + 2 * KT) // 2 + 1))

        @block.scalar
        def _(act):
            fn = nc.scalar.activation

            def split_hi(u, s, h=None):
                act.wait_ge(units_used, u + 1)
                act.wait_ge(raw_landed[s], h)
                fn(WHI[s][:, :], RAW[s][:, :], ACT.Copy).then_inc(hi_done, 1)

            def landed(L, k):
                return L * (LAYER_U // 2 * 16) + (k // 2 * 16 + 16)

            def swap(dst, src):
                for a, b in ((0, 32), (32, 0), (64, 96), (96, 64)):
                    last = fn(dst[a:a + 32, :], src[b:b + 32, 0:T], ACT.Copy)
                return last

            def rsqrt(bank, ready, inv, eps_col):
                fn(ONE[:, :], CST[:, C_ONE:C_ONE + 1], ACT.Ln)
                act.wait_ge(bank.full, ready)
                fn(RV[:, :], bank.t[:, 0:T], ACT.Ln, scale=inv, bias=CST[:, eps_col:eps_col + 1]).then_inc(norm_read, 1)
                act.drain()
                fn(RS[:, :], RV[:, :], ACT.Exp, scale=-0.5).then_inc(norm_ln, 1)

            act.sem_inc(hi_done, 2)
            for j in range(4):
                act.wait_ge(x_first[j], 16)
                fn(XSQ[:, j * 4 * T:(j + 1) * 4 * T], YX[:, j * 4 * T:(j + 1) * 4 * T], ACT.Square).then_inc(xsq_done, 1)
            act.wait_ge(const_in, 16)
            act.sem_inc(state_stored, 16)
            act.sem_inc(s1_stored, 16)
            act.sem_inc(csout_stored, 16)
            act.sem_inc(scout_stored, 16)
            with act.Fori(0, DEPTH) as L:
                rsqrt(T0, T0.in_pre(L, 0), 1.0 / DM, C_EPS)
                split_hi(unit(L, 0), 0, landed(L, 0))
                for i in range(KT):
                    if i == KT // 2:
                        act.wait_ge(dtw_in, L * 16 + 16)
                        fn(YHI[:, 0:UNIT], DTRAW, ACT.Copy).then_inc(dt_hi, 1)
                    act.wait_ge(h_scaled, L * KT + (i + 1))
                    fn(HHI[:, i * T:(i + 1) * T], HF[i % 6], ACT.Copy).then_inc(h_hi, 1)
                split_hi(unit(L, 1), 1, landed(L, 1))
                act.wait_ge(layer_in, L * 64 + 64)
                fn(DTP[0:32, 2:3], DTP[0:32, 1:2], ACT.Exp)
                for k in range(PRE_U):
                    act.wait_ge(units_used, used(unit(L, k)))
                    if k < 2:
                        swap(KSW[:, k, :], MAIN[k % 2]).then_inc(k_swapped, 1)
                    else:
                        fn(VTT[:, k - 2, :], MAIN[k % 2][:, 0:T], ACT.Copy).then_inc(v_ready, 1)
                        act.drain().then_inc(bank_free[k % 2], 1)
                    split_hi(unit(L, k + 2), k % 2, landed(L, k + 2))
                    if k == 0:
                        act.wait_ge(dt_abs, L + 1)
                        fn(DTE[0:32, :], DTU[0:32, :], ACT.Exp, scale=-1.0).then_inc(dt_exp, 1)
                        act.wait_ge(dt_u, L + 1)
                        fn(DTC[0:32, :], DTU[0:32, :], ACT.Ln).then_inc(dt_ln, 1)
                    if k == 1:
                        act.wait_ge(ac_ready, L + 1)
                        fn(AC3[0:32, :], AC0[0:32, :], ACT.Copy).then_inc(ac_hi, 1)
                        act.wait_ge(ac_rest, L + 1)
                        fn(X3[0:32, 0:T], DTR[0:32, :], ACT.Copy)
                        fn(AC3[32:64, :], DTR[0:32, :], ACT.Copy).then_inc(ac_mid, 1)
                        act.wait_ge(dt_ac, L + 1)
                        fn(W0[0:32, :], DTE[0:32, :], ACT.Exp, scale=-1.0).then_inc(dt_wexp, 1)
                    if k == 2:
                        for i in range(2):
                            act.wait_ge(k_ready, L * 2 + (i + 1))
                            act.dma_start(kout[L, 2 * i:2 * i + 2].rearrange("h d n -> (h d) n"), KTT[:, i, :]).then_inc(k_stored, 16)
                    if k == 3:
                        act.wait_ge(T0.full, T0.in_pre(L, 1))
                        fn(TOK[:, 0:192], T0.t[:, 0:192], ACT.Copy)
                        fn(TOK[0:NSM, 192:288], T0.t[0:NSM, 192:288], ACT.Copy).then_inc(tok_ready, 1)
                        act.drain().then_inc(T0.free, 1)
                for i, bk in enumerate((T0, T1)):
                    act.wait_ge(bk.full, bk.in_pre(L, 2 if i == 0 else 1))
                    fn(VT[:, i, 0:2 * P], bk.t[:, 0:2 * P], ACT.Copy)
                    fn(VT[0:NSM, i, 2 * P:3 * P], bk.t[0:NSM, 2 * P:3 * P], ACT.Copy).then_inc(v_tok, 1)
                    act.wait_ge(v_tok, L * 2 + (i + 1))
                    for h in range(2):
                        v_h = VT[:, i, :].rearrange("p (c h d) -> p c h d", c=3, h=2)[:, :, h, :]
                        act.dma_start(vout[L, 2 * i + h, 0:NPR].rearrange("(c p) d -> p c d", p=P), v_h[:, 0:2]).then_inc(v_stored, 16)
                        act.dma_start(vout[L, 2 * i + h, NPR:T], v_h[0:NSM, 2]).then_inc(v_stored, 16)
                    act.drain().then_inc(bk.free, 1)
                act.dma_start(kold[L], kc_t[L].rearrange("g d (b w) -> (g d) b w", w=P)[:, :, NS:P]).then_inc(old_copied, 16)
                act.dma_start(vold[L], vc_t[L][:, NS:P, :]).then_inc(old_copied, 16)

                with act.Fori(0, G) as g:
                    th_n = [0]

                    def tanh_half(src, w):
                        n = th_n[0]
                        th_n[0] += 1
                        act.wait_ge(th_used, L * 72 + g * 14 + (n + 1))
                        fn(TH[n % 2][:, 0:w], src, ACT.Tanh, scale=0.5).then_inc(th_ready, 1)

                    def decay_exp(h):
                        bk, n = ((A0, 4), (A1, 3))[h % 2]
                        m, i, r = MH[h % 6], h // 2, 64 * (h % 2)
                        act.wait_ge(bk.full, bk.in_grp(L, g, n + h // 2))
                        act.wait_ge(y_used, L * 16 + g * 4 + (i - 2 if i >= 3 else 0) + 1)
                        for c in range(2):
                            fn(m[:, c * P:(c + 1) * P], bk.t[:, c * P:(c + 1) * P], ACT.Relu, scale=-1.0, bias=TGV[:, c, 1, h:h + 1])
                        fn(m[0:NSM, NPR:T], bk.t[0:NSM, NPR:T], ACT.Relu, scale=-1.0, bias=TGV[0:NSM, 2, 1, h:h + 1])
                        fn(EA[i % 3][r:r + 64, :], bk.t[r:r + 64, P:T], ACT.Exp)
                        fn(DEC[:, h, :], bk.t[:, NPR - 1:T:4], ACT.Exp).then_inc(bk.free, 1)
                        act.drain()
                        fn(m[:, 0:NPR], m[:, 0:NPR], ACT.Exp, scale=-1.0)
                        fn(m[0:NSM, NPR:T], m[0:NSM, NPR:T], ACT.Exp, scale=-1.0).then_inc(decay_ready, 1)

                    for k in range(GRP_U):
                        b = k % 2
                        main = MAIN[b]
                        act.wait_ge(units_used, used(gunit(L, g, k)))
                        if k < 2:
                            swap(QS[:, k, :], main).then_inc(q_swapped, 1)
                        if k in (2, 3, 6, 20) or 14 <= k < 18:
                            tanh_half(main[:, 0:T], T)
                        if k in (4, 18):
                            i = k // 18
                            if k == 4:
                                act.wait_ge(sin_in, L * (G * 32) + g * 32 + 32)
                                act.wait_ge(gp_in, L * (G * 16) + g * 16 + 16)
                            else:
                                act.wait_ge(conv_saved, it(L, g, 6, 4) + 2)
                                act.wait_ge(xc_ready, it(L, g, 6, 4) + 2)
                            act.wait_ge(sc_done, L * (G * 2) + g * 2 + (i + 1))
                            act.wait_ge(sc_saved, L * (G * 2) + g * 2 + (i + 1))
                            fn(fsmp(USC, 2)[:, :, 0:2], smp(SCI[:, i * 16:(i + 1) * 16], 2), ACT.Copy)
                            fn(SCB, main[:, 0:T], ACT.Copy).then_inc(c_ready, 1)
                            act.drain().then_inc(bank_free[b], 1)
                        if 8 <= k < 14:
                            t = k - 8
                            f, s = FB[t % 2], AB[t % 2]
                            if t == 0:
                                act.wait_ge(sc_done, it(L, g, 2, 0) + 1)
                                act.wait_ge(sc_saved, it(L, g, 2, 0) + 1)
                            act.wait_ge(xc_ready, L * (G * 6) + g * 6 + (t + 1))
                            act.wait_ge(conv_saved, L * (G * 6) + g * 6 + (t + 1))
                            fn(fsmp(f, 3)[:, :, 0:3], smp(CSI[:, t * 24:(t + 1) * 24], 3), ACT.Copy)
                            fn(f[:, 3:3 + NPR], main[:, 0:NPR], ACT.Copy)
                            fn(fsmp(f, 3)[:, :, 3:7], smp(main[:, NPR:T]), ACT.Copy).then_inc(bank_free[b], 1)
                            act.drain()
                            fn(s[:, :], f[:, 0:CW], ACT.Identity, scale=GP[:, G_CW + 4 * t:G_CW + 4 * t + 1],
                               bias=GP[:, G_CB + t:G_CB + t + 1]).then_inc(tap_done, 1)
                        split_hi(gunit(L, g, k + 2), b, L * (LAYER_U // 2 * 16) + g * (GRP_U // 2 * 16) + ((PRE_U + k + 2) // 2 * 16 + 16))
                        if k == 2:
                            act.wait_ge(q_ready, it(L, g, 2, 1))
                            for j in range(4):
                                last = fn(QSM[0:64, j * NSM:(j + 1) * NSM], Q[64 * (j % 2):64 * (j % 2) + 64, j // 2, NPR:T], ACT.Copy)
                            last.then_inc(qsm_ready, 1)
                        if 8 <= k < 14:
                            act.wait_ge(conv_sum, it(L, g, 6, t))
                            tanh_half(s[:, :], CW)
                        if k in (5, 19):
                            i = k // 19
                            act.wait_ge(u_ready, it(L, g, 2, i))
                            fn(CSUM, USC[:, 0:SW], ACT.Copy, scale=GP[:, G_SW + 3 * i:G_SW + 3 * i + 1]).then_inc(stap_done, 1)
                        if k == 5:
                            act.wait_ge(att_max, it(L, g))
                            for j in range(4):
                                for c, (c0, c1) in enumerate(((0, P), (P, 3 * P))):
                                    fn(PR[:, j, c0:c1], PR[:, j, c0:c1], ACT.Exp, scale=HD ** -0.5, bias=NM[:, 2 * j + c:2 * j + c + 1],
                                       accum_out=DEN[:, 2 * j + c:2 * j + c + 1])
                            fn(MX[:, 0:8], MX[:, 0:8], ACT.Exp).then_inc(att_exp, 1)
                        if k == 6:
                            act.wait_ge(smp_max, it(L, g))
                            fn(PS, PS, ACT.Exp, scale=HD ** -0.5, bias=NM[:, 8:9], accum_out=DEN[:, 8:9])
                            fn(MX[:, 8:9], MX[:, 8:9], ACT.Exp).then_inc(smp_exp, 1)
                        if k == 8:
                            act.wait_ge(state_stored, L * (G * 16) + g * 16 + 16)
                            for j, (bk, n) in enumerate(((T0, 1), (T1, 1), (A0, 2), (A1, 1))):
                                act.wait_ge(bk.full, bk.in_grp(L, g, n))
                                fn(PT[:, j, :], bk.t[:, 0:3 * P], ACT.Copy).then_inc(pt_ready, 1)
                                act.drain().then_inc(bk.free, 1)
                        if k == 9:
                            for bk, b0 in ((YB, 0), (YO, 4)):
                                act.wait_ge(bk.full, bk.in_grp(L, g, 1))
                                fn(PTS[:, b0 * P:(b0 + 4) * P], bk.t[:, :], ACT.Copy).then_inc(bk.free, 1)
                            act.wait_ge(T0.full, T0.in_grp(L, g, 2))
                            fn(PTS[0:NSM, NB * P:9 * P], T0.t[0:NSM, 0:P], ACT.Copy).then_inc(pts_ready, 1)
                            act.drain().then_inc(T0.free, 1)
                        if k == 10:
                            act.wait_ge(A1.full, A1.in_grp(L, g, 2))
                            for j in range(4):
                                r = 64 * (j % 2)
                                last = fn(OS[r:r + 64, j // 2, :], A1.t[0:64, j * NSM:(j + 1) * NSM], ACT.Copy)
                            last.then_inc(os_ready, 1)
                            act.drain().then_inc(A1.free, 1)
                        if k == 12:
                            act.wait_ge(att_done, it(L, g))
                            act.wait_ge(YB.full, YB.in_grp(L, g, 2))
                            fn(BT[:, 0:2, :], YB.t[:, 0:2 * P].rearrange("p (c n) -> p c n", c=2), ACT.Copy)
                            for q in range(2):
                                last = fn(B3[q * NSM:(q + 1) * NSM, :], YB.t[0:NSM, 2 * P:3 * P], ACT.Copy)
                            last.then_inc(bt_ready, 1)
                        if k == 15:
                            act.wait_ge(T1.full, T1.in_grp(L, g, 4))
                            fn(S0, T1.t[:, :], ACT.Copy).then_inc(s0_ready, 1)
                            act.drain().then_inc(T1.free, 1)
                        if 14 <= k < 18:
                            decay_exp(2 * (k - 14))
                            decay_exp(2 * (k - 14) + 1)
                        if k == 16:
                            act.wait_ge(xt_ready, it(L, g, 3, 2))
                            for q in (0, 2):
                                last = fn(X3[q * NSM:(q + 1) * NSM, :], XW[0:NSM, 2, :], ACT.Copy)
                            last.then_inc(x3_hi, 1)
                        if k == 14:
                            act.wait_ge(conv_saved, it(L, g, 6, 5) + 2)
                            act.dma_start(conv_out[L, g], CSO[:, :]).then_inc(csout_stored, 16)
                        if k == 20:
                            act.wait_ge(s1_ready, it(L, g))
                            act.dma_start(ssm_p[L, g], S1).then_inc(s1_stored, 16)
                    rsqrt(T1, T1.in_grp(L, g, 7), 1.0 / GW, C_EPS + 1)
                    act.wait_ge(sc_saved, it(L, g, 2, 1) + 1)
                    act.dma_start(scv_out[L, g], SCO[:, :]).then_inc(scout_stored, 16)
                    act.wait_ge(smp_state, it(L, g) + 1)
                    act.dma_start(ssm_s[L, g], S0T).then_inc(state_stored, 16)

                act.wait_ge(units_used, unit(L, OUT_U0 + 2))
                act.wait_ge(sc_done, L * (G * 2) + (G * 2 + 1))
                for j in range(KT):
                    if j == 8:
                        act.wait_ge(ssd_done, L * G + (G + 1))
                        act.wait_ge(s1_stored, L * (G * 16) + (G * 16 + 16))
                    c, y = y_pair_at(j)
                    fn((HHI if j < 8 else YHI)[:, c:c + 2 * T], YX[:, y:y + 2 * T], ACT.Copy).then_inc(y_hi, 1)
                act.wait_ge(state_stored, L * (G * 16) + (G * 16 + 16))

                def mix_pair(mp, last=False):
                    for q in range(4):
                        if q % 2:
                            m = q // 2
                            act.wait_ge(units_used, L * LAYER_U + mp * 4 + used(OUT_U0 + 2 * m + 1))
                            act.wait_ge(mix_added, L * KT + mp * 2 + (m + 1))
                            fn(MIX[:, bass.ds((mp * 2 + m) * T, T)], MAIN[m][:, 0:T], ACT.Copy)
                            fn(MSQ[m][:, :], MAIN[m][:, 0:T], ACT.Square).then_inc(mix_sq, 1)
                            act.drain().then_inc(bank_free[m], 1)
                        split_hi(L * LAYER_U + mp * 4 + (OUT_U0 + q + 2), q % 2,
                                 L * (LAYER_U // 2 * 16) + mp * 32 + ((OUT_U0 + q + 2) // 2 * 16 + 16))
                        if last and q == 2:
                            act.wait_ge(p_in, L * 16 + 16)
                            fn(HHI[:, (KT - 2) * T:KT * T], PRAW, ACT.Copy).then_inc(p_hi, 1)

                with act.Fori(0, KT // 2 - 1) as mp:
                    mix_pair(mp)
                mix_pair(KT // 2 - 1, True)
                lag = 10
                for m in range(KT + lag):
                    if m == 2:
                        rsqrt(T0, T0.in_post(L, 0), 1.0 / DM, C_EPS)
                    if m == 8:
                        split_hi(unit(L, GATE_U0), 0, landed(L, GATE_U0))
                    if m == KT:
                        split_hi(unit(L, GATE_U0 + 1), 1, landed(L, GATE_U0 + 1))
                    if m < KT:
                        act.wait_ge(e_filled, L * KT + (m + 1))
                        c0 = (KT + m) * T
                        if m == 0:
                            act.wait_ge(p_lo, L + 1)
                        fn(YX[:, c0:c0 + T], MAIN[m % 2][:, 0:T], ACT.Copy, scale=0.5).then_inc(bank_free[m % 2], 1)
                    if m >= lag and m % 2 == 0:
                        c0 = (m - lag) * T
                        act.wait_ge(x_mid, L * (KT // 2) + ((m - lag) // 2 + 1))
                        fn(HHI[:, c0:c0 + 2 * T], YX[:, c0:c0 + 2 * T], ACT.Copy).then_inc(x_hi, 1)

                def square(m, tile):
                    act.wait_ge(x_out, L * KT + tile + 1)
                    act.wait_ge(x_added, L * KT + tile + 1)
                    fn(MSQ[m][:, :], YX[:, bass.ds(tile * T, T)], ACT.Square).then_inc(x_sq, 1)

                with act.Fori(0, KT // 2 - 1) as mp:
                    for m in range(2):
                        act.wait_ge(units_used, L * LAYER_U + mp * 2 + used(GATE_U0 + m))
                        split_hi(L * LAYER_U + mp * 2 + (GATE_U0 + m + 2), m,
                                 L * (LAYER_U // 2 * 16) + mp * 16 + ((GATE_U0 + m + 2) // 2 * 16 + 16))
                        act.wait_ge(th_used, L * 72 + mp * 2 + (56 + m + 1))
                        fn(TH[m][:, 0:T], MAIN[m][:, 0:T], ACT.Tanh, scale=0.5).then_inc(th_ready, 1)
                        square(m, mp * 2 + m)
                c0 = (KT - 2) * T
                act.wait_ge(x_most, L + 1)
                act.dma_start(xs[L + 1][:, 0:c0], YX[:, 0:c0]).then_inc(x_stored, 16)
                for m in range(2):
                    act.wait_ge(units_used, L * LAYER_U + used(GATE_U0 + KT - 2 + m))
                    act.wait_ge(th_used, L * 72 + (70 + m + 1))
                    fn(TH[m][:, 0:T], MAIN[m][:, 0:T], ACT.Tanh, scale=0.5).then_inc(th_ready, 1)
                    square(m, KT - 2 + m)
                act.wait_ge(x_final, L + 2)
                act.dma_start(xs[L + 1][:, c0:KT * T], YX[:, c0:KT * T]).then_inc(x_stored, 16)
            act.wait_ge(x_stored, DEPTH * 32 + 32)
            act.wait_ge(old_copied, DEPTH * 32)
            act.wait_ge(k_stored, DEPTH * 32)
            act.wait_ge(v_stored, DEPTH * 128)
            act.wait_ge(csout_stored, DEPTH * G * 16 + 16)
            act.wait_ge(scout_stored, DEPTH * G * 16 + 16)
            act.wait_ge(s1_stored, DEPTH * G * 16 + 16)
            act.wait_ge(state_stored, DEPTH * G * 16 + 16)

        @block.vector
        def _(dve):
            tt, ts, stt = nc.vector.tensor_tensor, nc.vector.tensor_scalar, nc.vector.scalar_tensor_tensor

            def lo(dst, raw, hi):
                return tt(dst, raw, hi.bitcast(F32), ALU.subtract)

            def split_lo(u, s, k=None):
                n = (KT - pool_blocks(k)) * BLK
                if n == 0:
                    dve.sem_inc(lo_done, 1)
                    return
                dve.wait_ge(hi_done, u + 3)
                lo(WLO[s][:, 0:n], RAW[s][:, 0:n], WHI[s][:, 0:n]).then_inc(lo_done, 1)

            def rsqrt(bank, n, inv, eps):
                dve.wait_ge(norm_read, n)
                ts(RA[:, :], bank.t[:, 0:T], -0.5 * inv, -0.5 * eps, ALU.mult, ALU.add)
                dve.wait_ge(norm_ln, n)
                tt(RV[:, :], RS[:, :], RS[:, :], ALU.mult).then_inc(bank.free, 1)
                dve.drain()
                tt(RV[:, :], RV[:, :], RA[:, :], ALU.mult)
                dve.drain()
                stt(RS[:, :], RV[:, :], 1.5, RS[:, :], ALU.add, ALU.mult)
                dve.drain()

            def rotate(dst, swapped, main, b):
                tt(dst, main[:, 0:T], COS, ALU.mult).then_inc(bank_free[b], 1)
                tt(swapped, swapped, SIN, ALU.mult)
                dve.drain()
                return tt(dst, dst, swapped, ALU.add)

            dve.sem_inc(lo_done, 2)
            dve.sem_inc(th_used, 2)
            dve.sem_inc(ssd_done, 1)
            dve.sem_inc(sc_done, 1)
            dve.sem_inc(xc_ready, 2)
            dve.sem_inc(y_used, 1)
            dve.sem_inc(smp_state, 1)
            for f in FB:
                nc.vector.memset(f[:, 0:3], 0.0)
            for j in range(1, 4):
                dve.wait_ge(xsq_done, j + 1)
                tt(XSQ[:, 0:4 * T], XSQ[:, 0:4 * T], XSQ[:, 4 * j * T:4 * (j + 1) * T], ALU.add)
                dve.drain()
            tt(XSQ[:, 0:2 * T], XSQ[:, 0:2 * T], XSQ[:, 2 * T:4 * T], ALU.add)
            dve.drain()
            tt(SQ[:, :], XSQ[:, 0:T], XSQ[:, T:2 * T], ALU.add).then_inc(xsq_sum, 1)
            dve.sem_inc(x_final, 1)
            dve.wait_ge(const_in, 16)
            with dve.Fori(0, DEPTH) as L:
                rsqrt(T0, L * 6 + 1, 1.0 / DM, EPS)
                dve.wait_ge(layer_in, L * 64 + 64)
                for i in range(KT + 2):
                    if i == 2:
                        split_lo(unit(L, 0), 0)
                    if i < KT:
                        f = HF[i % 6]
                        if i >= 6:
                            dve.wait_ge(*h_rest(L, i - 6))
                        stt(f, YX[:, i * T:(i + 1) * T], NRM[:, i:i + 1], RS[:, :], ALU.mult, ALU.mult).then_inc(h_scaled, 1)
                    j = i - 2
                    if j >= 0 and j % 3 == 2:
                        dve.wait_ge(h_hi, L * KT + (j + 1))
                        lo(HLO[:, j * T:(j + 1) * T], HF[j % 6], HHI[:, j * T:(j + 1) * T]).then_inc(h_lo_dve, 1)
                dve.wait_ge(dt_hi, L + 1)
                lo(YLO[:, 0:UNIT], DTRAW, YHI[:, 0:UNIT]).then_inc(dt_lo, 1)
                split_lo(unit(L, 1), 1)

                def step_sizes():
                    dve.wait_ge(T1.full, T1.in_pre(L, 0))
                    ts(DTR[0:32, :], T1.t[0:32, 0:T], DTP[0:32, 0:1], None, ALU.add).then_inc(T1.free, 1)
                    dve.drain()
                    stt(DTU[0:32, :], DTR[0:32, :], -1.0, DTR[0:32, :], ALU.mult, ALU.max).then_inc(dt_abs, 1)
                    dve.wait_ge(dt_exp, L + 1)
                    ts(DTU[0:32, :], DTE[0:32, :], 1.0, None, ALU.add).then_inc(dt_u, 1)
                    dve.drain()
                    ts(W0[0:32, :], DTU[0:32, :], -1.0, None, ALU.add)
                    dve.drain()
                    tt(W0[0:32, :], DTE[0:32, :], W0[0:32, :], ALU.subtract)
                    dve.drain()
                    dve.wait_ge(dt_ln, L + 1)
                    tt(DTC[0:32, :], DTC[0:32, :], W0[0:32, :], ALU.add)
                    dve.drain()
                    stt(DT0[0:32, :], DTR[0:32, :], 0.0, DTC[0:32, :], ALU.max, ALU.add)
                    dve.drain()
                    ts(DTR[0:32, :], DT0[0:32, :], DTP[0:32, 2:3], -1.0, ALU.mult, ALU.mult)
                    dve.drain()
                    nc.vector.tensor_tensor_scan(AC0[0:32, :], RST[0:32, :], DTR[0:32, :], 0.0, ALU.mult, ALU.add).then_inc(ac_ready, 1)
                    dve.drain()
                    for c in range(2):
                        ts(DTE[0:32, c * P:(c + 1) * P], AC0[0:32, c * P:(c + 1) * P], AC0[0:32, (c + 1) * P - 1:(c + 1) * P],
                           None, ALU.subtract)
                    ac = smp(AC0[0:32, NPR:T])
                    tt(smp(DTE[0:32, NPR:T]), ac, ac[:, :, NS - 1:NS].to_broadcast([32, NB, NS]), ALU.subtract).then_inc(dt_ac, 1)

                for k in range(PRE_U):
                    split_lo(unit(L, k + 2), k % 2)
                    if k < 2:
                        dve.wait_ge(k_swapped, L * 2 + (k + 1))
                        rotate(KTT[:, k, :], KSW[:, k, :], MAIN[k], k).then_inc(k_ready, 1)
                    if k == 0:
                        step_sizes()
                    if k == 1:
                        dve.wait_ge(ac_hi, L + 1)
                        tt(DTR[0:32, :], AC0[0:32, :], AC3[0:32, :].bitcast(F32), ALU.subtract).then_inc(ac_rest, 1)
                        dve.wait_ge(ac_mid, L + 1)
                        tt(AC3[64:96, :], DTR[0:32, :], X3[0:32, 0:T].bitcast(F32), ALU.subtract).then_inc(ac_lo, 1)
                        dve.wait_ge(dt_wexp, L + 1)
                        tt(W0[0:32, :], W0[0:32, :], DT0[0:32, :], ALU.mult).then_inc(dt_ready, 1)

                with dve.Fori(0, G) as g:
                    th_n = [0]

                    def gate(dst, main, b):
                        n = th_n[0]
                        th_n[0] += 1
                        dve.wait_ge(th_ready, L * 72 + g * 14 + (n + 1))
                        stt(dst, TH[n % 2][:, 0:T], 1.0, main[:, 0:T], ALU.add, ALU.mult).then_inc(th_used, 1)
                        return dve.drain().then_inc(bank_free[b], 1)

                    def mask_max(j):
                        bk = (A0, A1, T0, T1)[j]
                        dve.wait_ge(bk.full, bk.in_grp(L, g, 0))
                        tt(PR[:, j, :], bk.t[:, 0:3 * P], MSK[:, 0:3 * P], ALU.add).then_inc(bk.free, 1)
                        dve.drain()
                        nc.vector.reduce_max(MX[:, 2 * j:2 * j + 1], PR[:, j, 0:P], AX.X)
                        nc.vector.reduce_max(MX[:, 2 * j + 1:2 * j + 2], PR[:, j, P:3 * P], AX.X)

                    def row_stats(c0, c1, sink):
                        n = c1 - c0
                        dve.drain()
                        stt(NM[:, c0:c1].rearrange("p (j c) -> p j c", c=n if n == 1 else 2),
                            MX[:, c0:c1].rearrange("p (j c) -> p j c", c=n if n == 1 else 2), HD ** -0.5, sink, ALU.mult, ALU.max)
                        dve.drain()
                        ts(NM[:, c0:c1], NM[:, c0:c1], -1.0, None, ALU.mult)
                        dve.drain()
                        return tt(MX[:, c0:c1].rearrange("p (j c) -> p j c", c=n if n == 1 else 2),
                                  NM[:, c0:c1].rearrange("p (j c) -> p j c", c=n if n == 1 else 2), sink, ALU.add)

                    def half_over_den(c0, c1):
                        dve.drain()
                        tt(DEN[:, c0:c1], DEN[:, c0:c1], MX[:, c0:c1], ALU.add)
                        dve.drain()
                        nc.vector.reciprocal(DEN[:, c0:c1], DEN[:, c0:c1])
                        dve.drain()

                    def gated_y(i):
                        x = XC[:, 2 + i, :]
                        dve.wait_ge(YB.full, YB.in_grp(L, g, 3 + i))
                        stt(YT, x, GP[:, G_D + i:G_D + i + 1], YB.t[:, 0:T], ALU.mult, ALU.add).then_inc(YB.free, 1)
                        dve.wait_ge(YO.full, YO.in_grp(L, g, 3 + i))
                        tt(YS[:, 0:P + NSM], YO.t[:, 0:P + NSM], EA[i % 3], ALU.mult).then_inc(YO.free, 1)
                        dve.drain().then_inc(y_used, 1)
                        tt(YT[:, P:T], YT[:, P:T], YS[:, 0:P + NSM], ALU.add)
                        dve.drain()
                        tt(Z2[:, i, :], YT, Z2[:, i, :], ALU.mult).then_inc(y_gated, 1)
                        dve.drain()

                    for k in range(GRP_U):
                        b = k % 2
                        main = MAIN[b]
                        if k < 2:
                            dve.wait_ge(q_swapped, it(L, g, 2, k))
                            rotate(Q[:, k, :], QS[:, k, :], main, b).then_inc(q_ready, 1)
                        if k in (2, 3):
                            gate(G2[:, k - 2, :], main, b)
                        if k in (6, 20):
                            gate(SG2, main, b)
                        if 14 <= k < 18:
                            gate(Z2[:, k - 14, :], main, b)
                        if k in (5, 19):
                            i = k // 19
                            dve.wait_ge(c_ready, it(L, g, 2, i))
                            dve.wait_ge(units_used, used(gunit(L, g, k)))
                            tt(USC[:, 2:2 + NPR], main[:, 0:NPR], SCB[:, 0:NPR], ALU.mult)
                            tt(fsmp(USC, 2)[:, :, 2:6], smp(main[:, NPR:T]), smp(SCB[:, NPR:T]), ALU.mult).then_inc(u_ready, 1)
                            dve.drain().then_inc(bank_free[b], 1)
                        if k in (7, 21):
                            i = k // 21
                            dve.wait_ge(units_used, used(gunit(L, g, k)))
                            cs = CSUM[:, NPR:NPR + 48].rearrange("p (b t) -> p b t", t=6)[:, :, 2:6]
                            stt(SBB[:, 0:NPR], CSUM[:, 0:NPR], 0.5, main[:, 0:NPR], ALU.mult, ALU.mult)
                            stt(smp(SBB[:, NPR:T]), cs, 0.5, smp(main[:, NPR:T]), ALU.mult, ALU.mult)
                            dve.drain().then_inc(bank_free[b], 1)
                            if k == 7:
                                dve.wait_ge(x_stored, L * 32 + 32)
                                dve.wait_ge(x_slab0, 16)
                            tt(YX[:, bass.ds((g * 2 + 24 + i) * T, T)], SBB, SG2, ALU.mult).then_inc(sc_done, 1)
                        if 8 <= k < 14:
                            t = k - 8
                            f, s = FB[t % 2], AB[t % 2]
                            dve.wait_ge(tap_done, it(L, g, 6, t))
                            for j in range(1, 4):
                                last = stt(s[:, :], f[:, j:j + CW], GP[:, G_CW + 4 * t + j:G_CW + 4 * t + j + 1], s[:, :],
                                           ALU.mult, ALU.add)
                                if j < 3:
                                    dve.drain()
                            last.then_inc(conv_sum, 1)
                        split_lo(gunit(L, g, k + 2), b, k)
                        if k in (3, 4):
                            if k == 3:
                                dve.wait_ge(msk_in, L * (G * 16) + g * 16 + 16)
                                dve.wait_ge(gp_in, L * (G * 16) + g * 16 + 16)
                            mask_max(2 * (k - 3))
                            mask_max(2 * (k - 3) + 1)
                        if k == 4:
                            row_stats(0, 8, GP[:, G_SK:G_SK + 4].unsqueeze(2).to_broadcast([P, 4, 2])).then_inc(att_max, 1)
                        if k == 5:
                            for s, bk, n in ((0, YB, 0), (1, YO, 0), (2, A0, 1)):
                                w = 512 if s < 2 else NSM
                                dve.wait_ge(bk.full, bk.in_grp(L, g, n))
                                if s == 0:
                                    dve.wait_ge(state_stored, L * (G * 16) + g * 16 + 16)
                                tt(PS[:, s * 512:s * 512 + w], bk.t[:, 0:w], MSK[:, 3 * P + s * 512:3 * P + s * 512 + w],
                                   ALU.add).then_inc(bk.free, 1)
                            dve.drain()
                            nc.vector.reduce_max(MX[:, 8:9], PS, AX.X)
                            row_stats(8, 9, GP[:, G_SKS:G_SKS + 1].unsqueeze(2)).then_inc(smp_max, 1)
                        if k == 6:
                            wait_alone(dve, "dve", att_exp, it(L, g))
                            half_over_den(0, 8)
                            for j in range(4):
                                for c, (c0, c1) in enumerate(((0, P), (P, 3 * P))):
                                    last = ts(PR[:, j, c0:c1], PR[:, j, c0:c1], DEN[:, 2 * j + c:2 * j + c + 1], 0.5,
                                              ALU.mult, ALU.mult)
                            last.then_inc(att_prob, 1)
                        if k == 7:
                            wait_alone(dve, "dve", smp_exp, it(L, g))
                            half_over_den(8, 9)
                            ts(PS, PS, DEN[:, 8:9], 0.5, ALU.mult, ALU.mult).then_inc(smp_prob, 1)
                        if k in (6, 20):
                            i = k // 20
                            dve.wait_ge(stap_done, it(L, g, 2, i))
                            for j in (1, 2):
                                stt(CSUM, USC[:, j:j + SW], GP[:, G_SW + 3 * i + j:G_SW + 3 * i + j + 1], CSUM, ALU.mult, ALU.add)
                                dve.drain()
                        if 8 <= k < 14:
                            if t == 0:
                                dve.wait_ge(tok_ready, L + 1)
                                src = TOK[:, :].rearrange("p (v h) -> p v h", h=32)[:, :, bass.ds(g * HG, HG)]
                                dst = TG[:, :].rearrange("p (v h) -> p v h", h=HG)
                                nc.vector.tensor_copy(SEL[0:96, :], CST[0:96, bass.ds(g * HG + C_SEL, HG)])
                                nc.vector.tensor_copy(dst[:, 0:6, :], src[:, 0:6, :])
                                nc.vector.tensor_copy(dst[0:NSM, 6:9, :], src[0:NSM, 6:9, :]).then_inc(tg_ready, 1)
                            n = th_n[0]
                            th_n[0] += 1
                            dve.wait_ge(th_ready, L * 72 + g * 14 + (n + 1))
                            th = TH[n % 2]
                            stt(XC[:, t, 0:NPR], th[:, 0:NPR], 1.0, AB[t % 2][:, 0:NPR], ALU.add, ALU.mult)
                            ths = th[:, NPR:NPR + 56].rearrange("p (b t) -> p b t", t=7)[:, :, 3:7]
                            ss = AB[t % 2][:, NPR:NPR + 56].rearrange("p (b t) -> p b t", t=7)[:, :, 3:7]
                            stt(smp(XC[:, t, NPR:T]), ths, 1.0, ss, ALU.add, ALU.mult).then_inc(th_used, 1)
                            dve.drain()
                            ts(XC[:, t, :], XC[:, t, :], 0.5, None, ALU.mult).then_inc(xc_ready, 1)
                        if k == 10:
                            for a, (bk, n) in enumerate(((T1, 2), (A0, 3))):
                                dve.wait_ge(bk.full, bk.in_grp(L, g, n))
                                tt(YX[:, bass.ds((g * 2 + KT + a) * T, NPR)], bk.t[:, 0:NPR], G2[:, a, 0:NPR], ALU.mult).then_inc(bk.free, 1)
                        if k == 11:
                            dve.wait_ge(os_ready, it(L, g))
                            for a in range(2):
                                last = tt(YX[:, bass.ds((g * 2 + KT + a) * T + NPR, NSM)], OS[:, a, :], G2[:, a, NPR:T], ALU.mult)
                            last.then_inc(att_done, 1)
                            dve.drain()
                            dve.wait_ge(YO.full, YO.in_grp(L, g, 2))
                            tt(CBM[:, 0:NPR], YO.t[:, 0:NPR], TRI[:, 0:NPR], ALU.mult)
                            tt(CBM[0:NSM, NPR:T], YO.t[0:NSM, NPR:T], TRI[0:NSM, NPR:T], ALU.mult).then_inc(YO.free, 1)
                        if k == 12:
                            dve.wait_ge(bt_ready, it(L, g))
                            lo(B3[2 * NSM:3 * NSM, :], YB.t[0:NSM, 2 * P:3 * P], B3[0:NSM, :]).then_inc(b3_ready, 1)
                            dve.drain().then_inc(YB.free, 1)
                        if k in (14, 15):
                            for c in (0, 1) if k == 14 else (2,):
                                bk, n = ((T0, 3), (T1, 3), (T0, 4))[c]
                                w = P if c < 2 else NSM
                                dve.wait_ge(bk.full, bk.in_grp(L, g, n))
                                src = bk.t[0:w, :].rearrange("p (h d) -> p h d", d=HD)
                                for dst, v in ((XDT, 0), (XW, 2)):
                                    last = tt(dst[0:w, c, :].rearrange("p (h d) -> p h d", d=HD), src,
                                              TGV[0:w, c, v, :].unsqueeze(2).to_broadcast([w, HG, HD]), ALU.mult)
                                last.then_inc(bk.free, 1)
                                dve.drain().then_inc(xt_ready, 1)
                        if 15 <= k < 19:
                            for h in (2 * (k - 15), 2 * (k - 15) + 1):
                                m = MH[h % 6]
                                dve.wait_ge(decay_ready, it(L, g, HG, h))
                                tt(m[:, 0:NPR], m[:, 0:NPR], CBM[:, 0:NPR], ALU.mult)
                                tt(m[0:NSM, NPR:T], m[0:NSM, NPR:T], CBM[0:NSM, NPR:T], ALU.mult).then_inc(mh_ready, 1)
                        if k == 17:
                            dve.wait_ge(x3_hi, it(L, g))
                            lo(X3[NSM:2 * NSM, :], XW[0:NSM, 2, :], X3[0:NSM, :]).then_inc(x3_ready, 1)
                        if 16 <= k < 20:
                            gated_y(k - 16)
                        if k == 18:
                            dve.wait_ge(T0.full, T0.in_grp(L, g, 5))
                            dve.wait_ge(s1_stored, L * (G * 16) + g * 16 + 16)
                            tt(S1.rearrange("p (h d) -> p h d", d=HD), S0.rearrange("p (h d) -> p h d", d=HD),
                               DEC[:, :, 0:1].to_broadcast([P, HG, HD]), ALU.mult)
                            dve.drain()
                            tt(S1, T0.t[:, :], S1, ALU.add).then_inc(T0.free, 1)
                            dve.drain().then_inc(s1_ready, 1)
                        if k >= 19:
                            for b_, name, n in NEW_STATES[k]:
                                bk = BANKS[name]
                                st = S0T[:, b_ * GW:(b_ + 1) * GW]
                                dve.wait_ge(bk.full, bk.in_grp(L, g, n))
                                stv = st.rearrange("p (h d) -> p h d", d=HD)
                                tt(stv, stv, DEC[:, :, 1 + b_:2 + b_].to_broadcast([P, HG, HD]), ALU.mult)
                                dve.drain()
                                tt(st, bk.t[:, :], st, ALU.add).then_inc(bk.free, 1)
                    dve.drain().then_inc(smp_state, 1)
                    rsqrt(T1, L * 6 + g + 2, 1.0 / GW, 4 * EPS)
                    for i in range(4):
                        stt(YX[:, bass.ds((g * 4 + i) * T, T)], Z2[:, i, :], GP[:, G_NW + i:G_NW + i + 1], RS[:, :], ALU.mult, ALU.mult)
                    dve.drain().then_inc(ssd_done, 1)

                for j in range(KT):
                    if y_split(j)[0]:
                        c, y = y_pair_at(j)
                        hi, rest = (HHI, HLO) if j < 8 else (YHI, YLO)
                        dve.wait_ge(y_hi, L * KT + (j + 1))
                        lo(rest[:, c:c + 2 * T], YX[:, y:y + 2 * T], hi[:, c:c + 2 * T]).then_inc(y_lo, 1)
                with dve.Fori(0, KT // 2 - 1) as mp:
                    for q in range(4):
                        split_lo(L * LAYER_U + mp * 4 + (OUT_U0 + q + 2), q % 2)
                for q in range(4):
                    split_lo(unit(L, OUT_U0 + 2 * KT - 4 + q + 2), q % 2)
                    if q == 2:
                        dve.wait_ge(p_hi, L + 1)
                        lo(HLO[:, (KT - 2) * T:KT * T], PRAW, HHI[:, (KT - 2) * T:KT * T]).then_inc(p_lo, 1)
                rsqrt(T0, L * 6 + 6, 1.0 / DM, EPS)
                dve.wait_ge(xres_in, L * (KT * 8) + KT * 8)
                split_lo(unit(L, GATE_U0), 0)
                for j in range(KT // 2):
                    c0 = 2 * j * T
                    for i in (2 * j, 2 * j + 1):
                        mix = MIX[:, i * T:(i + 1) * T]
                        stt(mix, mix, NRM[:, KT + i:KT + i + 1], RS[:, :], ALU.mult, ALU.mult)
                    dve.drain()
                    x = YX[:, c0:c0 + 2 * T]
                    tt(x, x, MIX[:, c0:c0 + 2 * T], ALU.add).then_inc(x_mid, 1)
                split_lo(unit(L, GATE_U0 + 1), 1)

                def add_gated(mp, m):
                    dve.wait_ge(th_ready, L * 72 + mp * 2 + (56 + m + 1))
                    stt(RA[:, :], TH[m][:, 0:T], 1.0, YX[:, bass.ds((mp * 2 + KT + m) * T, T)], ALU.add, ALU.mult).then_inc(th_used, 1)
                    dve.drain().then_inc(bank_free[m], 1)
                    x = YX[:, bass.ds((mp * 2 + m) * T, T)]
                    tt(x, x, RA[:, :], ALU.add).then_inc(x_out, 1)
                    dve.drain()

                wait_alone(dve, "dve", x_lo, (L + 1) * (KT // 2))
                with dve.Fori(0, KT // 2 - 1) as mp:
                    for m in range(2):
                        split_lo(L * LAYER_U + mp * 2 + (GATE_U0 + m + 2), m)
                        add_gated(mp, m)
                dve.drain().then_inc(x_most, 1)
                for m in range(2):
                    dve.wait_ge(th_ready, L * 72 + (70 + m + 1))
                    e0, x_0 = (2 * KT - 2 + m) * T, (KT - 2 + m) * T
                    stt(RA[:, :], TH[m][:, 0:T], 1.0, YX[:, e0:e0 + T], ALU.add, ALU.mult).then_inc(th_used, 1)
                    dve.drain().then_inc(bank_free[m], 1)
                    tt(YX[:, x_0:x_0 + T], YX[:, x_0:x_0 + T], RA[:, :], ALU.add).then_inc(x_out, 1)
                    last = dve.drain()
                last.then_inc(x_final, 1)

        @block.gpsimd
        def _(pool):
            tt = nc.gpsimd.tensor_tensor

            def lo(dst, raw, hi):
                return tt(dst, raw, hi.bitcast(F32), ALU.subtract)

            def split_lo(u, s, k=None):
                n = (KT - pool_blocks(k)) * BLK
                pool.wait_ge(hi_done, u + 3)
                lo(WLO[s][:, n:UNIT], RAW[s][:, n:UNIT], WHI[s][:, n:UNIT]).then_inc(lop_done, 1)

            pool.sem_inc(lop_done, 2)
            pool.sem_inc(conv_saved, 2)
            pool.sem_inc(sc_saved, 1)
            pool.sem_inc(x_stored, 32)
            pool.sem_inc(mix_added, 2)
            pool.sem_inc(x_added, 2)
            pool.sem_inc(y_sq, 1)
            pool.wait_ge(xsq_done, 4)
            pool.wait_ge(raw_landed[1], 16)
            pool.dma_start(xs[0], YX[:, 0:KT * T]).then_inc(x_slab0, 16)
            pool.wait_ge(const_in, 16)
            with pool.Fori(0, DEPTH) as L:
                split_lo(unit(L, 0), 0)
                for i in range(KT):
                    if i % 3 < 2:
                        pool.wait_ge(h_hi, L * KT + (i + 1))
                        lo(HLO[:, i * T:(i + 1) * T], HF[i % 6], HHI[:, i * T:(i + 1) * T]).then_inc(h_lo, 1)
                split_lo(unit(L, 1), 1)
                for k in range(PRE_U):
                    split_lo(unit(L, k + 2), k % 2)
                with pool.Fori(0, G) as g:
                    for k in range(GRP_U):
                        if 17 <= k < 21:
                            i = k - 17
                            pool.wait_ge(y_gated, it(L, g, 4, i))
                            if i == 0:
                                tt(SQ[:, :], Z2[:, 0, :], Z2[:, 0, :], ALU.mult)
                            else:
                                tt(RV[:, :], Z2[:, i, :], Z2[:, i, :], ALU.mult)
                                pool.drain()
                                tt(SQ[:, :], SQ[:, :], RV[:, :], ALU.add)
                            if i < 3:
                                pool.drain()
                            else:
                                pool.drain().then_inc(y_sq, 1)
                        split_lo(gunit(L, g, k + 2), k % 2, k)
                        if 8 <= k < 14:
                            t = k - 8
                            f = FB[t % 2]
                            if t == 0:
                                pool.wait_ge(csout_stored, L * (G * 16) + g * 16 + 16)
                            wait_alone(pool, "pool", tap_done, it(L, g, 6, t))
                            nc.gpsimd.tensor_copy(CSO[:, t * 27:t * 27 + 3], f[:, NPR:NPR + 3])
                            nc.gpsimd.tensor_copy(smp(CSO[:, t * 27 + 3:(t + 1) * 27], 3), fsmp(f, 3)[:, :, 4:7]).then_inc(conv_saved, 1)
                        if k == 13:
                            pool.wait_ge(b3_ready, it(L, g))
                            w = 3 * NSM
                            tt(BM3[0:w, :, :], B3[0:w, :].bitcast(F32).unsqueeze(1).to_broadcast([w, NB, P]),
                               CST[0:w, C_SEQ:C_SEQ + NB].unsqueeze(2).to_broadcast([w, NB, P]), ALU.mult).then_inc(bm_ready, 1)
                        if k in (6, 20):
                            i = k // 20
                            if i == 0:
                                pool.wait_ge(scout_stored, L * (G * 16) + g * 16 + 16)
                            wait_alone(pool, "pool", u_ready, it(L, g, 2, i))
                            nc.gpsimd.tensor_copy(SCO[:, i * 18:i * 18 + 2], USC[:, NPR:NPR + 2])
                            nc.gpsimd.tensor_copy(smp(SCO[:, i * 18 + 2:(i + 1) * 18], 2), fsmp(USC, 2)[:, :, 4:6]).then_inc(sc_saved, 1)
                for j in range(KT):
                    if j == 8:
                        wait_alone(pool, "pool", ssd_done, L * G + (G + 1))
                    if not y_split(j)[0]:
                        c, y = y_pair_at(j)
                        hi, rest = (HHI, HLO) if j < 8 else (YHI, YLO)
                        pool.wait_ge(y_hi, L * KT + (j + 1))
                        lo(rest[:, c:c + 2 * T], YX[:, y:y + 2 * T], hi[:, c:c + 2 * T]).then_inc(y_lop, 1)
                wait_alone(pool, "pool", ssd_done, L * G + (G + 1))
                nc.gpsimd.memset(SQ[:, :], 0.0)
                pool.drain()
                with pool.Fori(0, KT // 2) as mp:
                    for q in range(4):
                        if q % 2:
                            m = q // 2
                            pool.wait_ge(mix_sq, L * KT + mp * 2 + (m + 1))
                            tt(SQ[:, :], SQ[:, :], MSQ[m][:, :], ALU.add).then_inc(mix_added, 1)
                            pool.drain()
                        split_lo(L * LAYER_U + mp * 4 + (OUT_U0 + q + 2), q % 2)
                split_lo(unit(L, GATE_U0), 0)
                for j in range(KT // 2):
                    pool.wait_ge(x_hi, L * (KT // 2) + (j + 1))
                    c0, c1 = 2 * j * T, 2 * (j + 1) * T
                    lo(HLO[:, c0:c1], YX[:, c0:c1], HHI[:, c0:c1]).then_inc(x_lo, 1)
                split_lo(unit(L, GATE_U0 + 1), 1)
                wait_alone(pool, "pool", T0.full, T0.in_post(L, 0))
                nc.gpsimd.memset(SQ[:, :], 0.0)
                pool.drain()
                with pool.Fori(0, KT // 2 - 1) as mp:
                    for m in range(2):
                        split_lo(L * LAYER_U + mp * 2 + (GATE_U0 + m + 2), m)
                        pool.wait_ge(x_sq, L * KT + mp * 2 + (m + 1))
                        tt(SQ[:, :], SQ[:, :], MSQ[m][:, :], ALU.add).then_inc(x_added, 1)
                        pool.drain()
                for m in range(2):
                    pool.wait_ge(x_sq, L * KT + (KT - 2 + m + 1))
                    tt(SQ[:, :], SQ[:, :], MSQ[m][:, :], ALU.add).then_inc(x_added, 1)
                    last = pool.drain()
                last.then_inc(xsq_sum, 1)


_INS = ["wts", "wdt", "x0", "p_t", "npre", "npost", "gpar", "dtpar", "s0_t", "kc_t", "vc_t", "cs_in", "sc_in",
        "consts", "masks", "resets"]
_OUTS = [("xs", (DEPTH + 1, P, KT * T)), ("kout", (DEPTH, G, HD, T)), ("vout", (DEPTH, G, T, HD)),
         ("kold", (DEPTH, G * HD, NB, P - NS)), ("vold", (DEPTH, G, P - NS, NB * HD)),
         ("conv_out", (DEPTH, G, P, 6 * 27)), ("scv_out", (DEPTH, G, P, 2 * 18)),
         ("ssm_p", (DEPTH, G, P, GW)), ("ssm_s", (DEPTH, G, P, NB * GW))]


def shape_constants():
    import numpy as np

    f = np.float32
    half = HD // 2
    inv = np.exp(f(-np.log(10000.0)) * np.arange(half, dtype=f) * f(2.0 / HD))
    pos = np.concatenate([np.arange(NPR), np.tile(1024 + np.arange(NS), NB)]).astype(f)
    ang = pos[None, :] * inv[np.arange(P) % half][:, None]
    sign = np.where(np.arange(P) % HD < half, -1.0, 1.0).astype(f)[:, None]
    c = np.zeros((P, NCONST), f)
    c[:, C_COS:C_COS + T] = np.cos(ang)
    c[:, C_SIN:C_SIN + T] = np.sin(ang) * sign
    c[:, C_ID:C_ID + P] = np.eye(P)
    s, l = np.arange(P)[:, None], np.arange(P)[None, :]
    for n in range(2):
        c[:, C_TRI + n * P:C_TRI + (n + 1) * P] = s <= l
    c[:NSM, C_TRI + NPR:C_TRI + T] = ((s <= l) & (s // NS == l // NS))[:NSM, :NSM]
    c[:, C_ONE:C_ONE + P] = 1.0
    c[:3 * NSM, C_SEQ:C_SEQ + NB] = np.arange(3 * NSM)[:, None] % NSM // NS == np.arange(NB)[None, :]
    c[:96, C_SEL:C_SEL + 32] = np.tile(np.eye(32), (3, 1))
    c[:, C_EPS], c[:, C_EPS + 1] = EPS, 4 * EPS
    m = np.zeros((P, NMASK), f)
    t = np.arange(P)[:, None]
    key = np.arange(2 * P)[None, :]
    m[:, 0:P] = np.where(key[:, :P] <= t, 0, -1e30)
    m[:, P:3 * P] = np.where((key <= P + t) & (key > t), 0, -1e30)
    b, tok = (t // NS) % NB, t % NS
    col = np.arange(NB * P)[None, :]
    m[:, 3 * P:3 * P + NB * P] = np.where((col // P == b) & (col % P > tok), 0, -1e30)
    new = np.arange(NSM)[None, :]
    m[:, 3 * P + NB * P:] = np.where((new // NS == b) & (new % NS <= tok), 0, -1e30)
    r = np.ones((32, T), f)
    r[:, [0, P]] = 0
    r[:, NPR::NS] = 0
    return c, m, r


def kernel(**inputs):
    import concourse.bacc as _bacc
    import numpy as np
    from concourse.bass_utils import run_bass_kernel_spmd as _run

    i = {k: np.asarray(v) for k, v in inputs.items()}
    D = DEPTH

    z0, xbc0 = 0, 2048
    x_0, b_0, c_0 = xbc0, xbc0 + 2048, xbc0 + 2048 + 512
    dt0 = xbc0 + 3072
    q0 = dt0 + 32
    k0, v0 = q0 + 1024, q0 + 1024 + 256
    ga0 = v0 + 256
    sb0 = ga0 + 1024
    scc0, sh0, sg0 = sb0 + 1024, sb0 + 2048, sb0 + 3072
    starts = [k0, k0 + P, v0, v0 + P]
    for g in range(G):
        starts += [q0 + g * 256, q0 + g * 256 + P, ga0 + g * 256, ga0 + g * 256 + P]
        short = [[w + (2 * g + n) * P for w in (scc0, sh0, sg0, sb0)] for n in range(2)]
        starts += short[0] + [b_0 + g * P, c_0 + g * P] + [x_0 + g * 512 + n * P for n in range(4)]
        starts += [z0 + g * 512 + n * P for n in range(4)] + short[1]
    w_in, w_out, ple, gate = i["w_in"], i["w_out"], i["ple_proj"], i["ple_gate"]
    wts = np.empty((D, LAYER_U, P, KT, P), np.float32)
    for u, c in enumerate(starts):
        wts[:, u] = w_in[:, :, c:c + P].reshape(D, KT, P, P).transpose(0, 2, 1, 3)
    for m in range(KT):
        w = w_out[:, :, m * P:(m + 1) * P].reshape(D, 2, KT, P, P).transpose(0, 1, 3, 2, 4)
        wts[:, OUT_U0 + 2 * m] = w[:, 1]
        wts[:, OUT_U0 + 2 * m + 1] = w[:, 0]
        wts[:, GATE_U0 + m] = gate[:, :, m * P:(m + 1) * P].reshape(D, KT, P, P).transpose(0, 2, 1, 3)
    pl = ple.reshape(D, 2, P, KT, P).transpose(0, 2, 3, 1, 4).reshape(D, P, 2, KT, P)
    wts[:, PLE_U0:PLE_U0 + 2] = pl.transpose(0, 2, 1, 3, 4)
    wdt = np.zeros((D, P, KT, P), np.float32)
    wdt[:, :, :, 0:32] = w_in[:, :, dt0:dt0 + 32].reshape(D, KT, P, 32).transpose(0, 2, 1, 3)

    def tokens(prompt, sample):
        a = np.concatenate([prompt[..., 0, :, :], sample.reshape(*sample.shape[:-3], NSM, sample.shape[-1])], axis=-2)
        n = a.shape[-1] // P
        a = a.reshape(*a.shape[:-1], n, P)
        a = np.moveaxis(a, (-1, -2, -3), (-3, -2, -1))
        return a.reshape(*a.shape[:-2], n * T)

    def conv_groups(w):
        lead = w.shape[:-1]
        x, b, c = w[..., :2048], w[..., 2048:2560], w[..., 2560:]
        return np.concatenate([b.reshape(*lead, G, 1, P), c.reshape(*lead, G, 1, P), x.reshape(*lead, G, 4, P)], axis=-2)

    gpar = np.zeros((D, G, P, NGP), np.float32)
    gpar[..., G_CW:G_CW + 24] = conv_groups(i["ssd_conv_w"]).transpose(0, 2, 4, 3, 1).reshape(D, G, P, 24)
    gpar[..., G_CB:G_CB + 6] = conv_groups(i["ssd_conv_b"]).transpose(0, 1, 3, 2)
    gpar[..., G_D:G_D + 4] = np.repeat(i["ssd_d"].reshape(D, G, 4, 2), HD, axis=3).transpose(0, 1, 3, 2)
    gpar[..., G_NW:G_NW + 4] = i["ssd_norm"].reshape(D, G, 4, P).transpose(0, 1, 3, 2)
    gpar[..., G_SW:G_SW + 6] = i["sc_conv_w"].reshape(D, 3, G, 2, P).transpose(0, 2, 4, 3, 1).reshape(D, G, P, 6)
    sinks = i["attn_sinks"].reshape(D, G, 4)
    gpar[..., G_SK:G_SK + 4] = sinks[:, :, None, :]
    gpar[..., G_SKS] = np.repeat(sinks, NSM, axis=2)
    consts, masks, resets = shape_constants()
    cs = conv_groups(i["state_ssd_conv"])
    sc = i["state_sc_conv"].reshape(D, NB, 2, G, 2, P)
    arrays = {
        "wts": wts.reshape(NUNITS, P, UNIT), "wdt": wdt.reshape(D, P, UNIT),
        "x0": tokens(i["x_prompt"], i["x_sample"]), "p_t": tokens(i["p_prompt"], i["p_sample"]),
        "npre": i["norm_pre"].reshape(D, KT, P).transpose(0, 2, 1), "npost": i["norm_post"].reshape(D, KT, P).transpose(0, 2, 1),
        "gpar": gpar, "dtpar": np.stack([i["ssd_dt_bias"], i["ssd_a_log"]], axis=-1),
        "s0_t": i["state_ssm"].reshape(D, NB, G, HG, HD, NST).transpose(0, 2, 5, 1, 3, 4).reshape(D, G, P, NB * GW),
        "kc_t": i["cache_k"].transpose(0, 3, 4, 1, 2).reshape(D, G, HD, NB * P),
        "vc_t": i["cache_v"].transpose(0, 3, 2, 1, 4).reshape(D, G, P, NB * HD),
        "cs_in": cs.transpose(0, 3, 5, 4, 1, 2).reshape(D, G, P, 6 * 24),
        "sc_in": sc.transpose(0, 3, 5, 4, 1, 2).reshape(D, G, P, 2 * 16),
        "consts": consts, "masks": masks, "resets": resets,
    }
    nc = _bacc.Bacc("TRN2", target_bir_lowering=False, num_devices=1)
    args = []
    for n in _INS:
        arrays[n] = np.ascontiguousarray(arrays[n])
        args.append(nc.dram_tensor(n, arrays[n].shape, F32, kind="ExternalInput").ap())
    for n, shape in _OUTS:
        args.append(nc.dram_tensor(n, shape, F32, kind="ExternalOutput").ap())
    hybrid_step(nc, *args)
    r = _run(nc, [arrays], core_ids=[0])
    o = {n: np.asarray(r.results[0][n]) for n, _ in _OUTS}

    y = o["xs"][DEPTH].reshape(P, KT, T).transpose(2, 1, 0).reshape(T, DM)
    k, v = o["kout"], o["vout"]
    pk = k[..., P:NPR].transpose(0, 3, 1, 2)[:, None]
    pv = v[:, :, P:NPR].transpose(0, 2, 1, 3)[:, None]
    k_new = k[..., NPR:].reshape(D, G, HD, NB, NS).transpose(0, 3, 4, 1, 2)
    v_new = v[:, :, NPR:].reshape(D, G, NB, NS, HD).transpose(0, 2, 3, 1, 4)
    k_old = o["kold"].reshape(D, G, HD, NB, P - NS).transpose(0, 3, 4, 1, 2)
    v_old = o["vold"].reshape(D, G, P - NS, NB, HD).transpose(0, 3, 2, 1, 4)
    co = o["conv_out"].reshape(D, G, P, 6, 9, 3).transpose(0, 4, 5, 1, 3, 2)
    co = np.concatenate([co[..., 2:, :].reshape(D, 9, 3, 2048), co[..., 0, :].reshape(D, 9, 3, 512),
                         co[..., 1, :].reshape(D, 9, 3, 512)], axis=-1)
    so = o["scv_out"].reshape(D, G, P, 2, 9, 2).transpose(0, 4, 5, 1, 3, 2).reshape(D, 9, 2, 1024)
    sp = o["ssm_p"].reshape(D, G, NST, HG, HD).transpose(0, 1, 3, 4, 2).reshape(D, 1, 32, HD, NST)
    ss = o["ssm_s"].reshape(D, G, NST, NB, HG, HD).transpose(0, 3, 1, 4, 5, 2).reshape(D, NB, 32, HD, NST)
    out = (y[None, :NPR], y[NPR:].reshape(NB, NS, DM), co[:, :1], sp, pk, pv, so[:, :1],
           co[:, 1:], ss, np.concatenate([k_old, k_new], axis=2), np.concatenate([v_old, v_new], axis=2), so[:, 1:])
    return tuple(np.ascontiguousarray(a) for a in out)
```
